# Optimizing a Trainium2 kernel written in Bass

```python
import math
import jax, jax.numpy as jnp
from jax import lax
import numpy as np

D_MODEL = 1024
BATCH = 1
SEQ = 128
DEPTH = 2
DEC_BATCH = 1
DEC_SEQ = 512
PAST_LEN = 128

GRID_W = 64
EXPAND = 2
D_INNER = EXPAND * D_MODEL
EPS = 1e-6
S5_WIDTH = D_INNER // 2
S5_GROUP = 16
S5_GROUPS = S5_WIDTH // S5_GROUP
S5_STATE = 64
HY_WIDTH = D_INNER - S5_WIDTH
HY_ORDER = 2
HY_SHORT = 3
HY_BANDS = 16
HY_EMB = 1 + 2 * HY_BANDS
HY_HID = 64
HY_DECAY_TARGET = 1e-2
HY_FAST = 0.3
HY_SLOW = 1.5
EVEN_PROJ = 2 * S5_WIDTH + 4 * HY_WIDTH
SSD_HEADDIM = 64
SSD_HEADS = D_INNER // SSD_HEADDIM
SSD_STATE = 128
SSD_GROUPS = 4
SSD_CONV = 3
SSD_CHUNK = 128
SSD_CONV_DIM = D_INNER + 2 * SSD_GROUPS * SSD_STATE
ODD_PROJ = D_INNER + SSD_CONV_DIM + 2 * SSD_HEADS
N_S5_LAYERS = (DEPTH + 1) // 2
N_SSD_LAYERS = DEPTH // 2

kernel_name = 'hybrid_s5_hyena_ssd_diffusion_step'

F32 = jnp.float32

def rmsnorm(x, w):
    xf = x.astype(F32)
    return xf * lax.rsqrt(jnp.mean(xf * xf, axis=-1, keepdims=True) + EPS) * w.astype(F32)

def dwconv(x, w, b):
    k = w.shape[0]
    y = lax.conv_general_dilated(x, w.astype(x.dtype)[:, None, :], window_strides=(1,),
                                 padding=[(k // 2, k // 2)], dimension_numbers=('NWC', 'WIO', 'NWC'),
                                 feature_group_count=x.shape[-1])
    return y + b

def s5_scan(ug, lam_bar, b_bar, c_mat, h0, reverse):
    bu = jnp.einsum('blgh,gph->blgp', ug.astype(jnp.complex64), b_bar)
    if reverse:
        bu = jnp.flip(bu, 1)
    bu = bu.at[:, 0].add(lam_bar * h0)
    a = jnp.broadcast_to(lam_bar, bu.shape)

    def combine(left, right):
        a_l, b_l = left
        a_r, b_r = right
        return a_r * a_l, a_r * b_l + b_r

    _, h = lax.associative_scan(combine, (a, bu), axis=1)
    h_final = h[:, -1]
    if reverse:
        h = jnp.flip(h, 1)
    y = jnp.einsum('blgp,ghp->blgh', h, c_mat).real
    return y, h_final

def s5_mixer(u, a_re, a_im, log_dt, b_re, b_im, c_re, c_im, d, glu_w, glu_b, h0):
    bsz, L, _ = u.shape
    ug = u.reshape(bsz, L, S5_GROUPS, S5_GROUP)
    lam = lax.complex(a_re.astype(F32), a_im.astype(F32))
    dt = jnp.exp(log_dt.astype(F32))[..., None]
    lam_bar = jnp.exp(lam * dt)
    b_bar = ((lam_bar - 1.0) / lam)[..., None] * lax.complex(b_re.astype(F32), b_im.astype(F32))
    c_mat = lax.complex(c_re.astype(F32), c_im.astype(F32))
    y_f, h_f = s5_scan(ug, lam_bar[0], b_bar[0], c_mat[0], h0[:, 0], reverse=False)
    y_b, h_b = s5_scan(ug, lam_bar[1], b_bar[1], c_mat[1], h0[:, 1], reverse=True)
    y = (y_f + y_b).reshape(bsz, L, S5_WIDTH) + u * d
    y = jax.nn.gelu(y)
    y = y * jax.nn.sigmoid(y @ glu_w + glu_b)
    return y, jnp.stack([h_f, h_b], axis=1)

def hyena_filters(L, w1, b1, freq1, w2, b2, freq2, w3):
    t = jnp.arange(L, dtype=F32)[:, None]
    t_norm = t / (L - 1)
    bands = jnp.linspace(1e-4, HY_BANDS - 1, HY_BANDS, dtype=F32)
    ang = (2.0 * math.pi / L) * t * bands
    emb = jnp.concatenate([t_norm, jnp.cos(ang), jnp.sin(ang)], axis=-1)
    f = jnp.sin(freq1 * (emb @ w1 + b1))
    f = jnp.sin(freq2 * (f @ w2 + b2))
    f = (f @ w3).reshape(L, HY_ORDER, 2, HY_WIDTH)
    deltas = jnp.abs(jnp.linspace(math.log(HY_DECAY_TARGET) / HY_SLOW, math.log(HY_DECAY_TARGET) / HY_FAST,
                                  HY_WIDTH, dtype=F32))
    window = jnp.exp(-t_norm * deltas)
    return f * window[:, None, None, :]

def long_conv(v, h_fwd, h_bwd, bias):
    L = v.shape[1]
    k = jnp.concatenate([h_fwd, jnp.zeros_like(h_fwd[:1]), jnp.flip(h_bwd[1:], 0)], axis=0)
    k_f = jnp.fft.rfft(k, n=2 * L, axis=0)
    v_f = jnp.fft.rfft(v, n=2 * L, axis=1)
    y = jnp.fft.irfft(v_f * k_f[None], n=2 * L, axis=1)[:, :L]
    return y + v * bias

def hyena_mixer(vx, short_w, short_b, w1, b1, freq1, w2, b2, freq2, w3, bias):
    L = vx.shape[1]
    vx = dwconv(vx, short_w, short_b)
    v, x1, x2 = jnp.split(vx, 3, axis=-1)
    filt = hyena_filters(L, w1, b1, freq1, w2, b2, freq2, w3)
    z = x1 * long_conv(v, filt[:, 0, 0], filt[:, 0, 1], bias[0])
    z = x2 * long_conv(z, filt[:, 1, 0], filt[:, 1, 1], bias[1])
    return z

def even_mixer(h, w_in, w_out, s5p, hyp, s5_h0):
    proj = h @ w_in
    u, g_a, vx, g_b = jnp.split(proj, [S5_WIDTH, 2 * S5_WIDTH, 2 * S5_WIDTH + 3 * HY_WIDTH], axis=-1)
    y_a, s5_final = s5_mixer(u, *s5p, s5_h0)
    y_b = hyena_mixer(vx, *hyp)
    y = jnp.concatenate([y_a * jax.nn.silu(g_a), y_b * jax.nn.silu(g_b)], axis=-1)
    return y @ w_out, s5_final

def ssd_scan(x, dt, a, b, c, h0):
    bsz, L, H, P = x.shape
    G, N = b.shape[2], b.shape[3]
    R, Q = H // G, SSD_CHUNK
    nc = L // Q
    x = x.reshape(bsz, nc, Q, G, R, P)
    dt = dt.reshape(bsz, nc, Q, G, R)
    b = b.reshape(bsz, nc, Q, G, N)
    c = c.reshape(bsz, nc, Q, G, N)
    da_cum = jnp.cumsum(dt * a.reshape(G, R), axis=2)
    xdt = x * dt[..., None]
    seg = da_cum[:, :, :, None] - da_cum[:, :, None, :]
    lower = jnp.tril(jnp.ones((Q, Q), bool))[:, :, None, None]
    decay = jnp.exp(jnp.where(lower, seg, -jnp.inf))
    cb = jnp.einsum('bcign,bcjgn->bcijg', c, b)
    scores = cb[..., None] * decay
    y_diag = jnp.einsum('bcijgr,bcjgrp->bcigrp', scores, xdt)
    xw = xdt * jnp.exp(da_cum[:, :, -1:] - da_cum)[..., None]
    states = jnp.einsum('bcjgn,bcjgrp->bcgrpn', b, xw)
    chunk_decay = jnp.exp(da_cum[:, :, -1])

    def step(hc, inp):
        s, dcy = inp
        return hc * dcy[..., None, None] + s, hc

    h_final, h_prev = lax.scan(step, h0.reshape(bsz, G, R, P, N),
                               (jnp.moveaxis(states, 1, 0), jnp.moveaxis(chunk_decay, 1, 0)))
    h_prev = jnp.moveaxis(h_prev, 0, 1)
    y_off = jnp.einsum('bcign,bcgrpn->bcigrp', c, h_prev) * jnp.exp(da_cum)[..., None]
    y = (y_diag + y_off).reshape(bsz, L, H, P)
    return y, h_final.reshape(bsz, H, P, N)

def ssd_mixer(h, w_in, conv_w, conv_b, a_log, dt_bias, d, norm_w, w_out, h0):
    bsz, L, _ = h.shape
    proj = h @ w_in
    z, xbc, dt_raw = jnp.split(proj, [D_INNER, D_INNER + SSD_CONV_DIM], axis=-1)
    xbc = jax.nn.silu(dwconv(xbc, conv_w, conv_b))
    x, b, c = jnp.split(xbc, [D_INNER, D_INNER + SSD_GROUPS * SSD_STATE], axis=-1)
    x = x.reshape(bsz, L, SSD_HEADS, SSD_HEADDIM)
    b = b.reshape(bsz, L, SSD_GROUPS, SSD_STATE)
    c = c.reshape(bsz, L, SSD_GROUPS, SSD_STATE)
    dt = jax.nn.softplus(dt_raw.reshape(bsz, L, 2, SSD_HEADS) + dt_bias)
    a = -jnp.exp(a_log.astype(F32))
    y_f, h_f = ssd_scan(x, dt[:, :, 0], a[0], b, c, h0[:, 0])
    y_b, h_b = ssd_scan(jnp.flip(x, 1), jnp.flip(dt[:, :, 1], 1), a[1], jnp.flip(b, 1), jnp.flip(c, 1), h0[:, 1])
    y = y_f + jnp.flip(y_b, 1) + x * d[:, None]
    y = rmsnorm(y.reshape(bsz, L, D_INNER) * jax.nn.silu(z), norm_w)
    return y @ w_out, jnp.stack([h_f, h_b], axis=1)

def setup_inputs(seed: int = 0) -> dict:
    key = jax.random.key(seed)
    ks = iter(jax.random.split(key, 64))

    def nrm(shape, scale):
        return scale * jax.random.normal(next(ks), shape, F32)

    def unif(shape, lo, hi):
        return jax.random.uniform(next(ks), shape, F32, lo, hi)

    n5, nd = N_S5_LAYERS, N_SSD_LAYERS
    G, P, GS, W = S5_GROUPS, S5_STATE, S5_GROUP, S5_WIDTH
    dt_ssd = jnp.exp(unif((nd, 2, SSD_HEADS), math.log(1e-3), math.log(1e-1)))
    return {
        'x_prompt': nrm((BATCH, SEQ, D_MODEL), 1.0),
        'x_sample': nrm((DEC_BATCH, DEC_SEQ, D_MODEL), 1.0),
        'state_s5_re': nrm((DEC_BATCH, n5, 2, G, P), 0.5),
        'state_s5_im': nrm((DEC_BATCH, n5, 2, G, P), 0.5),
        'state_ssd': nrm((DEC_BATCH, nd, 2, SSD_HEADS, SSD_HEADDIM, SSD_STATE), 0.5),
        'c': nrm((DEC_BATCH, D_MODEL), 1.0),
        'c_ctx': nrm((D_MODEL,), 1.0),
        'mod_w': nrm((DEPTH, D_MODEL, 3 * D_MODEL), 0.5 * D_MODEL ** -0.5),
        'mod_b': nrm((DEPTH, 3 * D_MODEL), 0.02),
        'norm_w': 1.0 + nrm((DEPTH, D_MODEL), 0.02),
        'final_norm_w': 1.0 + nrm((D_MODEL,), 0.02),
        'ev_w_in': nrm((n5, D_MODEL, EVEN_PROJ), D_MODEL ** -0.5),
        'ev_w_out': nrm((n5, D_INNER, D_MODEL), D_INNER ** -0.5),
        's5_a_re': -0.5 + nrm((n5, 2, G, P), 0.01),
        's5_a_im': math.pi * jnp.arange(P, dtype=F32) + nrm((n5, 2, G, P), 0.01),
        's5_log_dt': unif((n5, 2, G), math.log(1e-3), math.log(1e-1)),
        's5_b_re': nrm((n5, 2, G, P, GS), (2 * GS) ** -0.5),
        's5_b_im': nrm((n5, 2, G, P, GS), (2 * GS) ** -0.5),
        's5_c_re': nrm((n5, 2, G, GS, P), (2 * P) ** -0.5),
        's5_c_im': nrm((n5, 2, G, GS, P), (2 * P) ** -0.5),
        's5_d': 1.0 + nrm((n5, W), 0.1),
        's5_glu_w': nrm((n5, W, W), W ** -0.5),
        's5_glu_b': nrm((n5, W), 0.02),
        'hy_short_w': nrm((n5, HY_SHORT, 3 * HY_WIDTH), HY_SHORT ** -0.5),
        'hy_short_b': nrm((n5, 3 * HY_WIDTH), 0.02),
        'hy_f_w1': nrm((n5, HY_EMB, HY_HID), HY_EMB ** -0.5),
        'hy_f_b1': nrm((n5, HY_HID), 0.02),
        'hy_f_freq1': 1.0 + nrm((n5, HY_HID), 0.01),
        'hy_f_w2': nrm((n5, HY_HID, HY_HID), HY_HID ** -0.5),
        'hy_f_b2': nrm((n5, HY_HID), 0.02),
        'hy_f_freq2': 1.0 + nrm((n5, HY_HID), 0.01),
        'hy_f_w3': nrm((n5, HY_HID, HY_ORDER * 2 * HY_WIDTH), 0.1 * HY_HID ** -0.5),
        'hy_bias': nrm((n5, HY_ORDER, HY_WIDTH), 0.5),
        'ssd_w_in': nrm((nd, D_MODEL, ODD_PROJ), D_MODEL ** -0.5),
        'ssd_conv_w': nrm((nd, SSD_CONV, SSD_CONV_DIM), SSD_CONV ** -0.5),
        'ssd_conv_b': nrm((nd, SSD_CONV_DIM), 0.02),
        'ssd_a_log': jnp.log(unif((nd, 2, SSD_HEADS), 1.0, 16.0)),
        'ssd_dt_bias': dt_ssd + jnp.log(-jnp.expm1(-dt_ssd)),
        'ssd_d': 1.0 + nrm((nd, SSD_HEADS), 0.1),
        'ssd_norm_w': 1.0 + nrm((nd, D_INNER), 0.02),
        'ssd_w_out': nrm((nd, D_INNER, D_MODEL), D_INNER ** -0.5),
    }

def reference(x_prompt, x_sample, state_s5_re, state_s5_im, state_ssd, c, c_ctx, mod_w, mod_b, norm_w,
              final_norm_w, ev_w_in, ev_w_out, s5_a_re, s5_a_im, s5_log_dt, s5_b_re, s5_b_im, s5_c_re, s5_c_im,
              s5_d, s5_glu_w, s5_glu_b, hy_short_w, hy_short_b, hy_f_w1, hy_f_b1, hy_f_freq1, hy_f_w2, hy_f_b2,
              hy_f_freq2, hy_f_w3, hy_bias, ssd_w_in, ssd_conv_w, ssd_conv_b, ssd_a_log, ssd_dt_bias, ssd_d,
              ssd_norm_w, ssd_w_out):
    silu_ctx = jax.nn.silu(c_ctx.astype(F32))[None]
    silu_lat = jax.nn.silu(c.astype(F32))
    xp, xs = x_prompt, x_sample
    new_re, new_im, new_ssd = [], [], []
    for i in range(DEPTH):
        j = i // 2
        sh_p, sc_p, g_p = jnp.split(silu_ctx @ mod_w[i] + mod_b[i], 3, axis=-1)
        sh_s, sc_s, g_s = jnp.split(silu_lat @ mod_w[i] + mod_b[i], 3, axis=-1)
        hp = rmsnorm(xp, norm_w[i]) * (1.0 + sc_p[:, None]) + sh_p[:, None]
        hs = rmsnorm(xs, norm_w[i]) * (1.0 + sc_s[:, None]) + sh_s[:, None]
        if i % 2 == 0:
            s5p = (s5_a_re[j], s5_a_im[j], s5_log_dt[j], s5_b_re[j], s5_b_im[j], s5_c_re[j], s5_c_im[j],
                   s5_d[j], s5_glu_w[j], s5_glu_b[j])
            hyp = (hy_short_w[j], hy_short_b[j], hy_f_w1[j], hy_f_b1[j], hy_f_freq1[j], hy_f_w2[j], hy_f_b2[j],
                   hy_f_freq2[j], hy_f_w3[j], hy_bias[j])
            h0_ctx = jnp.zeros((xp.shape[0], 2, S5_GROUPS, S5_STATE), jnp.complex64)
            h0_lat = lax.complex(state_s5_re[:, j].astype(F32), state_s5_im[:, j].astype(F32))
            out_p, st = even_mixer(hp, ev_w_in[j], ev_w_out[j], s5p, hyp, h0_ctx)
            out_s, _ = even_mixer(hs, ev_w_in[j], ev_w_out[j], s5p, hyp, h0_lat)
            new_re.append(st.real)
            new_im.append(st.imag)
        else:
            sdp = (ssd_w_in[j], ssd_conv_w[j], ssd_conv_b[j], ssd_a_log[j], ssd_dt_bias[j], ssd_d[j],
                   ssd_norm_w[j], ssd_w_out[j])
            h0_ctx = jnp.zeros((xp.shape[0], 2, SSD_HEADS, SSD_HEADDIM, SSD_STATE), F32)
            out_p, st = ssd_mixer(hp, *sdp, h0_ctx)
            out_s, _ = ssd_mixer(hs, *sdp, state_ssd[:, j].astype(F32))
            new_ssd.append(st)
        xp = xp + (g_p[:, None] * out_p).astype(xp.dtype)
        xs = xs + (g_s[:, None] * out_s).astype(xs.dtype)
    y_prompt = rmsnorm(xp, final_norm_w).astype(x_prompt.dtype)
    y_sample = rmsnorm(xs, final_norm_w).astype(x_sample.dtype)
    return (y_prompt, y_sample, jnp.stack(new_re, axis=1), jnp.stack(new_im, axis=1), jnp.stack(new_ssd, axis=1))


_drawn_inputs = setup_inputs


def setup_inputs(seed=0):
    import zlib

    import numpy as np

    out = dict(_drawn_inputs(seed))
    spreads = {}
    factors = {'state_s5_re': 4.17,
     'state_s5_im': 4.166,
     'final_norm_w': 7.959,
     's5_a_re': 19.709,
     's5_c_re': 4.04,
     's5_c_im': 4.045,
     's5_d': 6.815,
     's5_glu_w': 2.896,
     's5_glu_b': 42.034,
     'hy_short_b': 8.0,
     'hy_f_b1': 8.0,
     'hy_f_freq1': 8.0,
     'hy_f_b2': 8.0,
     'hy_f_freq2': 64.0,
     'ssd_d': 4.725,
     'ssd_norm_w': 24.46}
    for name, (base, spread) in spreads.items():
        noise = np.random.default_rng([zlib.crc32(name.encode()), seed]).standard_normal(out[name].shape)
        drawn = base * np.exp(spread * noise) if base else spread * noise
        out[name] = __import__('jax').numpy.asarray(drawn.astype(out[name].dtype))
    for name, factor in factors.items():
        out[name] = (out[name] * factor).astype(out[name].dtype)
    return out
```

```python
import math

import numpy as np

import concourse.bass as bass
from concourse import mybir

F32 = mybir.dt.float32
BF16 = mybir.dt.bfloat16
ALU = mybir.AluOpType
ACT = mybir.ActivationFunctionType

P = 128
D = 1024
KT = D // P
NLAT, NCTX = 512, 128
NT = NLAT + NCTX
TT = NT // P
EPS = 1e-6
Q8 = 8
GS = 16
SP = 64
OCT = 8
NPAIR = 32
XC = NT // Q8 + 1
GAP = NLAT // Q8
SLOTS = XC + 1
SLOTW = 4 * NPAIR
LATX, CTXX = NLAT // Q8, NCTX // Q8
H1 = 1024
TWO_PI = 2.0 * math.pi
C1, C2 = 6.28125, float(np.float32(TWO_PI - 6.28125))
C3 = TWO_PI - 6.28125 - C2
MAGIC = 12582912.0
HW = 256
NW = H1 // HW
SH = 32
SHD = 64
SN = 128
SG = 4
DI = 2048

T_GF = 0
T_GI = T_GF + 2048
T_CS = T_GI + 2048
T_CX = T_CS + 2048
T_TN = T_CX + 640
T_M16 = T_TN + 5
T_UP = T_M16 + 16
T_LO = T_UP + 128
T_END = T_LO + 128


def constant_tables():
    n_all = 2 * NLAT
    korder = np.concatenate([np.arange(256), 511 - np.arange(256)])
    t = np.zeros((P, T_END), np.float64)
    w = TWO_PI * (korder + 0.5) / n_all
    s = (-1.0) ** korder
    for sign_i, sign in enumerate((1.0, -1.0)):
        for kt in range(2):
            tau = kt * P + np.arange(P)[:, None] + 0.5
            t[:, T_GF + (kt * 2 + sign_i) * 512:][:, :512] = np.cos(w * tau) + sign * s * np.sin(w * tau)
        for kt in range(4):
            wk, sk = w[kt * P:(kt + 1) * P, None], s[kt * P:(kt + 1) * P, None]
            tau = np.arange(256)[None, :] + 0.5
            t[:, T_GI + (kt * 2 + sign_i) * 256:][:, :256] = (np.cos(wk * tau) + sign * sk * np.sin(wk * tau)) / n_all
    for kt in range(4):
        n = lag_of(kt)[:, None]
        t[:, T_CS + kt * 512:][:, :256] = np.cos(w[:256] * n)
        t[:, T_CS + kt * 512 + 256:][:, :256] = s[:256] * np.sin(w[:256] * n)
    wc = TWO_PI * (np.arange(P) + 0.5) / (2 * NCTX)
    a = wc[None, :] * np.arange(P)[:, None]
    for i, m in enumerate((np.cos(a), -np.sin(a), np.sin(a), np.cos(a.T) / NCTX, -np.sin(a.T) / NCTX)):
        t[:, T_CX + i * P:][:, :P] = m
    f = np.float32
    for kt in range(4):
        t[:, T_TN + kt] = -(lag_of(kt).astype(f) / f(NLAT - 1))
    t[:, T_TN + 4] = -(np.arange(P).astype(f) / f(NCTX - 1))
    r = np.arange(P)
    t[:, T_M16:T_M16 + 16] = (r[:, None] % 16) == np.arange(16)[None, :]
    t[:, T_UP:T_UP + P] = r[:, None] <= r[None, :]
    t[:, T_LO:T_LO + P] = r[:, None] >= r[None, :]
    bands = np.linspace(1e-4, 15, 16, dtype=f)
    emb = np.zeros((33, NT), f)
    for L, cols, n in ((NLAT, slice(0, NLAT), np.concatenate([lag_of(k) for k in range(4)])), (NCTX, slice(NLAT, NT), r)):
        tm = n.astype(f)[:, None]
        ang = (f(2.0 * math.pi / L) * tm * bands).astype(f)
        emb[:, cols] = np.concatenate([tm / f(L - 1), np.cos(ang), np.sin(ang)], -1).T
    target = math.log(1e-2)
    deltas = np.abs(np.linspace(target / 1.5, target / 0.3, H1, dtype=f))[None, :]
    return t.astype(f), emb, deltas


def lag_of(kt):
    return 2 * (P * (kt % 2) + np.arange(P)) + kt // 2


class Arena:

    def __init__(self, tensor, width):
        self.tensor, self.width, self.taken = tensor, width, []

    def place(self, size, first, last):
        start = 0
        for a, b, f, l in sorted(self.taken):
            if f <= last and first <= l and a < start + size and start < b:
                start = b
        size += size % 2
        if start + size > self.width:
            raise ValueError(f"SBUF is full: {start + size} of {self.width} in stages {first}-{last}")
        self.taken.append((start, start + size, first, last))
        return start

    def at(self, base, dims, p0=0, np_=P):
        return bass.AP(self.tensor, p0 * self.width + base, [[self.width, np_]] + [list(d) for d in dims])


def build(nc, a, outs):
    from contextlib import ExitStack
    with ExitStack() as ctx:
        sems = {}

        def S(name):
            if name not in sems:
                sems[name] = ctx.enter_context(nc.semaphore(name))
            return sems[name]

        def psum(name, shape):
            return ctx.enter_context(nc.psum_tensor(name, shape, F32))

        width = 53200
        arena = Arena(ctx.enter_context(nc.sbuf_tensor("arena", [P, width], F32)), width)
        place, at = arena.place, arena.at
        GP = psum("gemm_pair", [P, 2, 1024])
        MP = psum("misc_banks", [P, 4, 512])

        RING, RSLOT, NSLOT = place(4 * 2048, 1, 9), 2048, 4
        IDENT, ONES = place(P, 1, 9), place(P, 1, 9)
        VR, VC = place(3 * P, 1, 1), place(3 * P, 1, 9)
        TAB = place(T_END - T_TN, 1, 9)
        SC, MV, AB, EPSB, STAT = place(16, 1, 9), place(96, 1, 9), place(32, 1, 9), place(2, 1, 9), place(40, 1, 9)
        HT = place(8 * NT, 1, 9)
        SVC = place(5 * 64, 1, 2)
        PC, PW = place(2 * 2 * NPAIR * 9, 1, 3), place(2 * 9 * 64, 1, 2)
        BBAR = place(2 * 64 * GS, 1, 3)
        SCA = place(256, 1, 2)
        X1 = place(TT * D, 1, 1)
        XN, SQ = place(2 * D, 1, 1), place(D, 1, 1)
        SV5, BRAW, TMP5 = place(5 * P, 1, 1), place(2 * 64 * GS, 1, 1), place(16 * 64, 1, 1)
        TMPB = place(2 * 1024, 1, 1)
        U, HS = place(64 * XC, 2, 4), place(SLOTS * SLOTW, 2, 3)
        GB = place(8 * NT, 2, 7)
        UT, MT = place(2 * NT, 2, 2), place(2 * 1024, 2, 2)
        BB, BL, TB = place(2 * 2048, 2, 2), place(2048, 2, 2), place(1024, 2, 2)
        SCT = place(512, 2, 2)
        YT, YW = U, 8 * XC
        CV, TC = place(2 * NT, 3, 5), place(576, 3, 3)
        CRAW, CT = place(2 * 2 * OCT * SP, 3, 3), place(384, 3, 3)
        CE, BBD = place(2 * 2304, 3, 3), place(512, 3, 3)
        WS, TTB = place(2 * 240, 3, 3), place(2 * 1024, 3, 3)
        YS, MT2 = place(8 * XC, 3, 3), place(1024, 3, 3)
        FS, FO = place(128, 3, 3), place(256, 3, 3)
        TA, TG = place(2 * NT, 4, 4), place(2 * NT, 4, 4)
        ZA = place(8 * NT, 4, 7)
        VS, XS, PQ = place(5 * H1, 5, 6), place(5 * H1, 5, 6), place(2 * NT, 5, 5)
        GF, GI, DEL = HT, HT + 2048, HT + 4096
        CS, CX = place(2048, 6, 6), place(640, 6, 6)
        TAPS, KH = place(2 * 5 * HW, 6, 6), place(2 * 5 * HW, 6, 6)
        FQ, PR = place(2 * 5 * HW, 6, 6), place(2 * 5 * HW, 6, 6)
        WIN, FE, FO2 = place(5 * HW, 6, 6), place(NT, 6, 6), place(NT, 6, 6)
        W3, FBIAS = place(2 * HW, 6, 6), place(2 * HW, 6, 6)
        HTMP, FCOL, MTMP = place(HW, 6, 6), place(4, 6, 6), place(HW, 6, 6)
        PT = YT2 = place(640, 6, 6)
        EMB, FA, FK = TAPS, FQ, PR
        XRES = place(TT * D, 7, 7)
        GR, DG = place(2 * D, 7, 7), place(2 * D, 7, 7)
        RT = place(1024, 7, 7)
        XN7, SQ7 = place(2 * D, 7, 7), place(D, 7, 7)
        Y = place(TT * DI, 8, 9)
        XCH, XT = place(4 * NT, 8, 8), place(TT * 512, 8, 8)
        BC, BTOK = place(2 * 2 * NT, 8, 8), place(TT * P, 8, 8)
        CBM, HP = place(2 * TT * P, 8, 8), place(2 * 4 * 512, 8, 8)
        XW, XD, YTMP = place(2 * 512, 8, 8), place(2 * 512, 8, 8), place(2 * 512, 8, 8)
        AM, EX, MM = place(2 * 1024, 8, 8), place(1024, 8, 8), place(2 * 1024, 8, 8)
        INIT, FOUT = place(2 * 512, 8, 8), place(2 * 512, 8, 8)
        CW = 2 * TT * SH
        DTB, AD, EE, WW, TOT, SPT = (place(n * CW, 8, 8) for n in (1, 1, 1, 1, 1, 3))
        SGT, SLT = place(P, 8, 8), place(P, 8, 8)
        BROW, AROW, DROW = place(64, 8, 8), place(64, 8, 8), place(SH, 8, 8)
        XRES9 = place(TT * D, 9, 9)
        GR9, DG9 = place(2 * D, 9, 9), place(2 * D, 9, 9)
        RT9, FNW = place(1024, 9, 9), place(D, 9, 9)
        ZT, SZ, SQZ = place(16 * NT, 9, 9), place(4 * 256, 9, 9), place(256, 9, 9)
        SQ9, SUMS = DG9, place(48, 9, 9)
        spill = nc.dram_tensor("residual_rows", (TT, P, D), F32, kind="Internal").ap()
        strips = nc.dram_tensor("strips", (OCT, P, 240), F32, kind="Internal").ap()
        turn_of = {}
        gemm_of = {}

        def ring(slot):
            return RING + slot * RSLOT

        def vcol(tile, row):
            return at(VC + tile * P + row, [(1, 1)])

        chunk = {}
        n = 0
        for name, cnt in (("mod0", 12), ("u", 4), ("gb", 4), ("x2", 4), ("ga_glu", 8), ("v", 4), ("x1", 4), ("mod1", 12),
                          ("ev_out", 8), ("ssd_dt", 1), ("ssd_g", 12), ("ssd_z", 8), ("ssd_out", 8)):
            chunk[name] = n
            n += cnt

        def barrier(eng, k):
            eng.drain().then_inc(S("stage_end"), 1)
            eng.wait_ge(S("stage_end"), 4 * k)

        STATES = ((0, 4), (1, 4), (0, 0), (1, 3), (0, 1), (1, 2), (0, 2), (1, 1))

        def coef(buf, d, t, g, n):
            return at(buf + d * TT * SH + t * SH + 8 * g, [(1, 8), (0, n)])

        block = ctx.enter_context(nc.Block())

        @block.tensor
        def _(pe):
            mm, tr = nc.tensor.matmul, nc.tensor.transpose
            ident = at(IDENT, [(1, P)])

            def turn(*name):
                t = turn_of[name] = len(turn_of)
                if t >= 4:
                    pe.wait_ge(S(f"bank_read{t % 4}"), t // 4)
                return MP[:, t % 4, :]

            def filled(ins):
                ins.then_inc(S("bank_filled"), 1)

            def ring_wait(i):
                pe.wait_ge(S(f"ring_full{i % NSLOT}"), 16 * (i // NSLOT + 1))

            def mod_vectors(layer):
                bank = turn("mod", layer)
                base = chunk[f"mod{layer}"]
                with pe.Fori(0, 3) as it:
                    for j in range(4):
                        pe.wait_ge(S(f"ring_full{(base + j) % NSLOT}"), it * 16 + 16 * ((base + j) // NSLOT + 1))
                        for m in range(2):
                            for k in range(KT):
                                last = mm(bank[:, bass.ds(it * 16 + (j * 4 + m * 2), 2)],
                                          at(ring((base + j) % NSLOT) + k * 256 + m * P, [(1, P)]),
                                          at(SC + 2 * k, [(1, 2)]), start=k == 0, stop=k == KT - 1)
                        last.then_inc(S("ring_used"), 1)
                filled(tr(bank[0:2, 64:192], at(SC, [(1, 2)]), ident))

            def normed_transposed(layer):
                xn = XN7 if layer else XN
                for t in range(TT):
                    pe.wait_ge(S("xn_ready"), layer * TT + t + 1)
                    for half in range(2):
                        bank = turn("xt", layer, t, half)
                        for j in range(4):
                            i = tr(bank[:, j * P:(j + 1) * P], at(xn + (t % 2) * D + (half * 4 + j) * P, [(1, P)]), ident)
                        filled(i)

            def gemm_tile(name, o, ci, m, rhs=HT, rw=NT):
                g = gemm_of[name, o] = len(gemm_of)
                if g >= 2:
                    pe.wait_ge(S(f"gemm_read{g % 2}"), g // 2)
                for k in range(KT):
                    w = at(ring(ci % NSLOT) + k * 256 + m * P, [(1, P)])
                    mm(GP[:, g % 2, 0:NLAT], w, at(rhs + k * rw, [(1, NLAT)]), start=k == 0, stop=k == KT - 1)
                    i = mm(GP[:, g % 2, NLAT:NT], w, at(rhs + k * rw + NLAT, [(1, NCTX)]), start=k == 0, stop=k == KT - 1)
                i.then_inc(S("gemm_filled"), 1)

            def part_tile(name, o, rhs=HT):
                ci = chunk[name] + o // 2
                if o % 2 == 0:
                    ring_wait(ci)
                gemm_tile(name, o, ci, o % 2, rhs)
                if o % 2:
                    used()

            def used():
                pe.wait_ge(S("gemm_filled"), len(gemm_of))
                pe.sem_inc(S("ring_used"), 1)

            pe.wait_ge(S("ident_ready"), 3)
            pe.wait_ge(S("rows_loaded"), 16 * 15)
            bank = turn("vec")
            for i, rows in enumerate((80, 112, 112)):
                last = tr(bank[:, i * P:i * P + rows], at(VR + i * P, [(1, P)], 0, rows), at(IDENT, [(1, rows)], 0, rows))
            filled(last)
            bank = turn("s5v")
            pe.wait_ge(S("s5rows"), 1)
            for i in range(5):
                last = tr(bank[:, i * 64:(i + 1) * 64], at(SV5 + i * P, [(1, P)], 0, 64), at(IDENT, [(1, 64)], 0, 64))
            filled(last)
            pe.wait_ge(S("cond_ready"), 1)
            mod_vectors(0)
            normed_transposed(0)
            barrier(pe, 1)

            def chunk_inputs(o):
                pe.wait_ge(S("ut_ready"), o + 1)
                for half in range(2):
                    bank = turn("ma", o, half)
                    for j in range(4):
                        i = tr(bank[0:80, j * P:(j + 1) * P], at(UT + (o % 2) * NT + half * 4 + j, [(Q8, 80)]), ident)
                    filled(i)
                pe.wait_ge(S("bb_ready"), o + 1)
                for dc in range(4):
                    bank = turn("bt", o, dc)
                    for q in range(4):
                        i = tr(bank[:, q * P:(q + 1) * P], at(BB + (o % 2) * 2048 + (dc * 4 + q) * P, [(1, P)]), ident)
                    filled(i)
                pe.wait_ge(S("mt_ready"), 2 * o + 2)
                for half in range(2):
                    bank = turn("ub", o, half)
                    for j in range(4):
                        i = tr(bank[:, j * 80:(j + 1) * 80], at(MT + (o % 2) * 1024 + (half * 4 + j) * P, [(1, P)], 0, 80),
                               at(IDENT, [(1, 80)], 0, 80))
                    filled(i)
                pe.wait_ge(S("u_ready"), 2 * o + 2)
                for dc in range(4):
                    pe.wait_ge(S("bl_ready"), 4 * o + dc + 1)
                    bank = turn("s", o, dc)
                    for q in range(4):
                        for g2 in range(2):
                            i = mm(bank[64 * g2:64 * g2 + 64, q * XC:(q + 1) * XC],
                                   at(BL + (dc * 4 + q) * P + 64 * g2, [(1, 64)]),
                                   at(U + (8 * o + 2 * q + g2) * XC, [(1, XC)]), start=True, stop=True)
                    filled(i)

            pe.wait_ge(S("u_gap"), 1)
            part_tile("u", 0)
            for o in range(OCT):
                if o + 1 < OCT:
                    part_tile("u", o + 1)
                chunk_inputs(o)
            for o in range(OCT):
                part_tile("gb", o)
            barrier(pe, 2)

            def c_transposed(o):
                bank = turn("ct", o)
                for dc in range(4):
                    for e in range(2):
                        i = mm(bank[64 * e:64 * e + 64, dc * 64:dc * 64 + 64],
                               at(CRAW + ((dc % 2 * 2 + dc // 2) * OCT + o) * SP, [(1, SP)]),
                               at(IDENT + 16 * e, [(32, 4), (1, 16)]), start=True, stop=True)
                filled(i)

            def lag_kernels(o):
                pe.wait_ge(S("ce_ready"), o + 1)
                bank = turn("k", o)
                for d in range(2):
                    for q in range(4):
                        for c in range(2):
                            i = mm(bank[32 * q:32 * q + 32, d * P:(d + 1) * P],
                                   at(BBD + (2 * d + c) * P + q * 32, [(1, 32)]),
                                   at(CE + (o % 2) * 2304 + ((2 * d + c) * 4 + q) * 144 + 16 * d, [(1, P)]),
                                   start=c == 0, stop=c == 1)
                filled(i)

            def s5_output(o):
                pe.wait_ge(S(f"t_loaded{o % 2}"), 16 * 8 * (o // 2 + 1))
                banks = [turn("y", o, e) for e in range(2)]
                for q in range(4):
                    for e in range(2):
                        mm(banks[e][:, q * XC:(q + 1) * XC], at(TTB + (o % 2) * 1024 + (2 * q + e) * P, [(1, P)]),
                           at(U + (8 * o + 2 * q + e) * XC, [(1, XC)]), start=True, stop=False)
                    for dc in range(4):
                        d, c = dc // 2, dc % 2
                        slot0, step = (0, SLOTW) if d == 0 else (XC - 1, -SLOTW)
                        for e in range(2):
                            i = mm(banks[e][:, q * XC:(q + 1) * XC],
                                   at(CE + (o % 2) * 2304 + (dc * 4 + q) * 144 + 16 * (1 - d), [(1, P)], 64 * e, 64),
                                   at(HS + slot0 * SLOTW + d * 64 + c * 32 + 4 * o + q, [(step, XC)], 64 * e, 64),
                                   start=False, stop=dc == 3)
                            if dc == 3 and q == 3:
                                filled(i)
                for half in range(2):
                    pe.wait_ge(S("ys_ready"), 2 * o + half + 1)
                    bank = turn("yt", o, half)
                    for j in range(4):
                        i = tr(bank[0:XC, j * P:(j + 1) * P], at(YS + (half * 4 + j) * XC, [(1, XC)]), ident)
                    filled(i)
                pe.wait_ge(S("mt2_ready"), 2 * o + 2)
                for half in range(2):
                    bank = turn("yc", o, half)
                    for j in range(4):
                        i = tr(bank[:, j * XC:(j + 1) * XC], at(MT2 + (half * 4 + j) * P, [(1, P)], 0, XC),
                               at(IDENT, [(1, XC)], 0, XC))
                    filled(i)

            pe.wait_ge(S("fs_ready"), 1)
            bank = turn("fs")
            for c in range(2):
                i = tr(bank[0:64, c * P:(c + 1) * P], at(FS + c * 64, [(1, 64)]), ident)
            filled(i)
            pe.wait_ge(S("c_loaded"), 16 * 4)
            c_transposed(0)
            for o in range(OCT + 1):
                if o < OCT:
                    part_tile("x2", o)
                    lag_kernels(o)
                if o + 1 < OCT:
                    c_transposed(o + 1)
                if o >= 1:
                    s5_output(o - 1)
            barrier(pe, 3)

            for ch in range(4):
                ci = chunk["ga_glu"] + 2 * ch
                ring_wait(ci)
                for m in range(2):
                    gemm_tile("ga", 2 * ch + m, ci, m)
                used()
                ring_wait(ci + 1)
                for m in range(2):
                    gemm_tile("glu", 2 * ch + m, ci + 1, m, YT, YW)
                used()
            barrier(pe, 4)

            def token_major(name, o):
                for half in range(2):
                    if half == 0:
                        pe.wait_ge(S(name + "_conv"), o + 1)
                    bank = turn(name + "t", o, half)
                    for j in range(4 if half == 0 else 1):
                        i = tr(bank[:, j * P:(j + 1) * P], at(PQ + (o % 2) * NT + (half * 4 + j) * P, [(1, P)]), ident)
                    filled(i)
            for name in ("v", "x1"):
                for o in range(OCT + 1):
                    if o < OCT:
                        part_tile(name, o)
                    if o >= 1:
                        token_major(name, o - 1)
            barrier(pe, 5)

            def mod_batch(b):
                bank = turn("mod1", b)
                for j in range(3):
                    ci = chunk["mod1"] + 3 * b + j
                    ring_wait(ci)
                    for m in range(2):
                        for k in range(KT):
                            i = mm(bank[:, (2 * j + m) * 2:(2 * j + m) * 2 + 2], at(ring(ci % NSLOT) + k * 256 + m * P, [(1, P)]),
                                   at(SC + 2 * k, [(1, 2)]), start=k == 0, stop=k == KT - 1)
                    if j < 2:
                        i.then_inc(S("ring_used"), 1)
                filled(i)
                pe.wait_ge(S("bank_filled"), len(turn_of))
                pe.sem_inc(S("ring_used"), 1)

            def mlp(n, w, kn, m, src):
                for half, (c0, cn) in enumerate(((0, 512), (512, P))):
                    bank = turn("mlp", n, half)
                    filled(mm(bank[0:m, 0:cn], at(w, [(1, m)], 0, kn), at(src + c0, [(1, cn)], 0, kn), start=True, stop=True))

            def taps(i):
                w, r = i // 2, i % 2
                if r == 0:
                    pe.wait_ge(S("w3_loaded"), 64 * (w + 1))
                for n in range(5):
                    bank = turn("f", i, n)
                    rhs = at(W3 + r * HW, [(1, HW)])
                    biased = n in (0, 4)
                    mm(bank[:, 0:HW], at(FE + n * P, [(1, P)]), rhs, start=True, stop=not biased)
                    if biased:
                        mm(bank[:, 0:HW], at(IDENT, [(1, P)], 0, 1), at(FBIAS + r * HW, [(1, HW)], 0, 1), start=False, stop=True)
                    filled(mm(bank[:, HW:2 * HW], at(FO2 + n * P, [(1, P)]), rhs, start=True, stop=True))

            def filter_transform(i):
                pe.wait_ge(S("taps_ready"), i + 1)
                for kind in range(2):
                    for ft in range(2):
                        bank = turn("kh", i, kind, ft)
                        for par in range(2):
                            for kt in range(2):
                                n = par * 2 + kt
                                j = mm(bank[:, par * HW:(par + 1) * HW], at(CS + n * 512 + kind * 256 + ft * P, [(1, P)]),
                                       at(TAPS + (kind * 5 + n) * HW, [(1, HW)]), start=kt == 0, stop=kt == 1)
                        filled(j)
                bank = turn("khc", i)
                for kind in range(2):
                    j = mm(bank[:, kind * HW:(kind + 1) * HW], at(CX + (0, 2)[kind] * P, [(1, P)]),
                           at(TAPS + (kind * 5 + 4) * HW, [(1, HW)]), start=True, stop=True)
                filled(j)

            def input_transform(i):
                w, r = i // 2, i % 2
                if r:
                    pe.wait_ge(S("z_ready"), w + 1)
                for ft in range(4):
                    bank = turn("vf", i, ft)
                    for pm in range(2):
                        for kt in range(2):
                            j = mm(bank[:, pm * HW:(pm + 1) * HW], at(GF + (kt * 2 + pm) * 512 + ft * P, [(1, P)]),
                                   at(VS + (pm * 2 + kt) * H1 + w * HW, [(1, HW)]), start=kt == 0, stop=kt == 1)
                    filled(j)
                bank = turn("vf", i, 4)
                for pm in range(2):
                    j = mm(bank[:, pm * HW:(pm + 1) * HW], at(CX + pm * P, [(1, P)]), at(VS + 4 * H1 + w * HW, [(1, HW)]),
                           start=True, stop=True)
                filled(j)

            def inverse_transform(i):
                pe.wait_ge(S("pr_ready"), i + 1)
                for tt in range(2):
                    bank = turn("yi", i, tt)
                    for pm in range(2):
                        for ft in range(4):
                            j = mm(bank[:, pm * HW:(pm + 1) * HW], at(GI + (ft * 2 + pm) * 256 + tt * P, [(1, P)]),
                                   at(PR + (pm * 5 + ft) * HW, [(1, HW)]), start=ft == 0, stop=ft == 3)
                    filled(j)
                bank = turn("yi", i, 2)
                for pm in range(2):
                    j = mm(bank[:, 0:HW], at(CX + (3 + pm) * P, [(1, P)]), at(PR + (pm * 5 + 4) * HW, [(1, HW)]),
                           start=pm == 0, stop=pm == 1)
                filled(j)

            def channel_major(w):
                pe.wait_ge(S("yh_ready"), w + 1)
                for m in range(2):
                    bank = turn("zt", w, m, 0)
                    for n in range(4):
                        j = tr(bank[:, n * P:(n + 1) * P], at(VS + n * H1 + w * HW + m * P, [(1, P)]), ident)
                    filled(j)
                    bank = turn("zt", w, m, 1)
                    filled(tr(bank[:, 0:P], at(VS + 4 * H1 + w * HW + m * P, [(1, P)]), ident))

            pe.wait_ge(S("mlp_loaded"), 16 * 5)
            mlp(1, W3 + HW, 33, 64, EMB)
            pe.wait_ge(S("mlp_ready"), 1)
            mlp(2, W3, 64, P, EMB + 640)
            pe.wait_ge(S("mlp_ready"), 2)
            pe.wait_ge(S("hy_tables"), 16 * 4)
            taps(0)
            filter_transform(0)
            for i in range(2 * NW):
                input_transform(i)
                if i + 1 < 2 * NW:
                    taps(i + 1)
                inverse_transform(i)
                if i + 1 < 2 * NW:
                    filter_transform(i + 1)
                if i % 2:
                    mod_batch(i // 2)
                    channel_major(i // 2)
            barrier(pe, 6)

            def gate_rows(layer):
                pe.wait_ge(S("dg_ready"), layer + 1)
                for w in range(2):
                    for half in range(2):
                        bank = turn("gr", layer, w, half)
                        for j in range(4):
                            i = mm(bank[:, j * P:(j + 1) * P], at(ONES, [(1, P)]), at((DG9 if layer else DG) + w * D + (half * 4 + j) * P, [(1, P)]),
                                   start=True, stop=True)
                        filled(i)

            def out_projection(layer, name, ztile):
                for half in range(2):
                    if layer or half:
                        pe.wait_ge(S("acc_read"), 4 * (2 * layer + half))
                    t4 = turn("acc4", layer, half)
                    acc = [GP[:, b // 2, (b % 2) * 512:(b % 2) * 512 + 512] for b in range(4)] + [t4]
                    for c in range(4):
                        ci = chunk[name] + half * 4 + c
                        ring_wait(ci)
                        for kk in range(4):
                            k = 4 * c + kk
                            for t in range(TT):
                                i = mm(acc[t], at(ztile(k) + t * P, [(1, P)]), at(ring(ci % NSLOT) + kk * 512, [(1, 512)]),
                                       start=k == 0, stop=k == 15)
                        if c < 3:
                            i.then_inc(S("ring_used"), 1)
                    filled(i)
                    pe.wait_ge(S("bank_filled"), len(turn_of))
                    pe.sem_inc(S("ring_used"), 1)
            gate_rows(0)
            out_projection(0, "ev_out", lambda k: ZA + k * NT if k < 8 else GB + (k - 8) * NT)
            normed_transposed(1)
            barrier(pe, 7)

            ring_wait(chunk["ssd_dt"])
            bank = turn("dt")
            for t in range(TT):
                for k in range(KT):
                    i = mm(bank[:, t * 64:(t + 1) * 64], at(HT + k * NT + t * P, [(1, P)]), at(ring(chunk["ssd_dt"] % NSLOT) + k * 64, [(1, 64)]),
                           start=k == 0, stop=k == KT - 1)
            filled(i)
            pe.wait_ge(S("bank_filled"), len(turn_of))
            pe.sem_inc(S("ring_used"), 1)
            pe.wait_ge(S("ad_ready"), 1)
            for nm, masks in (("ce", (TAB + T_UP - T_TN, TAB + T_LO - T_TN)), ("cw", (SGT, SLT)), ("ctot", (ONES, ONES))):
                bank = turn(nm)
                for d in range(2):
                    i = mm(bank[:, d * 160:(d + 1) * 160], at(masks[d], [(1, P)]), at(AD + d * 160, [(1, 160)]), start=True, stop=True)
                filled(i)

            def ssd_gemm(n):
                if n % 6 == 1:
                    pe.wait_ge(S(f"ssd_c_loaded{n // 6 % 2}"), 16 * (n // 12 + 1))
                part_tile("ssd_g", n)
            for n in range(6):
                ssd_gemm(n)

            def decay_sums(g, t):
                pe.wait_ge(S("am_ready"), 2 * (TT * g + t + 1))
                for half in range(2):
                    bank = turn("ar", g, t, half)
                    for d, mask in enumerate((SGT, SLT)):
                        i = mm(bank, at(mask, [(1, P)]), at(AM + d * 1024 + half * 512, [(1, 512)]), start=d == 0, stop=d == 1)
                    filled(i)

            def group(g):
                bc = BC + (g % 2) * 2 * NT
                pe.wait_ge(S("cv_ready"), 6 * g + 6)
                for t in range(TT):
                    bank = turn("xg", g, t)
                    for j in range(4):
                        i = tr(bank[:, j * P:(j + 1) * P], at(XCH + j * NT + t * P, [(1, P)]), ident)
                    filled(i)
                for part in range(2):
                    bank = turn("bg", g, part)
                    for j in range((4, 1)[part]):
                        i = tr(bank[:, j * P:(j + 1) * P], at(bc + (4 * part + j) * P, [(1, P)]), ident)
                    filled(i)
                for part in range(2):
                    bank = turn("cb", g, part)
                    for j in range((4, 1)[part]):
                        tok = (4 * part + j) * P
                        i = mm(bank[:, j * P:(j + 1) * P], at(bc + tok, [(1, P)]), at(bc + NT + tok, [(1, P)]), start=True, stop=True)
                    filled(i)
                pe.wait_ge(S("init_loaded"), 32 * (g + 1))
                for d in range(2):
                    bank = turn("in", g, d)
                    for j in range(4):
                        i = tr(bank[:, j * P:(j + 1) * P], at(INIT + d * 512 + j * P, [(1, P)]), ident)
                    filled(i)
                decay_sums(g, 0)
                pe.wait_ge(S("btok_ready"), g + 1)
                for k, (d, t) in enumerate(STATES):
                    pe.wait_ge(S("xw_ready"), 8 * g + k + 1)
                    bank = turn("st", g, k)
                    xw = XW + (k % 2) * 512
                    if t == 4:
                        for j in range(4):
                            i = mm(bank[:, j * P:(j + 1) * P], at(xw + j * P, [(1, P)]), at(BTOK + t * P, [(1, P)]), start=True, stop=True)
                    else:
                        i = mm(bank, at(BTOK + t * P, [(1, P)]), at(xw, [(1, 512)]), start=True, stop=True)
                    filled(i)
                for t in range(TT):
                    if t + 1 < TT:
                        decay_sums(g, t + 1)
                    if g < 3:
                        ssd_gemm(6 * (g + 1) + t)
                    if t == 0:
                        pe.wait_ge(S("hp_ready"), g + 1)
                    if t < 4:
                        for d in range(2):
                            bank = turn("yo", g, t, d)
                            filled(mm(bank, at(bc + NT + t * P, [(1, P)]), at(HP + (4 * d + t) * 512, [(1, 512)]), start=True, stop=True))
                    pe.wait_ge(S("mm_ready"), TT * g + t + 1)
                    bank = turn("yd", g, t)
                    for h in range(8):
                        for d in range(2):
                            i = mm(bank[:, h * 64:(h + 1) * 64], at(MM + d * 1024 + h * P, [(1, P)]), at(XD + d * 512 + h * 64, [(1, 64)]),
                                   start=d == 0, stop=d == 1)
                    filled(i)
                if g < 3:
                    ssd_gemm(6 * (g + 1) + 5)
            for g in range(SG):
                group(g)
            barrier(pe, 8)

            def z_transposed(c):
                pe.wait_ge(S("yz_ready"), TT * (c + 1))
                for m in range(2):
                    bank = turn("zz", c, m)
                    for t in range(4):
                        i = tr(bank[:, t * P:(t + 1) * P], at(Y + t * DI + (2 * c + m) * P, [(1, P)]), ident)
                    filled(i)
                bank = turn("zz", c, 2)
                for m in range(2):
                    i = tr(bank[:, m * P:(m + 1) * P], at(Y + 4 * DI + (2 * c + m) * P, [(1, P)]), ident)
                filled(i)
            gate_rows(1)
            for c in range(8):
                ci = chunk["ssd_z"] + c
                ring_wait(ci)
                for t in range(TT):
                    bank = turn("z", c, t)
                    for k in range(KT):
                        i = mm(bank[:, 0:256], at(HT + k * NT + t * P, [(1, P)]), at(ring(ci % NSLOT) + k * 256, [(1, 256)]),
                               start=k == 0, stop=k == KT - 1)
                    filled(i)
                pe.wait_ge(S("bank_filled"), len(turn_of))
                pe.sem_inc(S("ring_used"), 1)
                if c:
                    z_transposed(c - 1)
            z_transposed(7)
            pe.wait_ge(S("zt_ready"), 8)
            out_projection(1, "ssd_out", lambda k: ZT + k * NT)

        @block.scalar
        def _(act):
            A = nc.scalar.activation
            chain = [0]

            def link(ins):
                chain[0] += 1
                ins.then_inc(S("act_chain"), 1)
                act.wait_ge(S("act_chain"), chain[0])

            def bank_of(*name):
                t = turn_of[name]
                act.wait_ge(S("bank_filled"), t + 1)
                return MP[:, t % 4, :], S(f"bank_read{t % 4}")

            def tile_of(name, o):
                g = gemm_of[name, o]
                act.wait_ge(S("gemm_filled"), g + 1)
                return GP[:, g % 2, 0:NT], S(f"gemm_read{g % 2}")

            def norm_stat(layer, t, xbuf):
                link(A(at(SQ7 if layer else SQ, [(1, D)]), at(xbuf + t * D, [(1, D)]), ACT.Square, accum_out=at(STAT + t, [(1, 1)])))
                A(at(STAT + 8 + t, [(1, 1)]), at(STAT + t, [(1, 1)]), ACT.Sqrt, bias=at(EPSB, [(1, 1)]),
                  scale=1.0 / D).then_inc(S("rms_ready"), 1)

            def modulated(layer):
                for t in range(TT):
                    which = 0 if t < 4 else 1
                    for half in range(2):
                        bank, read = bank_of("xt", layer, t, half)
                        if t == 0 and half == 0:
                            act.wait_ge(S("mod_ready"), layer + 1)
                        for j in range(4):
                            kd = half * 4 + j
                            i = A(at(HT + kd * NT + t * P, [(1, P)]), bank[:, j * P:(j + 1) * P], ACT.Identity,
                                  scale=at(AB + kd * 2 + which, [(1, 1)]), bias=at(MV + layer * 48 + kd * 2 + which, [(1, 1)]))
                        i.then_inc(read, 1)

            def rows(tile, row0, src):
                act.dma_start(at(VR + tile * P, [(1, P)], row0, src.shape[0]), src).then_inc(S("rows_loaded"), 16)
            r = lambda ap, pat, **k: ap.rearrange(pat, **k)
            rows(0, 0, r(a["c"], "a (k p) -> (a k) p", p=P))
            rows(0, 8, r(a["c_ctx"], "(k p) -> k p", p=P))
            rows(0, 16, r(a["norm_w"], "l (k p) -> (l k) p", p=P))
            rows(0, 32, r(a["mod_b"], "l (k p) -> (l k) p", p=P))
            rows(1, 0, r(a["s5_glu_b"], "a (k p) -> (a k) p", p=P))
            rows(1, 8, r(a["s5_d"], "a (k p) -> (a k) p", p=P))
            rows(1, 16, r(a["hy_short_b"], "a (k p) -> (a k) p", p=P))
            for tap in range(3):
                rows(1, 40 + 24 * tap, r(a["hy_short_w"][0, tap], "(k p) -> k p", p=P))
            rows(2, 0, r(a["ssd_conv_b"], "a (k p) -> (a k) p", p=P))
            for tap in range(3):
                rows(2, 24 + 24 * tap, r(a["ssd_conv_w"][0, tap], "(k p) -> k p", p=P))
            rows(2, 96, r(a["ssd_norm_w"], "a (k p) -> (a k) p", p=P))
            for i, nm in enumerate(("s5_a_re", "s5_a_im")):
                act.dma_start(at(SV5 + i * P, [(1, P)], 0, 64), r(a[nm], "a d (q e) p -> (a d q) (e p)", e=2)).then_inc(S("s5_loaded"), 16)
            for i, nm in enumerate(("state_s5_re", "state_s5_im")):
                act.dma_start(at(SV5 + (2 + i) * P, [(1, P)], 0, 64),
                              r(a[nm], "b a d (q e) p -> (b a d q) (e p)", e=2)).then_inc(S("s5_loaded"), 16)
            act.dma_start(at(TMP5, [(1, 2)], 0, 64), r(a["s5_log_dt"], "a d (q e) -> (a d q) e", e=2)).then_inc(S("s5_loaded"), 16)
            act.dma_start(at(TAB, [(1, T_END - T_TN)]), a["tables"][:, T_TN:T_END]).then_inc(S("tab_loaded"), 16)
            for i, nm in enumerate(("s5_b_re", "s5_b_im")):
                act.dma_start(at(BRAW + i * 1024, [(16, 64), (1, 16)]),
                              r(a[nm], "a d (q e) p h -> (e p) (a d q) h", e=2)).then_inc(S("b_loaded"), 16)

            bank, read = bank_of("vec")
            A(at(SC, [(1, 2), (2, 8)]), bank[:, 0:16].rearrange("p (w k) -> p w k", w=2), ACT.Silu).then_inc(S("cond_ready"), 1)
            A(at(VC, [(1, 3 * P)])[:, 0:80], bank[:, 0:80], ACT.Copy)
            A(at(VC + P, [(1, 112)]), bank[:, P:P + 112], ACT.Copy)
            A(at(VC + 2 * P, [(1, 112)]), bank[:, 2 * P:2 * P + 112], ACT.Copy).then_inc(read, 1)
            act.drain().then_inc(S("cols_ready"), 1)
            bank, read = bank_of("s5v")
            A(at(SVC, [(1, 256)]), bank[:, 0:256], ACT.Copy)
            A(at(SVC + 256, [(1, 64)]), bank[:, 256:320], ACT.Exp).then_inc(read, 1)
            act.drain().then_inc(S("svc_ready"), 1)
            for t in range(TT):
                act.wait_ge(S(f"x_loaded{t}"), 16)
                if t == 0:
                    act.wait_ge(S("eps_ready"), 1)
                norm_stat(0, t, X1)
            act.wait_ge(S("s5_arg"), 1)
            A(at(TMP5 + 64 * 1, [(1, 64)]), at(TMP5, [(1, 64)]), ACT.Exp)
            A(at(TMP5 + 64 * 3, [(1, 128)]), at(TMP5 + 64 * 5, [(1, 128)]), ACT.Sin).then_inc(S("s5_fun"), 1)
            modulated(0)
            barrier(act, 1)

            def u_copy(o):
                tile, read = tile_of("u", o)
                if o >= 2:
                    act.wait_ge(S("bank_filled"), turn_of["ma", o - 2, 1] + 1)
                A(at(UT + (o % 2) * NT, [(1, NT)]), tile, ACT.Copy).then_inc(read, 1)
                act.drain().then_inc(S("ut_ready"), 1)

            def octet(o):
                for dc in range(4):
                    bank, read = bank_of("bt", o, dc)
                    if o >= 1:
                        act.wait_ge(S("bank_filled"), turn_of["s", o - 1, dc] + 1)
                    A(at(BL + dc * 512, [(1, 512)]), bank, ACT.Copy).then_inc(read, 1)
                    act.drain().then_inc(S("bl_ready"), 1)
                for half in range(2):
                    bank, read = bank_of("ub", o, half)
                    src = bank[:, 0:320].rearrange("p (g x) -> p g x", g=4)
                    dst = U + (8 * o + 4 * half) * XC
                    A(at(dst, [(XC, 4), (1, LATX)]), src[:, :, 0:LATX], ACT.Copy)
                    A(at(dst + GAP + 1, [(XC, 4), (1, CTXX)]), src[:, :, LATX:80], ACT.Copy).then_inc(read, 1)
                    act.drain().then_inc(S("u_ready"), 1)
                for c in range(2):
                    bank, read = bank_of("s", o, c)
                    A(at(HS + SLOTW + c * NPAIR + 4 * o, [(1, 4), (SLOTW, XC)]),
                      bank[:, 0:4 * XC].rearrange("p (q x) -> p q x", q=4), ACT.Copy).then_inc(read, 1)

            u_copy(0)
            for o in range(OCT):
                if o + 1 < OCT:
                    u_copy(o + 1)
                octet(o)
            act.drain().then_inc(S("hs_forward"), 1)
            for o in range(OCT):
                tile, read = tile_of("gb", o)
                A(at(GB + o * NT, [(1, NT)]), tile, ACT.Silu).then_inc(read, 1)
            barrier(act, 2)

            def conv_center(name, o, part, n):
                tile, _ = tile_of(name, o)
                if n >= 2:
                    act.wait_ge(S("cv_free"), n - 1)
                A(at(CV + (n % 2) * NT, [(1, NT)]), tile, ACT.Identity, scale=vcol(1, 40 + 24 + 8 * part + o),
                  bias=vcol(1, 16 + 8 * part + o)).then_inc(S("cv_center"), 1)

            bank, read = bank_of("fs")
            A(at(FO, [(1, 256)], 0, 64), bank[0:64, 0:256], ACT.Copy).then_inc(read, 1)
            act.drain().then_inc(S("fo_ready"), 1)
            def c_copies(o):
                bank, read = bank_of("ct", o)
                if o >= 1:
                    act.wait_ge(S("ce_ready"), o)
                src = bank[:, 0:256].rearrange("p (d c h) -> p d c h", d=2, c=2)
                A(at(CT, [(64, 2), (1, 64)]), src[:, :, 0, :], ACT.Copy)
                A(at(CT + 128, [(64, 2), (1, 64)]), src[:, :, 1, :], ACT.Copy, scale=-1.0)
                A(at(CT + 256, [(64, 2), (1, 64)]), src[:, :, 0, :], ACT.Copy, scale=-1.0).then_inc(read, 1)
                act.drain().then_inc(S("ct_ready"), 1)

            c_copies(0)
            for o in range(OCT + 1):
                if o < OCT:
                    conv_center("x2", o, 2, o)
                if o + 1 < OCT:
                    c_copies(o + 1)
                if o >= 1:
                    for half in range(2):
                        bank, read = bank_of("y", o - 1, half)
                        if o >= 2 and half == 0:
                            act.wait_ge(S("bank_filled"), turn_of["yt", o - 2, 1] + 1)
                        A(at(YS + half * 4 * XC, [(1, 4 * XC)]), bank[:, 0:4 * XC], ACT.Copy).then_inc(read, 1)
                        act.drain().then_inc(S("ys_ready"), 1)
                    for half in range(2):
                        bank, read = bank_of("yc", o - 1, half)
                        src = bank[:, 0:4 * XC].rearrange("p (t x) -> p t x", t=4)
                        dst = YT + (o - 1) * YW + 4 * half
                        A(at(dst, [(1, 4), (Q8, LATX)]), src[:, :, 0:LATX], ACT.Gelu_apprx_tanh)
                        A(at(dst + NLAT, [(1, 4), (Q8, CTXX)]), src[:, :, GAP + 1:XC], ACT.Gelu_apprx_tanh).then_inc(read, 1)
            barrier(act, 3)

            for ch in range(4):
                for m in range(2):
                    o = 2 * ch + m
                    tile, read = tile_of("ga", o)
                    if ch:
                        act.wait_ge(S("za_done"), o - 1)
                    A(at(TA + m * NT, [(1, NT)]), tile, ACT.Silu).then_inc(read, 1)
                for m in range(2):
                    o = 2 * ch + m
                    tile, read = tile_of("glu", o)
                    A(at(TG + m * NT, [(1, NT)]), tile, ACT.Sigmoid, bias=vcol(1, o)).then_inc(read, 1)
                    act.drain().then_inc(S("glu_ready"), 1)
            barrier(act, 4)

            n = 8
            for name, part, dst in (("v", 0, VS), ("x1", 1, XS)):
                for o in range(OCT + 1):
                    if o < OCT:
                        conv_center(name, o, part, n)
                        n += 1
                    if o >= 1:
                        bank, read = bank_of(name + "t", o - 1, 0)
                        A(at(dst + (o - 1) * P, [(H1, 4), (1, P)]), bank.rearrange("p (a b) -> p a b", a=4), ACT.Copy).then_inc(read, 1)
                        bank, read = bank_of(name + "t", o - 1, 1)
                        A(at(dst + 4 * H1 + (o - 1) * P, [(1, P)]), bank[:, 0:P], ACT.Copy).then_inc(read, 1)
            barrier(act, 5)

            def sine(n, dst, rows):
                act.wait_ge(S("sin_arg"), n)
                A(at(dst, [(1, NT)], 0, rows), at(FA, [(1, NT)], 0, rows), ACT.Sin)
                act.drain().then_inc(S("sin_done"), 1)
            act.wait_ge(S("hy_tables"), 16 * 4)
            sine(1, EMB + 640, 64)
            sine(2, FE, P)

            def windows(w):
                for n in range(5):
                    A(at(WIN + n * HW, [(1, HW)]), at(DEL + w * HW, [(1, HW)]), ACT.Exp, scale=at(TAB + n, [(1, 1)]))
                act.drain().then_inc(S("win_ready"), 1)

            def kh_copies(i):
                for kind in range(2):
                    for ft in range(2):
                        bank, _ = bank_of("kh", i, kind, ft)
                        n = 4 * i + 2 * kind + ft
                        if n >= 1:
                            act.wait_ge(S("kh_done"), n)
                        A(at(HTMP, [(1, HW)]), bank[:, HW:2 * HW], ACT.Copy).then_inc(S("kh_odd"), 1)
                bank, read = bank_of("khc", i)
                A(at(KH + 4 * HW, [(5 * HW, 2), (1, HW)]), bank.rearrange("p (a b) -> p a b", a=2), ACT.Copy).then_inc(read, 1)
                act.drain().then_inc(S("khc_ready"), 1)

            def vf_copies(i):
                if i:
                    act.wait_ge(S("pr_ready"), i)
                for ft in range(5):
                    bank, read = bank_of("vf", i, ft)
                    A(at(FQ + ft * HW, [(5 * HW, 2), (1, HW)]), bank.rearrange("p (a b) -> p a b", a=2), ACT.Copy).then_inc(read, 1)
                act.drain().then_inc(S("fq_ready"), 1)

            def yi_copies(i):
                for tt in range(2):
                    bank, _ = bank_of("yi", i, tt)
                    n = 2 * i + tt
                    if n >= 1:
                        act.wait_ge(S("yi_done"), n)
                    A(at(MTMP, [(1, HW)]), bank[:, HW:2 * HW], ACT.Copy).then_inc(S("yi_odd"), 1)
            windows(0)
            kh_copies(0)
            for i in range(2 * NW):
                vf_copies(i)
                if i % 2 and i + 1 < 2 * NW:
                    act.wait_ge(S("taps_ready"), i + 1)
                    windows(i // 2 + 1)
                yi_copies(i)
                if i + 1 < 2 * NW:
                    kh_copies(i + 1)
            barrier(act, 6)

            def gate_copies(layer):
                for w in range(2):
                    for half in range(2):
                        bank, read = bank_of("gr", layer, w, half)
                        A(at((GR9 if layer else GR) + w * D + half * 512, [(1, 512)]), bank, ACT.Copy).then_inc(read, 1)
                act.drain().then_inc(S("gr_ready"), 1)
            gate_copies(0)
            for t in range(TT):
                act.wait_ge(S("res_ready"), t + 1)
                norm_stat(1, t, XRES)
            modulated(1)
            barrier(act, 7)

            act.wait_ge(S("ssd_rows"), 48)
            A(at(AROW, [(1, 64)]), at(AROW, [(1, 64)]), ACT.Exp).then_inc(S("arow_ready"), 1)
            act.wait_ge(S("sp_arg"), 1)
            A(at(SPT + CW, [(1, CW)]), at(SPT + CW, [(1, CW)]), ACT.Exp).then_inc(S("sp_exp"), 1)
            for nm, dst in (("ce", EE), ("cw", WW), ("ctot", TOT)):
                bank, read = bank_of(nm)
                A(at(dst, [(1, CW)]), bank[:, 0:CW], ACT.Exp).then_inc(read, 1)
            act.drain().then_inc(S("coef_exp"), 1)

            def ssd_tile(n):
                g, j = n // 6, n % 6
                if j < 2:
                    return 16 + 4 * j + g, BC + (g % 2) * 2 * NT + j * NT
                return 4 * g + j - 2, XCH + (j - 2) * NT

            def center(n):
                tile, _ = tile_of("ssd_g", n)
                o, dst = ssd_tile(n)
                A(at(dst, [(1, NT)]), tile, ACT.Identity, scale=vcol(2, 24 + 24 + o), bias=vcol(2, o)).then_inc(S("cv_center8"), 1)

            def silu(n):
                act.wait_ge(S("cv_sides"), n + 1)
                o, dst = ssd_tile(n)
                A(at(dst, [(1, NT)]), at(dst, [(1, NT)]), ACT.Silu).then_inc(S("cv_ready"), 1)

            def decays(g, t):
                if TT * g + t:
                    act.wait_ge(S("mm_ready"), TT * g + t)
                for half in range(2):
                    bank, read = bank_of("ar", g, t, half)
                    A(at(EX + half * 512, [(1, 512)]), bank, ACT.Exp).then_inc(read, 1)
                act.drain().then_inc(S("ex_ready"), 1)

            center(0)
            for n in range(6):
                if n + 1 < 6:
                    center(n + 1)
                silu(n)
            for g in range(SG):
                if g:
                    act.wait_ge(S("yx_ready"), TT * g)
                for t in range(TT):
                    bank, read = bank_of("xg", g, t)
                    A(at(XT + t * 512, [(1, 512)]), bank, ACT.Copy).then_inc(read, 1)
                act.drain().then_inc(S("xt_ready"), 1)
                for part in range(2):
                    bank, read = bank_of("bg", g, part)
                    w = (512, P)[part]
                    A(at(BTOK + part * 512, [(1, w)]), bank[:, 0:w], ACT.Copy).then_inc(read, 1)
                act.drain().then_inc(S("btok_ready"), 1)
                for d in range(2):
                    bank, read = bank_of("in", g, d)
                    A(at(HP + (0, 7)[d] * 512, [(1, 512)]), bank, ACT.Copy).then_inc(read, 1)
                act.drain().then_inc(S("init_ready"), 1)
                decays(g, 0)
                for d in range(2):
                    bank, read = bank_of("st", g, d)
                    if g:
                        act.wait_ge(S("ssd_state_out"), 32 * g)
                    A(at(FOUT + d * 512, [(1, 512)]), bank, ACT.Copy).then_inc(read, 1)
                act.drain().then_inc(S("fout_ready"), 1)
                for t in range(TT):
                    if t + 1 < TT:
                        decays(g, t + 1)
                    if g < 3:
                        center(6 * (g + 1) + t)
                        silu(6 * (g + 1) + t)
                if g < 3:
                    center(6 * (g + 1) + 5)
                    silu(6 * (g + 1) + 5)
            barrier(act, 8)

            def z_copies(c):
                for m in range(2):
                    bank, read = bank_of("zz", c, m)
                    A(at(ZT + (2 * c + m) * NT, [(1, 512)]), bank, ACT.Identity, scale=vcol(2, 96 + 2 * c + m)).then_inc(read, 1)
                bank, read = bank_of("zz", c, 2)
                for m in range(2):
                    i = A(at(ZT + (2 * c + m) * NT + 512, [(1, P)]), bank[:, m * P:(m + 1) * P], ACT.Identity, scale=vcol(2, 96 + 2 * c + m))
                i.then_inc(read, 1)
                act.drain().then_inc(S("zt_ready"), 1)

            def z_squares(c):
                for t in range(TT):
                    act.wait_ge(S("yz_ready"), TT * c + t + 1)
                    link(A(at(SQZ, [(1, 256)]), at(Y + t * DI + c * 256, [(1, 256)]), ACT.Square, accum_out=at(SUMS + t * 8 + c, [(1, 1)])))
            gate_copies(1)
            for c in range(8):
                for t in range(TT):
                    n = TT * c + t
                    bank, read = bank_of("z", c, t)
                    if n >= 4:
                        act.wait_ge(S("yz_ready"), n - 3)
                    A(at(SZ + (n % 4) * 256, [(1, 256)]), bank[:, 0:256], ACT.Silu).then_inc(read, 1)
                    act.drain().then_inc(S("sz_ready"), 1)
                if c:
                    z_squares(c - 1)
                    z_copies(c - 1)
            z_squares(7)
            act.drain().then_inc(S("sums_ready"), 1)
            z_copies(7)
            act.wait_ge(S("sums_added"), 1)
            A(at(STAT + 24, [(1, TT)]), at(STAT + 24, [(1, TT)]), ACT.Sqrt, bias=at(EPSB, [(1, 1)]), scale=1.0 / DI).then_inc(S("zrms_ready"), 1)
            for t in range(TT):
                act.wait_ge(S("res_ready"), TT + t + 1)
                link(A(at(SQ9, [(1, D)]), at(XRES9 + t * D, [(1, D)]), ACT.Square, accum_out=at(STAT + t, [(1, 1)])))
                A(at(STAT + 8 + t, [(1, 1)]), at(STAT + t, [(1, 1)]), ACT.Sqrt, bias=at(EPSB, [(1, 1)]), scale=1.0 / D).then_inc(S("rms_ready"), 1)

        @block.vector
        def _(dve):
            V = nc.vector
            chain = [0]

            def link(ins):
                chain[0] += 1
                ins.then_inc(S("dve_chain"), 1)
                dve.wait_ge(S("dve_chain"), chain[0])

            def settle():
                link(dve.drain())

            def bank_of(*name):
                t = turn_of[name]
                dve.wait_ge(S("bank_filled"), t + 1)
                return MP[:, t % 4, :], S(f"bank_read{t % 4}")

            def tile_of(name, o):
                g = gemm_of[name, o]
                dve.wait_ge(S("gemm_filled"), g + 1)
                return GP[:, g % 2, 0:NT], S(f"gemm_read{g % 2}")

            def mul(o, x, y):
                return V.tensor_tensor(o, x, y, ALU.mult)

            def add(o, x, y):
                return V.tensor_tensor(o, x, y, ALU.add)

            def sub(o, x, y):
                return V.tensor_tensor(o, x, y, ALU.subtract)

            V.memset(at(EPSB, [(1, 2)]), EPS).then_inc(S("eps_ready"), 1)
            dve.wait_ge(S("s5_loaded"), 16 * 5)
            V.tensor_copy(at(SV5 + 4 * P, [(SP, 2), (1, SP)], 0, 64),
                          at(TMP5, [(1, 2)], 0, 64).unsqueeze(2).broadcast_to([64, 2, SP])).then_inc(S("s5rows"), 1)

            def f5(i, n=1):
                return at(TMP5 + 64 * i, [(1, 64 * n)])

            def sv(i):
                return at(SVC + 64 * i, [(1, 64)])
            dve.wait_ge(S("svc_ready"), 1)
            dve.wait_ge(S("s5rows"), 1)
            mul(f5(0), sv(0), sv(4))
            link(mul(f5(2), sv(1), sv(4)))

            def reduce_angle(x, k, n=64):
                link(V.tensor_scalar(k, x, 1.0 / TWO_PI, MAGIC, ALU.mult, ALU.add))
                link(V.tensor_scalar(k, k, MAGIC, None, ALU.subtract))
                for cst in (C1, C2, C3):
                    link(V.scalar_tensor_tensor(out=x, in0=k, scalar=-cst, in1=x, op0=ALU.mult, op1=ALU.add))
                link(V.tensor_scalar(x, x, 3.1415925, -3.1415925, ALU.min, ALU.max))
            reduce_angle(f5(2), f5(7))
            V.tensor_copy(f5(5), f5(2))
            link(V.scalar_tensor_tensor(out=f5(6), in0=f5(2), scalar=-1.0, in1=f5(2), op0=ALU.mult, op1=ALU.max))
            V.tensor_scalar(f5(6), f5(6), -1.0, math.pi / 2, ALU.mult, ALU.add).then_inc(S("s5_arg"), 1)

            def mod_finish(layer):
                bank, read = bank_of("mod", layer)
                mv = MV + layer * 48
                V.tensor_tensor(at(mv, [(2, 24), (1, 2)]), bank[:, 0:48].rearrange("p (m w) -> p m w", w=2),
                                at(VC + 32 + 24 * layer, [(1, 24)]).unsqueeze(2).broadcast_to([P, 24, 2]), ALU.add).then_inc(read, 1)
                settle()
                link(V.tensor_scalar(at(AB, [(1, 16)]), at(mv + 16, [(1, 16)]), 1.0, None, ALU.add))
                mul(at(AB, [(2, 8), (1, 2)]), at(AB, [(2, 8), (1, 2)]),
                    at(VC + 16 + 8 * layer, [(1, 8)]).unsqueeze(2).broadcast_to([P, 8, 2])).then_inc(S("mod_ready"), 1)

            def normed(layer, t, xbuf):
                dve.wait_ge(S("rms_ready"), layer * TT + t + 1)
                link(V.reciprocal(at(STAT + 16 + t, [(1, 1)]), at(STAT + 8 + t, [(1, 1)])))
                if t >= 2:
                    dve.wait_ge(S("bank_filled"), turn_of["xt", layer, t - 2, 1] + 1)
                V.tensor_scalar(at((XN7 if layer else XN) + (t % 2) * D, [(1, D)]), at(xbuf + t * D, [(1, D)]), at(STAT + 16 + t, [(1, 1)]),
                                None, ALU.mult).then_inc(S("xn_ready"), 1)

            dve.wait_ge(S("s5_fun"), 1)
            lr, li = at(PW + 64, [(1, 64)]), at(PW + 9 * 64 + 64, [(1, 64)])
            mul(lr, f5(1), f5(4))
            mul(li, f5(1), f5(3))
            V.memset(at(PW, [(1, 64)]), 1.0)
            link(V.memset(at(PW + 9 * 64, [(1, 64)]), 0.0))
            link(V.tensor_scalar(f5(7), lr, -1.0, None, ALU.add))
            mul(f5(8), f5(7), sv(0))
            mul(f5(9), li, sv(1))
            mul(f5(10), li, sv(0))
            mul(f5(11), f5(7), sv(1))
            mul(f5(12), sv(0), sv(0))
            link(mul(f5(13), sv(1), sv(1)))
            add(f5(8), f5(8), f5(9))
            sub(f5(10), f5(10), f5(11))
            link(add(f5(12), f5(12), f5(13)))
            link(V.reciprocal(f5(12), f5(12)))
            mul(f5(8), f5(8), f5(12))
            link(mul(f5(9), f5(10), f5(12)))

            def power(dst, src, n, e):
                def pw(c, k, m):
                    return at(PW + c * 576 + k * 64, [(64, m), (1, 64)])

                def pe_(c):
                    return at(PW + c * 576 + e * 64, [(0, n), (1, 64)])
                t = [at(TMPB + 256 * j, [(64, n), (1, 64)]) for j in range(4)]
                mul(t[0], pw(0, src, n), pe_(0))
                mul(t[1], pw(1, src, n), pe_(1))
                mul(t[2], pw(0, src, n), pe_(1))
                link(mul(t[3], pw(1, src, n), pe_(0)))
                sub(pw(0, dst, n), t[0], t[1])
                link(add(pw(1, dst, n), t[2], t[3]))
            power(2, 1, 1, 1)
            power(3, 1, 2, 2)
            power(5, 1, 4, 4)
            for c in range(2):
                V.tensor_copy(at(PC + c * 576, [(9, 32), (1, 9)]), at(PW + c * 576, [(1, 32), (64, 9)]))
                V.tensor_copy(at(PC + c * 576 + 288, [(9, 32), (1, 9)]), at(PW + c * 576 + 8 * 64 + 32, [(1, 32), (-64, 9)]))
            for d in range(2):
                for c in range(2):
                    V.tensor_copy(at(SCA + d * 64 + c * 32, [(1, 32)]), at(PW + 8 * 64 + d * 32, [(1, 32)]))
                    V.tensor_scalar(at(SCA + 128 + d * 64 + c * 32, [(1, 32)]), at(PW + 576 + 8 * 64 + d * 32, [(1, 32)]),
                                    1.0 if c else -1.0, None, ALU.mult)
            dve.wait_ge(S("b_loaded"), 32)

            def hb(x):
                return x.unsqueeze(2).broadcast_to([P, 64, GS])

            def braw(c):
                return at(BRAW + c * 1024, [(16, 64), (1, 16)])

            def bbar(c):
                return at(BBAR + c * 1024, [(16, 64), (1, 16)])
            t0, t1 = (at(TMPB + 1024 * j, [(16, 64), (1, 16)]) for j in range(2))
            mul(t0, braw(0), hb(f5(8)))
            link(mul(t1, braw(1), hb(f5(9))))
            link(sub(bbar(0), t0, t1))
            mul(t0, braw(0), hb(f5(9)))
            link(mul(t1, braw(1), hb(f5(8))))
            link(add(bbar(1), t0, t1))
            for t in range(2):
                normed(0, t, X1)
            mod_finish(0)
            for t in range(2, TT):
                normed(0, t, X1)
            barrier(dve, 1)

            def input_matrices(o):
                if o >= 2:
                    dve.wait_ge(S("bank_filled"), turn_of["bt", o - 2, 3] + 1)
                for d in range(2):
                    def pc(c):
                        return at(PC + c * 576 + d * 288 + 4 * o * 9 + d, [(9, 4), (1, 8), (0, GS)])

                    def bb_(c):
                        return at(BBAR + c * 1024 + (d * 32 + 4 * o) * GS, [(GS, 4), (0, 8), (1, GS)])

                    def big(c):
                        return at(BB + (o % 2) * 2048 + (2 * d + c) * 512, [(128, 4), (16, 8), (1, 16)])
                    t0, t1 = (at(TB + 512 * j, [(128, 4), (16, 8), (1, 16)]) for j in range(2))
                    mul(t0, pc(0), bb_(0))
                    link(mul(t1, pc(1), bb_(1)))
                    link(sub(big(0), t0, t1))
                    mul(t0, pc(0), bb_(1))
                    link(mul(t1, pc(1), bb_(0)))
                    i = add(big(1), t0, t1)
                    if d:
                        i.then_inc(S("bb_ready"), 1)
                        dve.wait_ge(S("bb_ready"), o + 1)
                    else:
                        link(i)

            def chunk_copies(o):
                for half in range(2):
                    bank, read = bank_of("ma", o, half)
                    if o >= 2:
                        dve.wait_ge(S("bank_filled"), turn_of["ub", o - 2, 1] + 1)
                    V.tensor_copy(at(MT + (o % 2) * 1024 + (7 - 4 * half) * 16, [(-16, 4), (P, 8), (1, 16)], 0, 80),
                                  bank[0:80, :].rearrange("p (t g h) -> p t g h", t=4, h=16)).then_inc(read, 1)
                    dve.drain().then_inc(S("mt_ready"), 1)

            def backward_inputs(o):
                for c in range(2):
                    bank, read = bank_of("s", o, 2 + c)
                    V.tensor_copy(at(HS + (XC) * SLOTW + 64 + c * NPAIR + 4 * o, [(1, 4), (-SLOTW, XC)]),
                                  bank[:, 0:4 * XC].rearrange("p (q x) -> p q x", q=4)).then_inc(read, 1)

            input_matrices(0)
            for o in range(OCT):
                if o + 1 < OCT:
                    input_matrices(o + 1)
                chunk_copies(o)
                backward_inputs(o)
            dve.wait_ge(S("hs_forward"), 1)
            settle()
            for d, slot in ((0, 0), (1, CTXX + 1)):
                for c in range(2):
                    V.tensor_copy(at(HS + slot * SLOTW + d * 64 + c * 32, [(1, 32)]), at(SVC + 64 * (2 + c) + d * 32, [(1, 32)]))
            V.memset(at(HS + 64, [(1, 64)]), 0.0)
            dve.drain().then_inc(S("scan_start"), 1)
            dstep = (CTXX + 1) * SLOTW + 64
            with dve.Fori(0, LATX - 1) as s:
                h = at(HS + s * SLOTW, [(dstep, 2), (1, 64)])
                hc = at(HS + s * SLOTW, [(dstep, 2), (32, 2), (1, 32)])
                hn = at(HS + SLOTW + s * SLOTW, [(dstep, 2), (1, 64)])
                m1, m2 = at(SCT, [(64, 2), (1, 64)]), at(SCT + 128, [(64, 2), (1, 64)])
                mul(m1, h, at(SCA, [(64, 2), (1, 64)])).then_inc(S("scan_lat"), 1)
                mul(at(SCT + 160, [(64, 2), (-32, 2), (1, 32)]), hc, at(SCA + 160, [(64, 2), (-32, 2), (1, 32)])).then_inc(S("scan_lat"), 1)
                dve.wait_ge(S("scan_lat"), s * 4 + 2)
                add(m1, m1, m2).then_inc(S("scan_lat"), 1)
                dve.wait_ge(S("scan_lat"), s * 4 + 3)
                add(hn, hn, m1).then_inc(S("scan_lat"), 1)
                dve.wait_ge(S("scan_lat"), s * 4 + 4)
            barrier(dve, 2)

            for c in range(2):
                V.tensor_copy(at(FS + c * 64, [(1, 32)]), at(HS + (SLOTS - 1) * SLOTW + c * 32, [(1, 32)]))
                V.tensor_copy(at(FS + c * 64 + 32, [(1, 32)]), at(HS + CTXX * SLOTW + 64 + c * 32, [(1, 32)]))
            dve.drain().then_inc(S("fs_ready"), 1)
            link(V.memset(at(BBD, [(1, 512)]), 0.0))
            def conv_sides(name, o, part, n):
                dve.wait_ge(S("cv_center"), n + 1)
                tile, read = tile_of(name, o)
                cv = CV + (n % 2) * NT
                for base, m in ((0, NLAT), (NLAT, NCTX)):
                    V.scalar_tensor_tensor(out=at(cv + base + 1, [(1, m - 1)]), in0=tile[:, base:base + m - 1],
                                           scalar=vcol(1, 40 + 8 * part + o), in1=at(cv + base + 1, [(1, m - 1)]),
                                           op0=ALU.mult, op1=ALU.add)
                settle()
                for base, m in ((0, NLAT), (NLAT, NCTX)):
                    i = V.scalar_tensor_tensor(out=at(cv + base, [(1, m - 1)]), in0=tile[:, base + 1:base + m],
                                               scalar=vcol(1, 40 + 48 + 8 * part + o), in1=at(cv + base, [(1, m - 1)]),
                                               op0=ALU.mult, op1=ALU.add)
                i.then_inc(read, 1)
                settle()
                return cv

            def output_matrices(o):
                dve.wait_ge(S("ct_ready"), o + 1)
                if o >= 2:
                    dve.wait_ge(S("bank_filled"), turn_of["y", o - 2, 1] + 1)
                for d in range(2):
                    def pc(c):
                        return at(PC + c * 576 + d * 288 + 4 * o * 9, [(9, 4), (1, 9), (0, GS)])

                    def ct(kind):
                        return at(CT + kind * 128 + d * 64, [(GS, 4), (0, 9), (1, GS)])

                    def big(c):
                        return at(CE + (o % 2) * 2304 + (2 * d + c) * 576, [(144, 4), (16, 9), (1, 16)])
                    other = at(TC, [(144, 4), (16, 9), (1, 16)])
                    for c in range(2):
                        mul(big(c), pc(0), ct(c))
                        link(mul(other, pc(1), ct(1 + c)))
                        link(add(big(c), big(c), other))
                for e in range(2):
                    V.tensor_copy(at(BBD + 16 * e, [(256, 2), (128, 2), (32, 4), (1, GS)], 64 * e, 64)[:, 0],
                                  at(BBAR + 4 * o * GS, [(512, 2), (1024, 2), (GS, 4), (1, GS)], 64 * e, 64)[:, 0])
                    V.tensor_copy(at(BBD + 16 * e, [(256, 2), (128, 2), (32, 4), (1, GS)], 64 * e, 64)[:, 1],
                                  at(BBAR + 4 * o * GS, [(512, 2), (1024, 2), (GS, 4), (1, GS)], 64 * e, 64)[:, 1])
                dve.drain().then_inc(S("ce_ready"), 1)

            def lag_strip(o):
                bank, read = bank_of("k", o)
                ws = WS + (o % 2) * 240
                if o >= 2:
                    dve.wait_ge(S(f"strip_out{o % 2}"), 16 * (o // 2))
                V.tensor_copy(at(ws + 112, [(1, P)]), bank[:, 0:P])
                V.tensor_copy(at(ws, [(1, 112)]), bank[:, P:P + 112])
                settle()
                add(at(ws + 112, [(1, 16)]), at(ws + 112, [(1, 16)]), bank[:, P + 112:2 * P]).then_inc(read, 1)
                settle()
                V.scalar_tensor_tensor(out=at(ws + 112, [(1, 16)]), in0=at(TAB + T_M16 - T_TN, [(1, 16)]), scalar=vcol(1, 8 + o),
                                       in1=at(ws + 112, [(1, 16)]), op0=ALU.mult, op1=ALU.add).then_inc(S("ws_ready"), 1)

            dve.wait_ge(S("tab_loaded"), 16)
            output_matrices(0)
            for o in range(OCT + 1):
                if o < OCT:
                    lag_strip(o)
                    cv = conv_sides("x2", o, 2, o)
                    mul(at(GB + o * NT, [(1, NT)]), at(GB + o * NT, [(1, NT)]), at(cv, [(1, NT)])).then_inc(S("cv_free"), 1)
                if o + 1 < OCT:
                    output_matrices(o + 1)
                if o >= 1:
                    for half in range(2):
                        bank, read = bank_of("yt", o - 1, half)
                        if o >= 2 and half == 0:
                            dve.wait_ge(S("bank_filled"), turn_of["yc", o - 2, 1] + 1)
                        V.tensor_copy(at(MT2 + half * 16, [(32, 4), (P, 8), (1, 16)], 0, XC),
                                      bank[0:XC, :].rearrange("p (g t h) -> p g t h", g=4, h=16)).then_inc(read, 1)
                        dve.drain().then_inc(S("mt2_ready"), 1)
            barrier(dve, 3)

            for o in range(OCT):
                m = o % 2
                dve.wait_ge(S("glu_ready"), o + 1)
                z = at(ZA + o * NT, [(1, NT)])
                mul(z, at(YT + o * YW, [(1, NT)]), at(TA + m * NT, [(1, NT)]))
                settle()
                mul(z, z, at(TG + m * NT, [(1, NT)])).then_inc(S("za_done"), 1)
            barrier(dve, 4)

            n = 8
            for name, part in (("v", 0), ("x1", 1)):
                for o in range(OCT):
                    cv = conv_sides(name, o, part, n)
                    if n >= 10:
                        prev = (name, o - 2) if o >= 2 else ("v", o + 6)
                        dve.wait_ge(S("bank_filled"), turn_of[prev[0] + "t", prev[1], 1] + 1)
                    pq = PQ + (o % 2) * NT
                    first, mirrored = at(cv, [(1, 256)]), at(cv + NLAT - 1, [(-1, 256)])
                    if name == "v":
                        add(at(pq, [(1, 256)]), first, mirrored)
                        sub(at(pq + 256, [(1, 256)]), first, mirrored)
                    else:
                        V.tensor_copy(at(pq, [(1, 256)]), first)
                        V.tensor_copy(at(pq + 256, [(1, 256)]), mirrored)
                    V.tensor_copy(at(pq + NLAT, [(1, NCTX)]), at(cv + NLAT, [(1, NCTX)])).then_inc(S("cv_free"), 1)
                    dve.drain().then_inc(S(name + "_conv"), 1)
                    n += 1
            barrier(dve, 5)

            def mlp_args(n, rows):
                for half, (c0, cn) in enumerate(((0, 512), (512, P))):
                    bank, read = bank_of("mlp", n, half)
                    V.tensor_scalar(at(FA + c0, [(1, cn)], 0, rows), bank[0:rows, 0:cn], at(FCOL + 2 * (n - 1), [(1, 1)], 0, rows),
                                    at(FCOL + 2 * (n - 1) + 1, [(1, 1)], 0, rows), ALU.add, ALU.mult).then_inc(read, 1)
                settle()
                reduce_angle(at(FA, [(1, NT)], 0, rows), at(FK, [(1, NT)], 0, rows))
                dve.drain().then_inc(S("sin_arg"), 1)
            dve.wait_ge(S("fcol_loaded"), 16 * 6)
            mlp_args(1, 64)
            dve.wait_ge(S("sin_done"), 1)
            dve.drain().then_inc(S("mlp_ready"), 1)
            mlp_args(2, P)
            dve.wait_ge(S("sin_done"), 2)
            V.tensor_copy(at(FO2, [(1, NT)], 0, 64), at(FE, [(1, NT)], 0, 64))
            link(V.tensor_scalar(at(FO2, [(1, NT)], 64, 64), at(FE, [(1, NT)], 64, 64), -1.0, None, ALU.mult))
            V.memset(at(FE, [(NLAT, 2)], 64, 64), 0.0)
            dve.drain().then_inc(S("mlp_ready"), 1)

            def window_taps(i):
                if i % 2 == 0:
                    dve.wait_ge(S("win_ready"), i // 2 + 1)
                if i:
                    dve.wait_ge(S("bank_filled"), turn_of["khc", i - 1] + 1)
                for n in range(5):
                    bank, read = bank_of("f", i, n)
                    mul(at(TAPS + n * HW, [(5 * HW, 2), (1, HW)]), bank.rearrange("p (a b) -> p a b", a=2),
                        at(WIN + n * HW, [(0, 2), (1, HW)])).then_inc(read, 1)
                dve.drain().then_inc(S("taps_ready"), 1)

            def kh_combine(i):
                for kind in range(2):
                    for ft in range(2):
                        bank, read = bank_of("kh", i, kind, ft)
                        n = 4 * i + 2 * kind + ft
                        dve.wait_ge(S("kh_odd"), n + 1)
                        odd = at(HTMP, [(1, HW)])
                        add(at(KH + (kind * 5 + ft) * HW, [(1, HW)]), bank[:, 0:HW], odd)
                        sub(at(KH + (kind * 5 + ft + 2) * HW, [(1, HW)]), bank[:, 0:HW], odd).then_inc(read, 1)
                        dve.drain().then_inc(S("kh_done"), 1)

            def products(i):
                dve.wait_ge(S("fq_ready"), i + 1)
                dve.wait_ge(S("khc_ready"), i + 1)
                if i:
                    dve.wait_ge(S("bank_filled"), turn_of["yi", i - 1, 2] + 1)
                n, part = 5 * HW, 640
                for c0 in (0, part):
                    p, q, kr, ki = (at(b + c0, [(1, part)]) for b in (FQ, FQ + n, KH, KH + n))
                    p1, q1, t = at(PR + c0, [(1, part)]), at(PR + n + c0, [(1, part)]), at(PT, [(1, part)])
                    mul(p1, kr, p)
                    link(mul(t, ki, q))
                    link(add(p1, p1, t))
                    mul(q1, kr, q)
                    link(mul(t, ki, p))
                    link(sub(q1, q1, t))
                dve.drain().then_inc(S("pr_ready"), 1)

            def outputs(i):
                w, r = i // 2, i % 2
                for tt in range(2):
                    bank, read = bank_of("yi", i, tt)
                    n = 2 * i + tt
                    dve.wait_ge(S("yi_odd"), n + 1)
                    odd = at(MTMP, [(1, HW)])
                    va, vb = (at(VS + (2 * h + tt) * H1 + w * HW, [(1, HW)]) for h in range(2))
                    if r:
                        add(va, bank[:, 0:HW], odd)
                        sub(vb, bank[:, 0:HW], odd).then_inc(read, 1)
                    else:
                        ta, tb = at(YT2, [(1, HW)]), at(YT2 + HW, [(1, HW)])
                        add(ta, bank[:, 0:HW], odd)
                        sub(tb, bank[:, 0:HW], odd).then_inc(read, 1)
                        settle()
                        mul(ta, ta, at(XS + tt * H1 + w * HW, [(1, HW)]))
                        mul(tb, tb, at(XS + (2 + tt) * H1 + w * HW, [(1, HW)]))
                        settle()
                        add(va, ta, tb)
                        sub(vb, ta, tb)
                    dve.drain().then_inc(S("yi_done"), 1)
                bank, read = bank_of("yi", i, 2)
                vc = at(VS + 4 * H1 + w * HW, [(1, HW)])
                if r:
                    V.tensor_copy(vc, bank[:, 0:HW]).then_inc(read, 1)
                else:
                    mul(vc, bank[:, 0:HW], at(XS + 4 * H1 + w * HW, [(1, HW)])).then_inc(read, 1)
                dve.drain().then_inc(S("yh_ready" if r else "z_ready"), 1)

            def gated(w):
                for m in range(2):
                    gb = GB + (2 * w + m) * NT
                    bank, read = bank_of("zt", w, m, 0)
                    mul(at(gb, [(1, 256)]), at(gb, [(1, 256)]), bank[:, 0:256])
                    back = at(gb + NLAT - 1, [(-1, 256)])
                    mul(back, back, bank[:, 256:512]).then_inc(read, 1)
                    bank, read = bank_of("zt", w, m, 1)
                    mul(at(gb + NLAT, [(1, P)]), at(gb + NLAT, [(1, P)]), bank[:, 0:P]).then_inc(read, 1)

            def mod_part(b):
                bank, read = bank_of("mod1", b)
                V.tensor_tensor(at(MV + 48 + 12 * b, [(2, 6), (1, 2)]), bank[:, 0:12].rearrange("p (m w) -> p m w", w=2),
                                at(VC + 56 + 6 * b, [(1, 6)]).unsqueeze(2).broadcast_to([P, 6, 2]), ALU.add).then_inc(read, 1)

            window_taps(0)
            kh_combine(0)
            for i in range(2 * NW):
                products(i)
                if i + 1 < 2 * NW:
                    window_taps(i + 1)
                outputs(i)
                if i + 1 < 2 * NW:
                    kh_combine(i + 1)
                if i % 2:
                    mod_part(i // 2)
                    gated(i // 2)
            barrier(dve, 6)

            def gates(layer):
                for w in range(2):
                    for k in range(8):
                        V.tensor_scalar(at((DG9 if layer else DG) + w * D + k * P, [(1, P)]), at(IDENT, [(1, P)]),
                                        at(MV + layer * 48 + 32 + 2 * k + w, [(1, 1)]), None, ALU.mult)
                dve.drain().then_inc(S("dg_ready"), 1)

            def scale_terms(layer):
                link(V.tensor_scalar(at(AB, [(1, 16)]), at(MV + layer * 48 + 16, [(1, 16)]), 1.0, None, ALU.add))
                mul(at(AB, [(2, 8), (1, 2)]), at(AB, [(2, 8), (1, 2)]),
                    at(VC + 16 + 8 * layer, [(1, 8)]).unsqueeze(2).broadcast_to([P, 8, 2])).then_inc(S("mod_ready"), 1)

            def residual(layer):
                for half in range(2):
                    if half == 0:
                        dve.wait_ge(S("gr_ready"), layer + 1)
                    acc4 = bank_of("acc4", layer, half)
                    for t in (0, 1, 2, 3, 4):
                        w = 0 if t < 4 else 1
                        acc, read = acc4
                        if t < 4:
                            acc, read = GP[:, t // 2, (t % 2) * 512:(t % 2) * 512 + 512], S("acc_read")
                        tmp = at((RT9 if layer else RT) + (t % 2) * 512, [(1, 512)])
                        x = at((XRES9 if layer else XRES) + t * D + half * 512, [(1, 512)])
                        gate = at((GR9 if layer else GR) + w * D + half * 512, [(1, 512)])
                        if layer:
                            V.scalar_tensor_tensor(out=tmp, in0=acc, scalar=at(STAT + 32 + t, [(1, 1)]), in1=gate,
                                                   op0=ALU.mult, op1=ALU.mult).then_inc(read, 1)
                        else:
                            mul(tmp, acc, gate).then_inc(read, 1)
                        settle()
                        add(x, x, tmp)
                        if half:
                            dve.drain().then_inc(S("res_ready"), 1)
                        settle()
            gates(0)
            scale_terms(1)
            dve.wait_ge(S("xres_loaded"), 80)
            residual(0)
            for t in range(TT):
                normed(1, t, XRES)
            barrier(dve, 7)

            tri = (TAB + T_UP - T_TN, TAB + T_LO - T_TN)
            sub(at(SGT, [(1, P)]), at(tri[1], [(1, P)]), at(IDENT, [(1, P)]))
            sub(at(SLT, [(1, P)]), at(tri[0], [(1, P)]), at(IDENT, [(1, P)]))
            x, y, z = (at(SPT + i * CW, [(1, CW)]) for i in range(3))
            dt, ad = at(DTB, [(1, CW)]), at(AD, [(1, CW)])
            dve.wait_ge(S("ssd_rows"), 48)
            bank, read = bank_of("dt")
            V.tensor_tensor(at(SPT, [(SH, TT), (TT * SH, 2), (1, SH)]), bank[:, 0:CW].rearrange("p (t d h) -> p t d h", t=TT, d=2),
                            at(BROW, [(0, TT), (SH, 2), (1, SH)]), ALU.add).then_inc(read, 1)
            settle()
            link(V.scalar_tensor_tensor(out=y, in0=x, scalar=-1.0, in1=x, op0=ALU.mult, op1=ALU.min))
            V.tensor_scalar(x, x, 0.0, None, ALU.max)
            dve.drain().then_inc(S("sp_arg"), 1)
            dve.wait_ge(S("sp_exp"), 1)
            link(V.tensor_scalar(z, y, 2.0, None, ALU.add))
            link(V.reciprocal(z, z))
            link(mul(y, y, z))
            link(mul(z, y, y))
            link(V.tensor_scalar(dt, z, 1.0 / 17, 1.0 / 15, ALU.mult, ALU.add))
            for k in (13, 11, 9, 7, 5, 3, 1):
                link(mul(dt, dt, z))
                link(V.tensor_scalar(dt, dt, 1.0 / k, None, ALU.add))
            link(mul(dt, dt, y))
            link(V.scalar_tensor_tensor(out=dt, in0=dt, scalar=2.0, in1=x, op0=ALU.mult, op1=ALU.add))
            dve.wait_ge(S("arow_ready"), 1)
            for d in range(2):
                V.scalar_tensor_tensor(out=at(AD + d * TT * SH, [(SH, TT), (1, SH)]), in0=at(DTB + d * TT * SH, [(SH, TT), (1, SH)]),
                                       scalar=-1.0, in1=at(AROW + d * SH, [(0, TT), (1, SH)]), op0=ALU.mult, op1=ALU.mult)
            dve.drain().then_inc(S("ad_ready"), 1)
            dve.wait_ge(S("coef_exp"), 1)
            link(mul(at(WW, [(1, CW)]), at(WW, [(1, CW)]), dt))

            def ssd_sides(n):
                g, j = n // 6, n % 6
                o, dst = (16 + 4 * j + g, BC + (g % 2) * 2 * NT + j * NT) if j < 2 else (4 * g + j - 2, XCH + (j - 2) * NT)
                dve.wait_ge(S("cv_center8"), n + 1)
                tile, read = tile_of("ssd_g", n)
                for base, m in ((0, NLAT), (NLAT, NCTX)):
                    V.scalar_tensor_tensor(out=at(dst + base + 1, [(1, m - 1)]), in0=tile[:, base:base + m - 1],
                                           scalar=vcol(2, 24 + o), in1=at(dst + base + 1, [(1, m - 1)]), op0=ALU.mult, op1=ALU.add)
                settle()
                for base, m in ((0, NLAT), (NLAT, NCTX)):
                    i = V.scalar_tensor_tensor(out=at(dst + base, [(1, m - 1)]), in0=tile[:, base + 1:base + m],
                                               scalar=vcol(2, 24 + 48 + o), in1=at(dst + base, [(1, m - 1)]), op0=ALU.mult, op1=ALU.add)
                i.then_inc(read, 1)
                dve.drain().then_inc(S("cv_sides"), 1)

            def heads(base, n=64):
                return at(base, [(n, 8), (1, n)])

            def state_input(g, k):
                d, t = STATES[k]
                if k >= 2:
                    dve.wait_ge(S("bank_filled"), turn_of["st", g, k - 2] + 1)
                mul(heads(XW + (k % 2) * 512), heads(XT + t * 512), coef(WW, d, t, g, 64)).then_inc(S("xw_ready"), 1)

            def state_step(g, k):
                d, t = STATES[k]
                bank, read = bank_of("st", g, k)
                if k == 2:
                    dve.wait_ge(S("init_ready"), g + 1)
                src = HP + (4 * d + t) * 512
                dst = src + (512, -512)[d]
                link(mul(heads(dst), heads(src), coef(TOT, d, t, g, 64)))
                add(at(dst, [(1, 512)]), at(dst, [(1, 512)]), bank).then_inc(read, 1)
                settle()

            for n in range(6):
                ssd_sides(n)
            for g in range(SG):
                settle()
                dve.wait_ge(S("xt_ready"), g + 1)
                for part in range(2):
                    bank, read = bank_of("cb", g, part)
                    m = (4, 1)[part]
                    for d in range(2):
                        i = mul(at(CBM + d * TT * P + part * 512, [(P, m), (1, P)]), bank[:, 0:m * P].rearrange("p (a b) -> p a b", a=m),
                                at(tri[d], [(0, m), (1, P)]))
                    i.then_inc(read, 1)
                for k in range(8):
                    state_input(g, k)
                    if k > 2:
                        state_step(g, k - 1)
                state_step(g, 7)
                settle()
                dve.sem_inc(S("hp_ready"), 1)
                for t in range(TT):
                    n = TT * g + t
                    dve.wait_ge(S("ex_ready"), n + 1)
                    if n:
                        dve.wait_ge(S("bank_filled"), (turn_of["yd", g, t - 1] if t else turn_of["yd", g - 1, 4]) + 1)
                    for d in range(2):
                        mul(heads(MM + d * 1024, P), heads(EX, P), at(CBM + (TT * d + t) * P, [(0, 8), (1, P)]))
                        mul(heads(XD + d * 512), heads(XT + t * 512), coef(DTB, d, t, g, 64))
                    dve.drain().then_inc(S("mm_ready"), 1)
                    if g < 3:
                        ssd_sides(6 * (g + 1) + t)
                    tf, tb = YTMP, YTMP + 512
                    dve.wait_ge(S("yx_ready"), n + 1)
                    out = at(Y + t * DI + g * 512, [(1, 512)])
                    if t < 4:
                        for d in range(2):
                            bank, read = bank_of("yo", g, t, d)
                            mul(heads((tf, tb)[d]), bank.rearrange("p (h c) -> p h c", h=8), coef(EE, d, t, g, 64)).then_inc(read, 1)
                        settle()
                        add(at(tf, [(1, 512)]), at(tf, [(1, 512)]), at(tb, [(1, 512)]))
                        settle()
                        add(out, out, at(tf, [(1, 512)]))
                        settle()
                    bank, read = bank_of("yd", g, t)
                    add(out, out, bank).then_inc(read, 1)
                    settle()
                if g < 3:
                    ssd_sides(6 * (g + 1) + 5)
            barrier(dve, 8)

            gates(1)
            for c in range(8):
                for t in range(TT):
                    n = TT * c + t
                    dve.wait_ge(S("sz_ready"), n + 1)
                    y = at(Y + t * DI + c * 256, [(1, 256)])
                    mul(y, y, at(SZ + (n % 4) * 256, [(1, 256)])).then_inc(S("yz_ready"), 1)
            dve.wait_ge(S("sums_ready"), 1)
            V.tensor_reduce(at(STAT + 24, [(1, TT)]), at(SUMS, [(8, TT), (1, 8)]), mybir.AxisListType.X, ALU.add).then_inc(S("sums_added"), 1)
            dve.wait_ge(S("zrms_ready"), 1)
            link(V.reciprocal(at(STAT + 32, [(1, TT)]), at(STAT + 24, [(1, TT)])))
            dve.wait_ge(S("xres_loaded"), 160)
            residual(1)
            dve.wait_ge(S("fnw_loaded"), 16)
            for t in range(TT):
                dve.wait_ge(S("rms_ready"), 2 * TT + t + 1)
                link(V.reciprocal(at(STAT + 16 + t, [(1, 1)]), at(STAT + 8 + t, [(1, 1)])))
                x = at(XRES9 + t * D, [(1, D)])
                V.scalar_tensor_tensor(out=x, in0=x, scalar=at(STAT + 16 + t, [(1, 1)]), in1=at(FNW, [(1, D)]),
                                       op0=ALU.mult, op1=ALU.mult).then_inc(S("y_ready"), 1)

        @block.gpsimd
        def _(pool):
            G = nc.gpsimd
            G.memset(at(ONES, [(1, P)]), 1.0).then_inc(S("ident_ready"), 1)
            G.memset(at(IDENT, [(1, P)]), 0.0).then_inc(S("ident_ready"), 1)
            pool.wait_ge(S("ident_ready"), 2)
            G.affine_select(out=at(IDENT, [(1, P)]), in_=at(IDENT, [(1, P)]), compare_op=ALU.not_equal, fill=1.0, base=0,
                            pattern=[[-1, P]], channel_multiplier=1).then_inc(S("ident_ready"), 1)
            barrier(pool, 1)
            G.memset(at(U + GAP, [(XC, 64)]), 0.0).then_inc(S("u_gap"), 1)
            pool.wait_ge(S("scan_start"), 1)
            dstep = (LATX + 1) * SLOTW - 64
            h0 = HS + 64
            with pool.Fori(0, CTXX) as s:
                h = at(h0 + s * SLOTW, [(dstep, 2), (1, 64)])
                hc = at(h0 + s * SLOTW, [(dstep, 2), (32, 2), (1, 32)])
                hn = at(h0 + SLOTW + s * SLOTW, [(dstep, 2), (1, 64)])
                m1, m2 = at(SCT + 256, [(64, 2), (1, 64)]), at(SCT + 384, [(64, 2), (1, 64)])
                G.tensor_tensor(m1, h, at(SCA + 64, [(-64, 2), (1, 64)]), ALU.mult).then_inc(S("scan_ctx"), 1)
                G.tensor_tensor(at(SCT + 416, [(64, 2), (-32, 2), (1, 32)]), hc,
                                at(SCA + 224, [(-64, 2), (-32, 2), (1, 32)]), ALU.mult).then_inc(S("scan_ctx"), 1)
                pool.wait_ge(S("scan_ctx"), s * 4 + 2)
                G.tensor_tensor(m1, m1, m2, ALU.add).then_inc(S("scan_ctx"), 1)
                pool.wait_ge(S("scan_ctx"), s * 4 + 3)
                G.tensor_tensor(hn, hn, m1, ALU.add).then_inc(S("scan_ctx"), 1)
                pool.wait_ge(S("scan_ctx"), s * 4 + 4)
            barrier(pool, 2)

            for c, nm in enumerate(("s5_c_re", "s5_c_im")):
                for d in range(2):
                    pool.dma_start(at(CRAW + (2 * c + d) * OCT * SP, [(SP, OCT), (1, SP)]),
                                   a[nm][0, d].rearrange("(o g) h p -> (g h) o p", g=8)).then_inc(S("c_loaded"), 16)
            pool.wait_ge(S("fo_ready"), 1)
            for c, nm in enumerate(("new_re", "new_im")):
                pool.dma_start(outs[nm].rearrange("b a d (q e) p -> (b a d q) (e p)", e=2),
                               at(FO + c * P, [(1, P)], 0, 64)).then_inc(S("s5_state_out"), 16)
            for o in range(OCT):
                pool.wait_ge(S("ws_ready"), o + 1)
                pool.dma_start(strips[o], at(WS + (o % 2) * 240, [(1, 240)])).then_inc(S(f"strip_out{o % 2}"), 16)
                pool.wait_ge(S(f"strip_out{o % 2}"), 16 * (o // 2 + 1))
                if o >= 2:
                    pool.wait_ge(S("bank_filled"), turn_of["y", o - 2, 1] + 1)
                for t in range(Q8):
                    pool.dma_start(at(TTB + (o % 2) * 1024, [(P, 8), (1, P)], 16 * t, 16),
                                   strips[o].rearrange("(g h) c -> h g c", h=GS)[:, :, 16 * t:16 * t + P]).then_inc(S(f"t_loaded{o % 2}"), 16)
            pool.wait_ge(S("s5_state_out"), 32)
            barrier(pool, 3)
            barrier(pool, 4)
            barrier(pool, 5)

            pool.dma_start(at(EMB, [(1, NT)], 0, 33), a["emb"]).then_inc(S("mlp_loaded"), 16)
            pool.dma_start(at(W3 + HW, [(1, 64)], 0, 33), a["hy_f_w1"][0]).then_inc(S("mlp_loaded"), 16)
            for j in range(2):
                pool.dma_start(at(W3 + 64 * j, [(1, 64)], 0, 64), a["hy_f_w2"][0]).then_inc(S("mlp_loaded"), 16)
            pool.dma_start(at(CX, [(1, 640)]), a["tables"][:, T_CX:T_CX + 640]).then_inc(S("mlp_loaded"), 16)
            for j, nm in enumerate(("hy_f_b1", "hy_f_freq1")):
                pool.dma_start(at(FCOL + j, [(1, 1)], 0, 64), a[nm].rearrange("a h -> h a")).then_inc(S("fcol_loaded"), 16)
            for j, nm in enumerate(("hy_f_b2", "hy_f_freq2")):
                for copy in range(2):
                    pool.dma_start(at(FCOL + 2 + j, [(1, 1)], 64 * copy, 64), a[nm].rearrange("a h -> h a")).then_inc(S("fcol_loaded"), 16)
            pool.dma_start(at(GF, [(1, 2048)]), a["tables"][:, T_GF:T_GF + 2048]).then_inc(S("hy_tables"), 16)
            pool.dma_start(at(GI, [(1, 2048)]), a["tables"][:, T_GI:T_GI + 2048]).then_inc(S("hy_tables"), 16)
            pool.dma_start(at(CS, [(1, 2048)]), a["tables"][:, T_CS:T_CS + 2048]).then_inc(S("hy_tables"), 16)
            pool.dma_start(at(DEL, [(1, H1)]), a["deltas"].partition_broadcast(P)[:, 0] if len(a["deltas"].partition_broadcast(P).shape) == 3
                           else a["deltas"].partition_broadcast(P)).then_inc(S("hy_tables"), 16)
            for w in range(NW):
                pool.wait_ge(S("bank_filled"), (turn_of["f", 2 * w - 1, 4] if w else turn_of["mlp", 2, 1]) + 1)
                w3 = a["hy_f_w3"][0].rearrange("h (r d c) -> d h r c", r=2, d=2)
                for d in range(2):
                    pool.dma_start(at(W3, [(HW, 2), (1, HW)], 64 * d, 64), w3[d, :, :, w * HW:(w + 1) * HW]).then_inc(S("w3_loaded"), 16)
                for r_ in range(2):
                    pool.dma_start(at(FBIAS + r_ * HW, [(1, HW)], 0, 1), a["hy_bias"][0, r_:r_ + 1, w * HW:(w + 1) * HW]).then_inc(S("w3_loaded"), 16)
            barrier(pool, 6)
            for t in range(TT):
                src = a["x_sample"][0, t * P:(t + 1) * P, :] if t < 4 else a["x_prompt"][0]
                pool.dma_start(at(XRES + t * D, [(1, D)]), src).then_inc(S("xres_loaded"), 16)
            for t in range(TT):
                pool.wait_ge(S("res_ready"), t + 1)
                pool.dma_start(spill[t], at(XRES + t * D, [(1, D)])).then_inc(S("spilled"), 16)
            pool.wait_ge(S("spilled"), 16 * TT)
            barrier(pool, 7)

            for row, nm, n in ((BROW, "ssd_dt_bias", 64), (AROW, "ssd_a_log", 64), (DROW, "ssd_d", SH)):
                src = a[nm][0].rearrange("d h -> (d h)") if n == 64 else a[nm][0]
                pool.dma_start(at(row, [(1, n)]), src.partition_broadcast(P)).then_inc(S("ssd_rows"), 16)

            def load_init(g):
                for d in range(2):
                    pool.dma_start(at(INIT + d * 512, [(P, 4), (1, P)]),
                                   a["state_ssd"][0, 0, d, 8 * g:8 * g + 8].rearrange("(j e) p n -> (e p) j n", e=2)).then_inc(S("init_loaded"), 16)

            def masked(g, t):
                n = TT * g + t
                if n:
                    pool.wait_ge(S("bank_filled"), (turn_of["ar", g, t - 1, 1] if t else turn_of["ar", g - 1, 4, 1]) + 1)
                for d, mask in enumerate((TAB + T_UP - T_TN, TAB + T_LO - T_TN)):
                    G.tensor_tensor(at(AM + d * 1024, [(P, 8), (1, P)]), at(mask, [(0, 8), (1, P)]), coef(AD, d, t, g, P),
                                    ALU.mult).then_inc(S("am_ready"), 1)
            load_init(0)
            pool.wait_ge(S("ssd_rows"), 48)
            pool.wait_ge(S("ad_ready"), 1)
            masked(0, 0)
            for g in range(SG):
                pool.wait_ge(S("xt_ready"), g + 1)
                for t in range(TT):
                    G.tensor_tensor(at(Y + t * DI + g * 512, [(64, 8), (1, 64)]), at(XT + t * 512, [(64, 8), (1, 64)]),
                                    at(DROW + 8 * g, [(1, 8), (0, 64)]), ALU.mult).then_inc(S("yx_ready"), 1)
                    if t == 0 and g < 3:
                        pool.wait_ge(S("bank_filled"), turn_of["in", g, 1] + 1)
                        load_init(g + 1)
                    if t + 1 < TT:
                        masked(g, t + 1)
                pool.wait_ge(S("fout_ready"), g + 1)
                for d in range(2):
                    pool.dma_start(outs["new_ssd"][0, 0, d, 8 * g:8 * g + 8].rearrange("(j e) p n -> (e p) j n", e=2),
                                   at(FOUT + d * 512, [(P, 4), (1, P)])).then_inc(S("ssd_state_out"), 16)
                if g < 3:
                    masked(g + 1, 0)
            pool.wait_ge(S("ssd_state_out"), 32 * SG)
            barrier(pool, 8)

            for t in range(TT):
                pool.dma_start(at(XRES9 + t * D, [(1, D)]), spill[t]).then_inc(S("xres_loaded"), 16)
            pool.dma_start(at(FNW, [(1, D)]), a["final_norm_w"].partition_broadcast(P)).then_inc(S("fnw_loaded"), 16)
            for t in range(TT):
                pool.wait_ge(S("y_ready"), t + 1)
                dst = outs["y_sample"][0, t * P:(t + 1) * P, :] if t < 4 else outs["y_prompt"][0]
                pool.dma_start(dst, at(XRES9 + t * D, [(1, D)])).then_inc(S("y_out"), 16)
            pool.wait_ge(S("y_out"), 16 * TT)

        @block.sync
        def _(sp):
            for t in range(TT):
                src = a["x_sample"][0, t * P:(t + 1) * P, :] if t < 4 else a["x_prompt"][0]
                sp.dma_start(at(X1 + t * D, [(1, D)]), src).then_inc(S(f"x_loaded{t}"), 16)

            def stream(name, count, src, sub_):
                base = chunk[name]
                assert base % NSLOT == 0 and count % NSLOT == 0

                def four(it, first):
                    for j in range(4):
                        if first is None or first + j >= NSLOT:
                            sp.wait_ge(S("ring_used"), it * 4 + (base + j - NSLOT + 1))
                        sp.dma_start(at(ring(j), sub_), src(it * 4 + j)).then_inc(S(f"ring_full{j}"), 16)
                done = 0
                if base == 0:
                    four(0, 0)
                    done = 1
                if count // 4 - done > 0:
                    with sp.Fori(done, count // 4) as it:
                        four(it, None)
            sub8 = [(256, 8), (1, 256)]

            def cols8(w, c0):
                v = w.rearrange("(k p) n -> p k n", p=P)
                return lambda i: v[:, :, bass.ds(i * 256 + c0, 256)]
            stream("mod0", 12, cols8(a["mod_w"][0], 0), sub8)
            win = a["ev_w_in"][0]
            stream("u", 4, cols8(win, 0), sub8)
            stream("gb", 4, cols8(win, 5 * 1024), sub8)

            stream("x2", 4, cols8(win, 4 * 1024), sub8)
            wglu = a["s5_glu_w"][0].rearrange("(k p) n -> p k n", p=P)
            wga = win.rearrange("(k p) n -> p k n", p=P)
            for i in range(8):
                n = chunk["ga_glu"] + i
                sp.wait_ge(S("ring_used"), n - NSLOT + 1)
                c0 = (i // 2) * 256
                src = wglu[:, :, c0:c0 + 256] if i % 2 else wga[:, :, 1024 + c0:1024 + c0 + 256]
                sp.dma_start(at(ring(n % NSLOT), sub8), src).then_inc(S(f"ring_full{n % NSLOT}"), 16)
            stream("v", 4, cols8(win, 2 * 1024), sub8)
            stream("x1", 4, cols8(win, 3 * 1024), sub8)

            stream("mod1", 12, cols8(a["mod_w"][1], 0), sub8)

            def stream_out(name, w):
                v = w.rearrange("(c k p) n -> c p k n", k=4, p=P)
                for i in range(8):
                    n = chunk[name] + i
                    sp.wait_ge(S("ring_used"), n - NSLOT + 1)
                    sp.dma_start(at(ring(n % NSLOT), [(512, 4), (1, 512)]),
                                 v[i % 4, :, :, (i // 4) * 512:(i // 4) * 512 + 512]).then_inc(S(f"ring_full{n % NSLOT}"), 16)
            stream_out("ev_out", a["ev_w_out"][0])

            def load_chunk(n, dims, src):
                sp.wait_ge(S("ring_used"), n - NSLOT + 1)
                sp.dma_start(at(ring(n % NSLOT), dims), src).then_inc(S(f"ring_full{n % NSLOT}"), 16)
            wssd = a["ssd_w_in"][0].rearrange("(k p) n -> p k n", p=P)
            load_chunk(chunk["ssd_dt"], [(64, 8), (1, 64)], wssd[:, :, 5120:5184])
            for g in range(SG):
                n = chunk["ssd_g"] + 3 * g
                load_chunk(n, [(256, 8), (1, P)], wssd[:, :, 2 * DI + g * P:2 * DI + (g + 1) * P])
                sp.dma_start(at(ring(n % NSLOT) + P, [(256, 8), (1, P)]),
                             wssd[:, :, 2 * DI + 512 + g * P:2 * DI + 512 + (g + 1) * P]).then_inc(S(f"ssd_c_loaded{g % 2}"), 16)
                for j in range(2):
                    c0 = DI + g * 512 + j * 256
                    load_chunk(n + 1 + j, sub8, wssd[:, :, c0:c0 + 256])
            for c in range(8):
                load_chunk(chunk["ssd_z"] + c, sub8, wssd[:, :, c * 256:(c + 1) * 256])
            stream_out("ssd_out", a["ssd_w_out"][0])


_OUTS = [("y_prompt", (1, NCTX, D)), ("y_sample", (1, NLAT, D)), ("new_re", (1, 1, 2, 64, SP)), ("new_im", (1, 1, 2, 64, SP)),
         ("new_ssd", (1, 1, 2, SH, SHD, SN))]


def kernel(**inputs):
    import concourse.bacc as bacc
    from concourse.bass_utils import run_bass_kernel_spmd

    arrays = {name: np.ascontiguousarray(value) for name, value in inputs.items()}
    arrays["tables"], arrays["emb"], arrays["deltas"] = constant_tables()
    nc = bacc.Bacc("TRN2", target_bir_lowering=False, num_devices=1)
    ins = {name: nc.dram_tensor(name, value.shape, mybir.dt.from_np(value.dtype), kind="ExternalInput").ap()
           for name, value in arrays.items()}
    outs = {name: nc.dram_tensor(name, shape, F32, kind="ExternalOutput").ap() for name, shape in _OUTS}
    build(nc, ins, outs)
    result = run_bass_kernel_spmd(nc, [arrays], core_ids=[0]).results[0]
    return tuple(result[name] for name, _ in _OUTS)
```

```python
import math

import numpy as np

import concourse.bass as bass
from concourse import mybir

F32 = mybir.dt.float32
F32R = mybir.dt.float32r
BF16 = mybir.dt.bfloat16
ALU = mybir.AluOpType
ACT = mybir.ActivationFunctionType

P = 128
D = 1024
KT = D // P
NLAT, NCTX = 512, 128
NT = NLAT + NCTX
TT = NT // P
EPS = 1e-6
Q8 = 8
GS = 16
SP = 64
OCT = 8
NPAIR = 32
XC = NT // Q8 + 1
GAP = NLAT // Q8
SLOTS = XC + 1
SLOTW = 4 * NPAIR
LATX, CTXX = NLAT // Q8, NCTX // Q8
H1 = 1024
TWO_PI = 2.0 * math.pi
C1, C2 = 6.28125, float(np.float32(TWO_PI - 6.28125))
C3 = TWO_PI - 6.28125 - C2
MAGIC = 12582912.0
HW = 256
NW = H1 // HW
SH = 32
SHD = 64
SN = 128
SG = 4
DI = 2048

T_GF = 0
T_GI = T_GF + 2048
T_CS = T_GI + 2048
T_CX = T_CS + 2048
T_TN = T_CX + 640
T_M16 = T_TN + 5
T_UP = T_M16 + 16
T_LO = T_UP + 128
T_END = T_LO + 128


def constant_tables():
    n_all = 2 * NLAT
    korder = np.concatenate([np.arange(256), 511 - np.arange(256)])
    t = np.zeros((P, T_END), np.float64)
    w = TWO_PI * (korder + 0.5) / n_all
    s = (-1.0) ** korder
    for sign_i, sign in enumerate((1.0, -1.0)):
        for kt in range(2):
            tau = kt * P + np.arange(P)[:, None] + 0.5
            t[:, T_GF + (kt * 2 + sign_i) * 512:][:, :512] = np.cos(w * tau) + sign * s * np.sin(w * tau)
        for kt in range(4):
            wk, sk = w[kt * P:(kt + 1) * P, None], s[kt * P:(kt + 1) * P, None]
            tau = np.arange(256)[None, :] + 0.5
            t[:, T_GI + (kt * 2 + sign_i) * 256:][:, :256] = (np.cos(wk * tau) + sign * sk * np.sin(wk * tau)) / n_all
    for kt in range(4):
        n = lag_of(kt)[:, None]
        t[:, T_CS + kt * 512:][:, :256] = np.cos(w[:256] * n)
        t[:, T_CS + kt * 512 + 256:][:, :256] = s[:256] * np.sin(w[:256] * n)
    wc = TWO_PI * (np.arange(P) + 0.5) / (2 * NCTX)
    a = wc[None, :] * np.arange(P)[:, None]
    for i, m in enumerate((np.cos(a), -np.sin(a), np.sin(a), np.cos(a.T) / NCTX, -np.sin(a.T) / NCTX)):
        t[:, T_CX + i * P:][:, :P] = m
    f = np.float32
    for kt in range(4):
        t[:, T_TN + kt] = -(lag_of(kt).astype(f) / f(NLAT - 1))
    t[:, T_TN + 4] = -(np.arange(P).astype(f) / f(NCTX - 1))
    r = np.arange(P)
    t[:, T_M16:T_M16 + 16] = (r[:, None] % 16) == np.arange(16)[None, :]
    t[:, T_UP:T_UP + P] = r[:, None] <= r[None, :]
    t[:, T_LO:T_LO + P] = r[:, None] >= r[None, :]
    bands = np.linspace(1e-4, 15, 16, dtype=f)
    emb = np.zeros((33, NT), f)
    for L, cols, n in ((NLAT, slice(0, NLAT), np.concatenate([lag_of(k) for k in range(4)])), (NCTX, slice(NLAT, NT), r)):
        tm = n.astype(f)[:, None]
        ang = (f(2.0 * math.pi / L) * tm * bands).astype(f)
        emb[:, cols] = np.concatenate([tm / f(L - 1), np.cos(ang), np.sin(ang)], -1).T
    target = math.log(1e-2)
    deltas = np.abs(np.linspace(target / 1.5, target / 0.3, H1, dtype=f))[None, :]
    return t.astype(f), emb, deltas


def lag_of(kt):
    return 2 * (P * (kt % 2) + np.arange(P)) + kt // 2


class Arena:

    def __init__(self, tensor, width):
        self.tensor, self.width, self.taken = tensor, width, []

    def place(self, size, first, last):
        size += size % 2
        gaps, at_ = [], 0
        for a, b in sorted((a, b) for a, b, f, l in self.taken if f <= last and first <= l):
            if a - at_ >= size:
                gaps.append((a - at_, at_))
            at_ = max(at_, b)
        start = min(gaps)[1] if gaps else at_
        if start + size > self.width:
            raise ValueError(f"SBUF is full: {start + size} of {self.width} in stages {first}-{last}")
        self.taken.append((start, start + size, first, last))
        return start

    def at(self, base, dims, p0=0, np_=P):
        return bass.AP(self.tensor, p0 * self.width + base, [[self.width, np_]] + [list(d) for d in dims])


def build(nc, a, outs):
    from contextlib import ExitStack
    with ExitStack() as ctx:
        sems = {}

        def S(name):
            if name not in sems:
                sems[name] = ctx.enter_context(nc.semaphore(name))
            return sems[name]

        def psum(name, shape):
            return ctx.enter_context(nc.psum_tensor(name, shape, F32))

        width = 53208
        arena = Arena(ctx.enter_context(nc.sbuf_tensor("arena", [P, width], F32)), width)
        place, at = arena.place, arena.at
        GP = psum("gemm_pair", [P, 2, 1024])
        MP = psum("misc_banks", [P, 4, 512])

        RING, RSLOT, NSLOT = place(4 * 2048, 1, 9), 2048, 4
        IDENT, ONES = place(P, 1, 9), place(P, 1, 9)
        VC = place(3 * P, 1, 9)
        TAB = place(T_END - T_TN, 1, 9)
        SC, MV, AB, EPSB, STAT = place(16, 1, 9), place(96, 1, 9), place(32, 1, 9), place(2, 1, 9), place(40, 1, 9)
        HT = place(8 * NT, 1, 9)
        VR = place(3 * P, 1, 1)
        SVC = place(5 * 64, 1, 2)
        PC, PW = place(2 * 2 * NPAIR * 9, 1, 3), place(2 * 9 * 64, 1, 2)
        BBAR = place(2 * 64 * GS, 1, 3)
        SCA = place(256, 1, 2)
        X1, MROW = place(TT * D, 1, 1), place(4 * 512, 1, 1)
        XN, SQ = place(2 * D, 1, 1), place(D, 1, 1)
        SV5, BRAW, TMP5 = place(5 * P, 1, 1), place(2 * 64 * GS, 1, 1), place(16 * 64, 1, 1)
        TMPB = place(2 * 1024, 1, 1)
        U, HS = place(64 * XC, 2, 4), place(SLOTS * SLOTW, 2, 3)
        GB = place(8 * NT, 2, 7)
        BL = place(2048, 2, 3)
        UT, MT = place(2 * NT, 2, 2), place(2 * 1024, 2, 2)
        BB, TB = place(2 * 2048, 2, 2), place(1024, 2, 2)
        CVX, TLX = BB, BB + 2 * NT
        SCT, SCB, SCP = place(512, 2, 2), place(256, 2, 2), place(256, 2, 2)
        YT, YW = U, 8 * XC
        CV, TC = place(2 * NT, 5, 5), place(576, 3, 3)
        CRAW, CT = BL, place(384, 3, 3)
        CE, BBD = place(3 * 2304, 3, 3), place(512, 3, 3)
        WS, TTB = (place(240, 3, 3), place(240, 3, 3)), place(2 * 1024, 3, 3)
        YS, MT2 = place(8 * XC, 3, 3), place(1024, 3, 3)
        FS, FO = CE + 2 * 2304, CE + 2 * 2304 + P
        TA, TG = place(2 * NT, 4, 4), place(2 * NT, 4, 4)
        ZA = place(8 * NT, 4, 7)
        VS, XS, PQ = place(5 * H1, 5, 6), place(5 * H1, 5, 6), place(2 * NT, 5, 5)
        GF, GI, DEL = HT, HT + 2048, HT + 4096
        CS, CX = place(2048, 5, 6), place(640, 5, 6)
        TAPS, FQ = place(2 * 5 * HW, 4, 6), place(2 * 5 * HW, 5, 6)
        PR, FE, FO2, W3 = place(2 * 5 * HW, 5, 6), place(NT, 5, 6), place(NT, 5, 6), place(2 * HW, 4, 6)
        KH, FBIAS, FCOL = place(2 * 5 * HW, 6, 6), place(HW, 5, 6), place(4, 4, 6)
        WIN, HTMP, MTMP = place(5 * HW, 6, 6), place(2 * HW, 6, 6), place(2 * HW, 6, 6)
        PT = YT2 = place(640, 6, 6)
        EMB, FA, FK = TAPS, FQ, PR
        XRES = place(TT * D, 7, 7)
        GR, DG = place(2 * D, 7, 7), place(2 * D, 7, 7)
        RT = place(1024, 7, 7)
        XN7, SQ7 = place(2 * D, 7, 7), place(D, 7, 7)
        Y = place(TT * DI, 8, 9)
        XCH, XT = place(4 * NT, 8, 8), place(TT * 512, 8, 8)
        BC, BTOK = place(2 * 2 * NT, 8, 8), place(TT * P, 8, 8)
        CBM, HP = place(2 * TT * P, 8, 8), place(2 * 4 * 512, 8, 8)
        XW, YTMP = place(2 * 512, 8, 8), place(2 * 512, 8, 8)
        AM, EX, MM = place(2 * 1024, 8, 8), place(2 * 1024, 8, 8), place(2 * 1024, 8, 8)
        INIT, FOUT = place(2 * 512, 8, 8), place(2 * 512, 8, 8)
        CW = 2 * TT * SH
        DTB, AD, EE, WW, TOT, SPT = (place(n * CW, 8, 8) for n in (1, 1, 1, 1, 1, 3))
        SGT, SLT = place(P, 8, 8), place(P, 8, 8)
        BROW, AROW, DROW = place(64, 8, 8), place(64, 8, 8), place(SH, 8, 8)
        XRES9 = place(TT * D, 9, 9)
        GR9, DG9 = place(2 * D, 9, 9), place(2 * D, 9, 9)
        RT9, FNW = place(1024, 9, 9), place(D, 9, 9)
        ZT, SZ, SQZ = place(16 * NT, 9, 9), place(4 * 256, 9, 9), place(256, 9, 9)
        SQ9, SUMS = DG9, place(48, 9, 9)
        spill = nc.dram_tensor("residual_rows", (TT, P, D), F32, kind="Internal").ap()
        strips = nc.dram_tensor("strips", (OCT, P, 240), F32, kind="Internal").ap()
        turn_of, slot_of = {}, {}
        uses = [0] * 8
        gemm_of = {}

        def ring(slot):
            return RING + slot * RSLOT

        def vcol(tile, row):
            return at(VC + tile * P + row, [(1, 1)])

        chunk = {}
        n = 0
        for name, cnt in (("mod0", 8), ("u", 4), ("gb", 4), ("x2", 4), ("ga_glu", 8), ("v", 4), ("x1", 4), ("mod1", 16),
                          ("ev_out", 8), ("ssd_dt", 1), ("ssd_g", 12), ("ssd_z", 8), ("ssd_out", 8)):
            chunk[name] = n
            n += cnt

        def bank_ap(b):
            return MP[:, b, :] if b < 4 else GP[:, b // 2 - 2, (b % 2) * 512:(b % 2) * 512 + 512]

        def barrier(eng, k):
            eng.drain().then_inc(S("stage_end"), 1)
            eng.wait_ge(S("stage_end"), 4 * k)

        ITEMS = tuple((2 * pair + w, r) for pair in range(NW // 2) for r in range(2) for w in range(2))
        STATES = ((0, 4), (1, 4), (0, 0), (1, 3), (0, 1), (1, 2), (0, 2), (1, 1))

        def next_tiles(g, t):
            return () if g == SG - 1 else [6 * (g + 1) + n for n in ((0, 1), (2,), (3,), (4,), (5,))[t]]

        def coef(buf, d, t, g, n):
            return at(buf + d * TT * SH + t * SH + 8 * g, [(1, 8), (0, n)])

        block = ctx.enter_context(nc.Block())

        @block.tensor
        def _(pe):
            mm, tr = nc.tensor.matmul, nc.tensor.transpose
            ident = at(IDENT, [(1, P)])

            rotation = [0, 1, 2, 3]

            def turn(*name):
                t = turn_of[name] = len(turn_of)
                b = slot_of[name] = rotation[0]
                rotation.append(rotation.pop(0))
                if uses[b]:
                    pe.wait_ge(S(f"bank_read{b}"), uses[b])
                uses[b] += 1
                return bank_ap(b)

            def filled(ins):
                ins.then_inc(S("bank_filled"), 1)

            def ring_wait(i):
                pe.wait_ge(S(f"ring_full{i % NSLOT}"), 16 * (i // NSLOT + 1))

            def mod_rows(name, b):
                bank = turn(name, "rows", b)
                for j in range(2):
                    ci = chunk[name] + 2 * b + j
                    ring_wait(ci)
                    for k in range(KT):
                        i = mm(bank[0:2, j * 256:(j + 1) * 256], at(SC + 2 * k, [(1, 2)]), at(ring(ci % NSLOT) + k * 256, [(1, 256)]),
                               start=k == 0, stop=k == KT - 1)
                filled(i)

            def mod_columns(name, b, src):
                pe.wait_ge(S("mod_rows"), (0 if name == "mod0" else 4) + b + 1)
                bank = turn(name, "columns", b)
                for j in range(4):
                    i = tr(bank[:, 2 * j:2 * j + 2], at(src + j * P, [(1, P)], 0, 2), at(IDENT, [(1, 2)], 0, 2))
                filled(i)

            def normed_transposed(layer):
                xn = XN7 if layer else XN
                for t in range(TT):
                    pe.wait_ge(S("xn_ready"), layer * TT + t + 1)
                    for half in range(2):
                        bank = turn("xt", layer, t, half)
                        for j in range(4):
                            i = tr(bank[:, j * P:(j + 1) * P], at(xn + (t % 2) * D + (half * 4 + j) * P, [(1, P)]), ident)
                        filled(i)

            def gemm_tile(name, o, ci, m, rhs=HT, rw=NT):
                g = gemm_of[name, o] = len(gemm_of)
                if g >= 2:
                    pe.wait_ge(S(f"gemm_read{g % 2}"), g // 2)
                for k in range(KT):
                    w = at(ring(ci % NSLOT) + k * 256 + m * P, [(1, P)])
                    mm(GP[:, g % 2, 0:NLAT], w, at(rhs + k * rw, [(1, NLAT)]), start=k == 0, stop=k == KT - 1)
                    i = mm(GP[:, g % 2, NLAT:NT], w, at(rhs + k * rw + NLAT, [(1, NCTX)]), start=k == 0, stop=k == KT - 1)
                i.then_inc(S("gemm_filled"), 1)

            def part_tile(name, o, rhs=HT):
                ci = chunk[name] + o // 2
                if o % 2 == 0:
                    ring_wait(ci)
                gemm_tile(name, o, ci, o % 2, rhs)
                if o % 2:
                    used()

            def used():
                pe.wait_ge(S("gemm_filled"), len(gemm_of))
                pe.sem_inc(S("ring_used"), 1)

            pe.wait_ge(S("ident_ready"), 3)
            pe.wait_ge(S("cond_rows"), 32)
            bank = turn("cond")
            filled(tr(bank[:, 0:16], at(VR, [(1, P)], 0, 16), at(IDENT, [(1, 16)], 0, 16)))
            pe.wait_ge(S("cond_ready"), 1)
            mod_rows("mod0", 0)
            pe.wait_ge(S("bank_filled"), len(turn_of))
            pe.sem_inc(S("ring_used"), 2)
            pe.wait_ge(S("rows_loaded"), 16 * 13)
            bank = turn("vec")
            for i, rows in enumerate((80, 112, 112)):
                last = tr(bank[:, i * P:i * P + rows], at(VR + i * P, [(1, P)], 0, rows), at(IDENT, [(1, rows)], 0, rows))
            filled(last)
            bank = turn("s5v")
            pe.wait_ge(S("s5rows"), 1)
            for i in range(5):
                last = tr(bank[:, i * 64:(i + 1) * 64], at(SV5 + i * P, [(1, P)], 0, 64), at(IDENT, [(1, 64)], 0, 64))
            filled(last)
            for b in range(1, 5):
                if b < 4:
                    mod_rows("mod0", b)
                    pe.wait_ge(S("bank_filled"), len(turn_of))
                    pe.sem_inc(S("ring_used"), 2)
                mod_columns("mod0", b - 1, MROW + (b - 1) * 512)
            normed_transposed(0)
            barrier(pe, 1)

            def chunk_inputs(o):
                pe.wait_ge(S("ut_ready"), o + 1)
                for half in range(2):
                    bank = turn("ma", o, half)
                    for j in range(4):
                        i = tr(bank[0:80, j * P:(j + 1) * P], at(UT + (o % 2) * NT + half * 4 + j, [(Q8, 80)]), ident)
                    filled(i)
                pe.wait_ge(S("bb_ready"), o + 1)
                for dc in range(4):
                    bank = turn("bt", o, dc)
                    for q in range(4):
                        i = tr(bank[:, q * P:(q + 1) * P], at(BB + (o % 2) * 2048 + (dc * 4 + q) * P, [(1, P)]), ident)
                    filled(i)
                pe.wait_ge(S("mt_ready"), 2 * o + 2)
                for half in range(2):
                    bank = turn("ub", o, half)
                    for j in range(4):
                        i = tr(bank[:, j * 80:(j + 1) * 80], at(MT + (o % 2) * 1024 + (half * 4 + j) * P, [(1, P)], 0, 80),
                               at(IDENT, [(1, 80)], 0, 80))
                    filled(i)
                pe.wait_ge(S("u_ready"), 2 * o + 2)
                for dc in range(4):
                    pe.wait_ge(S("bl_ready"), 4 * o + dc + 1)
                    bank = turn("s", o, dc)
                    for q in range(4):
                        for g2 in range(2):
                            i = mm(bank[64 * g2:64 * g2 + 64, q * XC:(q + 1) * XC],
                                   at(BL + (dc * 4 + q) * P + 64 * g2, [(1, 64)]),
                                   at(U + (8 * o + 2 * q + g2) * XC, [(1, XC)]), start=True, stop=True)
                    filled(i)

            pe.wait_ge(S("u_gap"), 1)
            part_tile("u", 0)
            for o in range(OCT):
                if o + 1 < OCT:
                    part_tile("u", o + 1)
                chunk_inputs(o)
            for name in ("gb", "x2"):
                for o in range(OCT):
                    part_tile(name, o)
            barrier(pe, 2)
            rotation[:] = range(8)

            def c_transposed(o):
                bank = turn("ct", o)
                for dc in range(4):
                    for e in range(2):
                        i = mm(bank[64 * e:64 * e + 64, dc * 64:dc * 64 + 64],
                               at(CRAW + ((dc % 2 * 2 + dc // 2) * OCT + o) * SP, [(1, SP)]),
                               at(IDENT + 16 * e, [(32, 4), (1, 16)]), start=True, stop=True)
                filled(i)

            def lag_kernels(o):
                pe.wait_ge(S("ce_ready"), o + 1)
                bank = turn("k", o)
                for d in range(2):
                    for q in range(4):
                        for c in range(2):
                            i = mm(bank[32 * q:32 * q + 32, d * P:(d + 1) * P],
                                   at(BBD + (2 * d + c) * P + q * 32, [(1, 32)]),
                                   at(CE + (o % 3) * 2304 + ((2 * d + c) * 4 + q) * 144 + 16 * d, [(1, P)]),
                                   start=c == 0, stop=c == 1)
                filled(i)

            def s5_output(o):
                pe.wait_ge(S(f"t_loaded{o % 2}"), 16 * 8 * (o // 2 + 1))
                banks = [turn("y", o, e) for e in range(2)]
                for q in range(4):
                    for e in range(2):
                        mm(banks[e][:, q * XC:(q + 1) * XC], at(TTB + (o % 2) * 1024 + (2 * q + e) * P, [(1, P)]),
                           at(U + (8 * o + 2 * q + e) * XC, [(1, XC)]), start=True, stop=False)
                    for dc in range(4):
                        d, c = dc // 2, dc % 2
                        slot0, step = (0, SLOTW) if d == 0 else (XC - 1, -SLOTW)
                        for e in range(2):
                            i = mm(banks[e][:, q * XC:(q + 1) * XC],
                                   at(CE + (o % 3) * 2304 + (dc * 4 + q) * 144 + 16 * (1 - d), [(1, P)], 64 * e, 64),
                                   at(HS + slot0 * SLOTW + d * 64 + c * 32 + 4 * o + q, [(step, XC)], 64 * e, 64),
                                   start=False, stop=dc == 3)
                            if dc == 3 and q == 3:
                                filled(i)

            def tokens_of(o):
                for half in range(2):
                    pe.wait_ge(S("ys_ready"), 2 * o + half + 1)
                    bank = turn("yt", o, half)
                    for j in range(4):
                        i = tr(bank[0:XC, j * P:(j + 1) * P], at(YS + (half * 4 + j) * XC, [(1, XC)]), ident)
                    filled(i)

            def channels_of(o):
                pe.wait_ge(S("mt2_ready"), 2 * o + 2)
                for half in range(2):
                    bank = turn("yc", o, half)
                    for j in range(4):
                        i = tr(bank[:, j * XC:(j + 1) * XC], at(MT2 + (half * 4 + j) * P, [(1, P)], 0, XC),
                               at(IDENT, [(1, XC)], 0, XC))
                    filled(i)

            pe.wait_ge(S("c_loaded"), 16 * 4)
            c_transposed(0)
            pe.wait_ge(S("fs_ready"), 1)
            bank = turn("fs")
            for c in range(2):
                i = tr(bank[0:64, c * P:(c + 1) * P], at(FS + c * 64, [(1, 64)]), ident)
            filled(i)
            for o in range(OCT + 2):
                if o >= 2:
                    tokens_of(o - 2)
                if o < OCT:
                    lag_kernels(o)
                if o + 1 < OCT:
                    c_transposed(o + 1)
                if o >= 2:
                    channels_of(o - 2)
                if 1 <= o <= OCT:
                    s5_output(o - 1)
            barrier(pe, 3)
            rotation[:] = range(4)

            for ch in range(4):
                ci = chunk["ga_glu"] + 2 * ch
                ring_wait(ci)
                for m in range(2):
                    gemm_tile("ga", 2 * ch + m, ci, m)
                used()
                ring_wait(ci + 1)
                for m in range(2):
                    gemm_tile("glu", 2 * ch + m, ci + 1, m, YT, YW)
                used()
            barrier(pe, 4)

            def token_major(name, o):
                for half in range(2):
                    if half == 0:
                        pe.wait_ge(S(name + "_conv"), o + 1)
                    bank = turn(name + "t", o, half)
                    for j in range(4 if half == 0 else 1):
                        i = tr(bank[:, j * P:(j + 1) * P], at(PQ + (o % 2) * NT + (half * 4 + j) * P, [(1, P)]), ident)
                    filled(i)
            def mlp(n, w, kn, m, src):
                for half, (c0, cn) in enumerate(((0, 512), (512, P))):
                    bank = turn("mlp", n, half)
                    filled(mm(bank[0:m, 0:cn], at(w, [(1, m)], 0, kn), at(src + c0, [(1, cn)], 0, kn), start=True, stop=True))

            pe.wait_ge(S("mlp_loaded"), 16 * 4)
            mlp(1, W3 + HW, 33, 64, EMB)
            for name in ("v", "x1"):
                for o in range(OCT + 1):
                    if o < OCT:
                        part_tile(name, o)
                    if name == "v" and o == 0:
                        pe.wait_ge(S("mlp_ready"), 1)
                        mlp(2, W3, 64, P, EMB + 640)
                    if o >= 1:
                        token_major(name, o - 1)
            barrier(pe, 5)

            def taps(i):
                pe.wait_ge(S(f"w3_loaded{i % 2}"), 32 * (i // 2 + 1))
                pe.wait_ge(S("fbias_loaded"), 16 * (i + 1))
                for n in range(5):
                    bank = turn("f", i, n)
                    rhs = at(W3 + (i % 2) * HW, [(1, HW)])
                    biased = n in (0, 4)
                    mm(bank[:, 0:HW], at(FE + n * P, [(1, P)]), rhs, start=True, stop=not biased)
                    if biased:
                        mm(bank[:, 0:HW], at(IDENT, [(1, P)], 0, 1), at(FBIAS, [(1, HW)], 0, 1), start=False, stop=True)
                    filled(mm(bank[:, HW:2 * HW], at(FO2 + n * P, [(1, P)]), rhs, start=True, stop=True))

            def filter_transform(i):
                pe.wait_ge(S("taps_ready"), i + 1)
                for kind in range(2):
                    for ft in range(2):
                        bank = turn("kh", i, kind, ft)
                        for par in range(2):
                            for kt in range(2):
                                n = par * 2 + kt
                                j = mm(bank[:, par * HW:(par + 1) * HW], at(CS + n * 512 + kind * 256 + ft * P, [(1, P)]),
                                       at(TAPS + (kind * 5 + n) * HW, [(1, HW)]), start=kt == 0, stop=kt == 1)
                        filled(j)
                bank = turn("khc", i)
                for kind in range(2):
                    j = mm(bank[:, kind * HW:(kind + 1) * HW], at(CX + (0, 2)[kind] * P, [(1, P)]),
                           at(TAPS + (kind * 5 + 4) * HW, [(1, HW)]), start=True, stop=True)
                filled(j)

            def input_transform(i):
                w, r = ITEMS[i]
                if r:
                    pe.wait_ge(S("z_ready"), w + 1)
                for ft in range(4):
                    bank = turn("vf", i, ft)
                    for pm in range(2):
                        for kt in range(2):
                            j = mm(bank[:, pm * HW:(pm + 1) * HW], at(GF + (kt * 2 + pm) * 512 + ft * P, [(1, P)]),
                                   at(VS + (pm * 2 + kt) * H1 + w * HW, [(1, HW)]), start=kt == 0, stop=kt == 1)
                    filled(j)
                bank = turn("vf", i, 4)
                for pm in range(2):
                    j = mm(bank[:, pm * HW:(pm + 1) * HW], at(CX + pm * P, [(1, P)]), at(VS + 4 * H1 + w * HW, [(1, HW)]),
                           start=True, stop=True)
                filled(j)

            def inverse_transform(i):
                pe.wait_ge(S("pr_ready"), i + 1)
                for tt in range(2):
                    bank = turn("yi", i, tt)
                    for pm in range(2):
                        for ft in range(4):
                            j = mm(bank[:, pm * HW:(pm + 1) * HW], at(GI + (ft * 2 + pm) * 256 + tt * P, [(1, P)]),
                                   at(PR + (pm * 5 + ft) * HW, [(1, HW)]), start=ft == 0, stop=ft == 3)
                    filled(j)
                bank = turn("yi", i, 2)
                for pm in range(2):
                    j = mm(bank[:, 0:HW], at(CX + (3 + pm) * P, [(1, P)]), at(PR + (pm * 5 + 4) * HW, [(1, HW)]),
                           start=pm == 0, stop=pm == 1)
                filled(j)

            def channel_major(w):
                pe.wait_ge(S("yh_ready"), w + 1)
                for m in range(2):
                    bank = turn("zt", w, m, 0)
                    for n in range(4):
                        j = tr(bank[:, n * P:(n + 1) * P], at(VS + n * H1 + w * HW + m * P, [(1, P)]), ident)
                    filled(j)
                    bank = turn("zt", w, m, 1)
                    filled(tr(bank[:, 0:P], at(VS + 4 * H1 + w * HW + m * P, [(1, P)]), ident))

            pe.wait_ge(S("cs_loaded"), 32)
            rotation[:] = range(8)

            def mod_free(b):
                mod_columns("mod1", b, ring((chunk["mod1"] + 2 * b) % NSLOT))
                pe.wait_ge(S("bank_filled"), len(turn_of))
                pe.sem_inc(S("ring_used"), 2)
            taps(0)
            filter_transform(0)
            pe.wait_ge(S("hy_tables"), 32)
            input_transform(0)
            taps(1)
            for i in range(2 * NW):
                if i + 1 < 2 * NW:
                    filter_transform(i + 1)
                if i + 2 < 2 * NW:
                    taps(i + 2)
                if i and ITEMS[i - 1][1]:
                    channel_major(ITEMS[i - 1][0])
                if i + 1 < 2 * NW:
                    input_transform(i + 1)
                if i:
                    mod_free(i - 1)
                mod_rows("mod1", i)
                inverse_transform(i)
            channel_major(NW - 1)
            mod_free(2 * NW - 1)
            barrier(pe, 6)
            rotation[:] = range(4)

            def gate_rows(layer):
                pe.wait_ge(S("dg_ready"), layer + 1)
                for w in range(2):
                    for half in range(2):
                        bank = turn("gr", layer, w, half)
                        for j in range(4):
                            i = mm(bank[:, j * P:(j + 1) * P], at(ONES, [(1, P)]), at((DG9 if layer else DG) + w * D + (half * 4 + j) * P, [(1, P)]),
                                   start=True, stop=True)
                        filled(i)

            def out_projection(layer, name, ztile):
                for half in range(2):
                    t4 = turn("acc4", layer, half)
                    acc = [GP[:, b // 2, (b % 2) * 512:(b % 2) * 512 + 512] for b in range(4)] + [t4]
                    for c in range(4):
                        ci = chunk[name] + half * 4 + c
                        ring_wait(ci)
                        for kk in range(4):
                            k = 4 * c + kk
                            for t in range(TT):
                                if k == 0 and t < 4 and layer + half:
                                    pe.wait_ge(S("acc_read"), 4 * (2 * layer + half - 1) + t + 1)
                                i = mm(acc[t], at(ztile(k) + t * P, [(1, P)]), at(ring(ci % NSLOT) + kk * 512, [(1, 512)]),
                                       start=k == 0, stop=k == 15)
                        if c < 3:
                            i.then_inc(S("ring_used"), 1)
                    filled(i)
                    pe.wait_ge(S("bank_filled"), len(turn_of))
                    pe.sem_inc(S("ring_used"), 1)
            gate_rows(0)
            out_projection(0, "ev_out", lambda k: ZA + k * NT if k < 8 else GB + (k - 8) * NT)
            normed_transposed(1)
            barrier(pe, 7)

            ring_wait(chunk["ssd_dt"])
            bank = turn("dt")
            for t in range(TT):
                for k in range(KT):
                    i = mm(bank[:, t * 64:(t + 1) * 64], at(HT + k * NT + t * P, [(1, P)]), at(ring(chunk["ssd_dt"] % NSLOT) + k * 64, [(1, 64)]),
                           start=k == 0, stop=k == KT - 1)
            filled(i)
            pe.wait_ge(S("bank_filled"), len(turn_of))
            pe.sem_inc(S("ring_used"), 1)

            def ssd_gemm(n):
                if n % 6 == 1:
                    pe.wait_ge(S(f"ssd_c_loaded{n // 6 % 2}"), 16 * (n // 12 + 1))
                part_tile("ssd_g", n)
            for n in range(6):
                ssd_gemm(n)
            pe.wait_ge(S("ad_ready"), 1)
            for nm, masks in (("ce", (TAB + T_UP - T_TN, TAB + T_LO - T_TN)), ("cw", (SGT, SLT)), ("ctot", (ONES, ONES))):
                bank = turn(nm)
                for d in range(2):
                    i = mm(bank[:, d * 160:(d + 1) * 160], at(masks[d], [(1, P)]), at(AD + d * 160, [(1, 160)]), start=True, stop=True)
                filled(i)


            def decay_sums(g, t):
                pe.wait_ge(S("am_ready"), 2 * (TT * g + t + 1))
                for half in range(2):
                    bank = turn("ar", g, t, half)
                    for d, mask in enumerate((SGT, SLT)):
                        i = mm(bank, at(mask, [(1, P)]), at(AM + d * 1024 + half * 512, [(1, 512)]), start=d == 0, stop=d == 1)
                    filled(i)

            def group(g):
                bc = BC + (g % 2) * 2 * NT
                pe.wait_ge(S("cv_ready"), 6 * g + 2)
                for part in range(2):
                    bank = turn("bg", g, part)
                    for j in range((4, 1)[part]):
                        i = tr(bank[:, j * P:(j + 1) * P], at(bc + (4 * part + j) * P, [(1, P)]), ident)
                    filled(i)
                for part in range(2):
                    bank = turn("cb", g, part)
                    for j in range((4, 1)[part]):
                        tok = (4 * part + j) * P
                        i = mm(bank[:, j * P:(j + 1) * P], at(bc + tok, [(1, P)]), at(bc + NT + tok, [(1, P)]), start=True, stop=True)
                    filled(i)
                pe.wait_ge(S("init_loaded"), 32 * (g + 1))
                for d in range(2):
                    bank = turn("in", g, d)
                    for j in range(4):
                        i = tr(bank[:, j * P:(j + 1) * P], at(INIT + d * 512 + j * P, [(1, P)]), ident)
                    filled(i)
                pe.wait_ge(S("cv_ready"), 6 * g + 6)
                for t in range(TT):
                    bank = turn("xg", g, t)
                    for j in range(4):
                        i = tr(bank[:, j * P:(j + 1) * P], at(XCH + j * NT + t * P, [(1, P)]), ident)
                    filled(i)
                decay_sums(g, 0)
                pe.wait_ge(S("btok_ready"), g + 1)
                for k, (d, t) in enumerate(STATES):
                    pe.wait_ge(S("xw_ready"), 8 * g + k + 1)
                    bank = turn("st", g, k)
                    xw = XW + (k % 2) * 512
                    if t == 4:
                        for j in range(4):
                            i = mm(bank[:, j * P:(j + 1) * P], at(xw + j * P, [(1, P)]), at(BTOK + t * P, [(1, P)]), start=True, stop=True)
                    else:
                        i = mm(bank, at(BTOK + t * P, [(1, P)]), at(xw, [(1, 512)]), start=True, stop=True)
                    filled(i)
                for t in range(TT):
                    for n in next_tiles(g, t):
                        ssd_gemm(n)
                    if t + 1 < TT:
                        decay_sums(g, t + 1)
                    if t == 0:
                        pe.wait_ge(S("hp_ready"), g + 1)
                    if t < 4:
                        for d in range(2):
                            bank = turn("yo", g, t, d)
                            filled(mm(bank, at(bc + NT + t * P, [(1, P)]), at(HP + (4 * d + t) * 512, [(1, 512)]), start=True, stop=True))
                    pe.wait_ge(S("mm_ready"), TT * g + t + 1)
                    bank = turn("yd", g, t)
                    for h in range(8):
                        i = mm(bank[:, h * 64:(h + 1) * 64], at(EX + (TT * g + t) % 2 * 1024 + h * P, [(1, P)]),
                               at(XT + t * 512 + h * 64, [(1, 64)]), start=True, stop=True)
                    filled(i)
            for g in range(SG):
                group(g)
            barrier(pe, 8)

            def z_transposed(c):
                pe.wait_ge(S("yz_ready"), TT * (c + 1))
                for m in range(2):
                    bank = turn("zz", c, m)
                    for t in range(4):
                        i = tr(bank[:, t * P:(t + 1) * P], at(Y + t * DI + (2 * c + m) * P, [(1, P)]), ident)
                    filled(i)
                bank = turn("zz", c, 2)
                for m in range(2):
                    i = tr(bank[:, m * P:(m + 1) * P], at(Y + 4 * DI + (2 * c + m) * P, [(1, P)]), ident)
                filled(i)
            gate_rows(1)
            for c in range(8):
                ci = chunk["ssd_z"] + c
                ring_wait(ci)
                for t in range(TT):
                    bank = turn("z", c, t)
                    for k in range(KT):
                        i = mm(bank[:, 0:256], at(HT + k * NT + t * P, [(1, P)]), at(ring(ci % NSLOT) + k * 256, [(1, 256)]),
                               start=k == 0, stop=k == KT - 1)
                    filled(i)
                pe.wait_ge(S("bank_filled"), len(turn_of))
                pe.sem_inc(S("ring_used"), 1)
                if c:
                    z_transposed(c - 1)
            z_transposed(7)
            pe.wait_ge(S("zt_ready"), 8)
            out_projection(1, "ssd_out", lambda k: ZT + k * NT)

        @block.scalar
        def _(act):
            A = nc.scalar.activation
            chain = [0]

            def link(ins):
                chain[0] += 1
                ins.then_inc(S("act_chain"), 1)
                act.wait_ge(S("act_chain"), chain[0])

            def bank_of(*name):
                t = turn_of[name]
                act.wait_ge(S("bank_filled"), t + 1)
                return bank_ap(slot_of[name]), S(f"bank_read{slot_of[name]}")

            def tile_of(name, o):
                g = gemm_of[name, o]
                act.wait_ge(S("gemm_filled"), g + 1)
                return GP[:, g % 2, 0:NT], S(f"gemm_read{g % 2}")

            def norm_stat(layer, t, xbuf):
                link(A(at(SQ7 if layer else SQ, [(1, D)]), at(xbuf + t * D, [(1, D)]), ACT.Square, accum_out=at(STAT + t, [(1, 1)])))
                A(at(STAT + 8 + t, [(1, 1)]), at(STAT + t, [(1, 1)]), ACT.Sqrt, bias=at(EPSB, [(1, 1)]),
                  scale=1.0 / D).then_inc(S("rms_ready"), 1)

            def mod_row_copy(name, b, dst):
                bank, read = bank_of(name, "rows", b)
                A(at(dst, [(1, 512)], 0, 2), bank[0:2, :], ACT.Copy).then_inc(read, 1)
                act.drain().then_inc(S("mod_rows"), 1)

            def modulated(layer):
                for t in range(TT):
                    which = 0 if t < 4 else 1
                    for half in range(1):
                        bank, read = bank_of("xt", layer, t, half)
                        if t == 0 and half == 0:
                            act.wait_ge(S("mod_ready"), layer + 1)
                        for j in range(4):
                            kd = half * 4 + j
                            i = A(at(HT + kd * NT + t * P, [(1, P)]), bank[:, j * P:(j + 1) * P], ACT.Identity,
                                  scale=at(AB + kd * 2 + which, [(1, 1)]), bias=at(MV + layer * 48 + kd * 2 + which, [(1, 1)]))
                        i.then_inc(read, 1)

            def rows(tile, row0, src, sem="rows_loaded"):
                act.dma_start(at(VR + tile * P, [(1, P)], row0, src.shape[0]), src).then_inc(S(sem), 16)
            r = lambda ap, pat, **k: ap.rearrange(pat, **k)
            rows(0, 0, r(a["c"], "a (k p) -> (a k) p", p=P), "cond_rows")
            rows(0, 8, r(a["c_ctx"], "(k p) -> k p", p=P), "cond_rows")
            rows(0, 16, r(a["norm_w"], "l (k p) -> (l k) p", p=P))
            rows(0, 32, r(a["mod_b"], "l (k p) -> (l k) p", p=P))
            rows(1, 0, r(a["s5_glu_b"], "a (k p) -> (a k) p", p=P))
            rows(1, 8, r(a["s5_d"], "a (k p) -> (a k) p", p=P))
            rows(1, 16, r(a["hy_short_b"], "a (k p) -> (a k) p", p=P))
            for tap in range(3):
                rows(1, 40 + 24 * tap, r(a["hy_short_w"][0, tap], "(k p) -> k p", p=P))
            rows(2, 0, r(a["ssd_conv_b"], "a (k p) -> (a k) p", p=P))
            for tap in range(3):
                rows(2, 24 + 24 * tap, r(a["ssd_conv_w"][0, tap], "(k p) -> k p", p=P))
            rows(2, 96, r(a["ssd_norm_w"], "a (k p) -> (a k) p", p=P))
            for i, nm in enumerate(("s5_a_re", "s5_a_im")):
                act.dma_start(at(SV5 + i * P, [(1, P)], 0, 64), r(a[nm], "a d (q e) p -> (a d q) (e p)", e=2)).then_inc(S("s5_loaded"), 16)
            for i, nm in enumerate(("state_s5_re", "state_s5_im")):
                act.dma_start(at(SV5 + (2 + i) * P, [(1, P)], 0, 64),
                              r(a[nm], "b a d (q e) p -> (b a d q) (e p)", e=2)).then_inc(S("s5_loaded"), 16)
            act.dma_start(at(TMP5, [(1, 2)], 0, 64), r(a["s5_log_dt"], "a d (q e) -> (a d q) e", e=2)).then_inc(S("s5_loaded"), 16)
            act.dma_start(at(TAB, [(1, T_END - T_TN)]), a["tables"][:, T_TN:T_END]).then_inc(S("tab_loaded"), 16)
            for i, nm in enumerate(("s5_b_re", "s5_b_im")):
                act.dma_start(at(BRAW + i * 1024, [(16, 64), (1, 16)]),
                              r(a[nm], "a d (q e) p h -> (e p) (a d q) h", e=2)).then_inc(S("b_loaded"), 16)

            bank, read = bank_of("cond")
            A(at(SC, [(1, 2), (2, 8)]), bank[:, 0:16].rearrange("p (w k) -> p w k", w=2), ACT.Silu).then_inc(read, 1)
            act.drain().then_inc(S("cond_ready"), 1)
            bank, read = bank_of("vec")
            A(at(VC, [(1, 3 * P)])[:, 0:80], bank[:, 0:80], ACT.Copy)
            A(at(VC + P, [(1, 112)]), bank[:, P:P + 112], ACT.Copy)
            A(at(VC + 2 * P, [(1, 112)]), bank[:, 2 * P:2 * P + 112], ACT.Copy).then_inc(read, 1)
            act.drain().then_inc(S("cols_ready"), 1)
            bank, read = bank_of("s5v")
            A(at(SVC, [(1, 256)]), bank[:, 0:256], ACT.Copy)
            A(at(SVC + 256, [(1, 64)]), bank[:, 256:320], ACT.Exp).then_inc(read, 1)
            act.drain().then_inc(S("svc_ready"), 1)
            act.wait_ge(S("s5_arg"), 1)
            A(at(TMP5 + 64 * 1, [(1, 64)]), at(TMP5, [(1, 64)]), ACT.Exp)
            A(at(TMP5 + 64 * 3, [(1, 128)]), at(TMP5 + 64 * 5, [(1, 128)]), ACT.Sin).then_inc(S("s5_fun"), 1)
            for b in range(2):
                mod_row_copy("mod0", b, MROW + b * 512)
            for t in range(TT):
                act.wait_ge(S(f"x_loaded{t}"), 16)
                if t == 0:
                    act.wait_ge(S("eps_ready"), 1)
                norm_stat(0, t, X1)
            for b in range(2, 4):
                mod_row_copy("mod0", b, MROW + b * 512)
            modulated(0)
            barrier(act, 1)

            def u_copy(o):
                tile, read = tile_of("u", o)
                if o >= 2:
                    act.wait_ge(S("bank_filled"), turn_of["ma", o - 2, 1] + 1)
                A(at(UT + (o % 2) * NT, [(1, NT)]), tile, ACT.Copy).then_inc(read, 1)
                act.drain().then_inc(S("ut_ready"), 1)

            def octet(o):
                for dc in range(4):
                    bank, read = bank_of("bt", o, dc)
                    if o >= 1:
                        act.wait_ge(S("bank_filled"), turn_of["s", o - 1, dc] + 1)
                    A(at(BL + dc * 512, [(1, 512)]), bank, ACT.Copy).then_inc(read, 1)
                    act.drain().then_inc(S("bl_ready"), 1)
                for half in range(2):
                    bank, read = bank_of("ub", o, half)
                    src = bank[:, 0:320].rearrange("p (g x) -> p g x", g=4)
                    dst = U + (8 * o + 4 * half) * XC
                    A(at(dst, [(XC, 4), (1, LATX)]), src[:, :, 0:LATX], ACT.Copy)
                    A(at(dst + GAP + 1, [(XC, 4), (1, CTXX)]), src[:, :, LATX:80], ACT.Copy).then_inc(read, 1)
                    act.drain().then_inc(S("u_ready"), 1)
                for c in range(2):
                    bank, read = bank_of("s", o, c)
                    A(at(HS + SLOTW + c * NPAIR + 4 * o, [(1, 4), (SLOTW, XC)]),
                      bank[:, 0:4 * XC].rearrange("p (q x) -> p q x", q=4), ACT.Copy).then_inc(read, 1)

            u_copy(0)
            for o in range(OCT):
                if o + 1 < OCT:
                    u_copy(o + 1)
                octet(o)
            act.drain().then_inc(S("hs_forward"), 1)
            for o in range(OCT):
                tile, read = tile_of("gb", o)
                A(at(GB + o * NT, [(1, NT)]), tile, ACT.Silu).then_inc(read, 1)
            for o in range(OCT):
                tile, read = tile_of("x2", o)
                if o >= 2:
                    act.wait_ge(S("x2_used"), o - 1)
                for tap, dst in ((1, CVX + (o % 2) * NT), (0, TLX + (o % 2) * 2 * NT), (2, TLX + (o % 2) * 2 * NT + NT)):
                    i = A(at(dst, [(1, NT)]), tile, ACT.Identity, scale=vcol(1, 40 + 24 * tap + 16 + o),
                          bias=vcol(1, 16 + 16 + o) if tap == 1 else 0.0)
                i.then_inc(read, 1)
                act.drain().then_inc(S("x2_ready"), 1)
            barrier(act, 2)

            def conv_center(name, o, part, n):
                tile, _ = tile_of(name, o)
                if n >= 2:
                    act.wait_ge(S("cv_free"), n - 1)
                A(at(CV + (n % 2) * NT, [(1, NT)]), tile, ACT.Identity, scale=vcol(1, 40 + 24 + 8 * part + o),
                  bias=vcol(1, 16 + 8 * part + o)).then_inc(S("cv_center"), 1)

            def c_copies(o):
                bank, read = bank_of("ct", o)
                if o >= 1:
                    act.wait_ge(S("ce_ready"), o)
                src = bank[:, 0:256].rearrange("p (d c h) -> p d c h", d=2, c=2)
                A(at(CT, [(64, 2), (1, 64)]), src[:, :, 0, :], ACT.Copy)
                A(at(CT + 128, [(64, 2), (1, 64)]), src[:, :, 1, :], ACT.Copy, scale=-1.0)
                A(at(CT + 256, [(64, 2), (1, 64)]), src[:, :, 0, :], ACT.Copy, scale=-1.0).then_inc(read, 1)
                act.drain().then_inc(S("ct_ready"), 1)
            c_copies(0)
            bank, read = bank_of("fs")
            A(at(FO, [(1, 256)], 0, 64), bank[0:64, 0:256], ACT.Copy).then_inc(read, 1)
            act.drain().then_inc(S("fo_ready"), 1)
            for o in range(OCT + 2):
                if o + 1 < OCT:
                    c_copies(o + 1)
                if o >= 2:
                    for half in range(2):
                        bank, read = bank_of("yc", o - 2, half)
                        src = bank[:, 0:4 * XC].rearrange("p (t x) -> p t x", t=4)
                        dst = YT + (o - 2) * YW + 4 * half
                        A(at(dst, [(1, 4), (Q8, LATX)]), src[:, :, 0:LATX], ACT.Gelu_apprx_tanh)
                        A(at(dst + NLAT, [(1, 4), (Q8, CTXX)]), src[:, :, GAP + 1:XC], ACT.Gelu_apprx_tanh).then_inc(read, 1)
                if 1 <= o <= OCT:
                    for half in range(2):
                        bank, read = bank_of("y", o - 1, half)
                        if o >= 2 and half == 0:
                            act.wait_ge(S("bank_filled"), turn_of["yt", o - 2, 1] + 1)
                        A(at(YS + half * 4 * XC, [(1, 4 * XC)]), bank[:, 0:4 * XC], ACT.Copy).then_inc(read, 1)
                        act.drain().then_inc(S("ys_ready"), 1)
            barrier(act, 3)

            for ch in range(4):
                for m in range(2):
                    o = 2 * ch + m
                    tile, read = tile_of("ga", o)
                    if ch:
                        act.wait_ge(S("za_done"), o - 1)
                    A(at(TA + m * NT, [(1, NT)]), tile, ACT.Silu).then_inc(read, 1)
                for m in range(2):
                    o = 2 * ch + m
                    tile, read = tile_of("glu", o)
                    A(at(TG + m * NT, [(1, NT)]), tile, ACT.Sigmoid, bias=vcol(1, o)).then_inc(read, 1)
                    act.drain().then_inc(S("glu_ready"), 1)
            barrier(act, 4)

            def sine(n, dst, rows):
                act.wait_ge(S("sin_arg"), n)
                A(at(dst, [(1, NT)], 0, rows), at(FA, [(1, NT)], 0, rows), ACT.Sin)
                act.drain().then_inc(S("sin_done"), 1)
            n = 0
            sine(1, EMB + 640, 64)
            for name, part, dst in (("v", 0, VS), ("x1", 1, XS)):
                for o in range(OCT + 1):
                    if o < OCT:
                        conv_center(name, o, part, n)
                        n += 1
                    if name == "v" and o == 0:
                        sine(2, FE, P)
                    if o >= 1:
                        bank, read = bank_of(name + "t", o - 1, 0)
                        A(at(dst + (o - 1) * P, [(H1, 4), (1, P)]), bank.rearrange("p (a b) -> p a b", a=4), ACT.Copy).then_inc(read, 1)
                        bank, read = bank_of(name + "t", o - 1, 1)
                        A(at(dst + 4 * H1 + (o - 1) * P, [(1, P)]), bank[:, 0:P], ACT.Copy).then_inc(read, 1)
            barrier(act, 5)

            act.wait_ge(S("deltas_loaded"), 16)

            def windows(w):
                for n in range(5):
                    A(at(WIN + n * HW, [(1, HW)]), at(DEL + w * HW, [(1, HW)]), ACT.Exp, scale=at(TAB + n, [(1, 1)]))
                act.drain().then_inc(S("win_ready"), 1)

            def kh_copies(i):
                for kind in range(2):
                    for ft in range(2):
                        bank, _ = bank_of("kh", i, kind, ft)
                        n = 4 * i + 2 * kind + ft
                        if n >= 2:
                            act.wait_ge(S("kh_done"), n - 1)
                        A(at(HTMP + (n % 2) * HW, [(1, HW)]), bank[:, HW:2 * HW], ACT.Copy).then_inc(S("kh_odd"), 1)
                bank, read = bank_of("khc", i)
                if i:
                    act.wait_ge(S("pr_ready"), i)
                A(at(KH + 4 * HW, [(5 * HW, 2), (1, HW)]), bank.rearrange("p (a b) -> p a b", a=2), ACT.Copy).then_inc(read, 1)
                act.drain().then_inc(S("khc_ready"), 1)

            def vf_copies(i):
                if i:
                    act.wait_ge(S("pr_ready"), i)
                for ft in range(5):
                    bank, read = bank_of("vf", i, ft)
                    A(at(FQ + ft * HW, [(5 * HW, 2), (1, HW)]), bank.rearrange("p (a b) -> p a b", a=2), ACT.Copy).then_inc(read, 1)
                act.drain().then_inc(S("fq_ready"), 1)

            def yi_copies(i):
                for tt in range(2):
                    bank, _ = bank_of("yi", i, tt)
                    n = 2 * i + tt
                    if n >= 2:
                        act.wait_ge(S("yi_done"), n - 1)
                    A(at(MTMP + (n % 2) * HW, [(1, HW)]), bank[:, HW:2 * HW], ACT.Copy).then_inc(S("yi_odd"), 1)
            windows(0)
            kh_copies(0)
            vf_copies(0)
            act.wait_ge(S("taps_ready"), 1)
            windows(ITEMS[1][0])
            for i in range(2 * NW):
                if i + 2 < 2 * NW:
                    act.wait_ge(S("taps_ready"), i + 2)
                    windows(ITEMS[i + 2][0])
                if i + 1 < 2 * NW:
                    kh_copies(i + 1)
                    vf_copies(i + 1)
                mod_row_copy("mod1", i, ring((chunk["mod1"] + 2 * i) % NSLOT))
                yi_copies(i)
            barrier(act, 6)

            def gate_copies(layer):
                for w in range(2):
                    for half in range(2):
                        bank, read = bank_of("gr", layer, w, half)
                        A(at((GR9 if layer else GR) + w * D + half * 512, [(1, 512)]), bank, ACT.Copy).then_inc(read, 1)
                act.drain().then_inc(S("gr_ready"), 1)
            gate_copies(0)
            for t in range(TT):
                act.wait_ge(S("res_ready"), t + 1)
                norm_stat(1, t, XRES)
            modulated(1)
            barrier(act, 7)

            act.wait_ge(S("ssd_rows"), 48)
            A(at(AROW, [(1, 64)]), at(AROW, [(1, 64)]), ACT.Exp).then_inc(S("arow_ready"), 1)
            act.wait_ge(S("sp_arg"), 1)
            A(at(SPT + CW, [(1, CW)]), at(SPT + CW, [(1, CW)]), ACT.Exp).then_inc(S("sp_exp"), 1)
            def ssd_tile(n):
                g, j = n // 6, n % 6
                if j < 2:
                    return 16 + 4 * j + g, BC + (g % 2) * 2 * NT + j * NT
                return 4 * g + j - 2, XCH + (j - 2) * NT

            def center(n):
                tile, _ = tile_of("ssd_g", n)
                o, dst = ssd_tile(n)
                A(at(dst, [(1, NT)]), tile, ACT.Identity, scale=vcol(2, 24 + 24 + o), bias=vcol(2, o)).then_inc(S("cv_center8"), 1)

            def silu(n):
                act.wait_ge(S("cv_sides"), n + 1)
                o, dst = ssd_tile(n)
                A(at(dst, [(1, NT)]), at(dst, [(1, NT)]), ACT.Silu).then_inc(S("cv_ready"), 1)

            def decays(g, t):
                n = TT * g + t
                if n >= 2:
                    act.wait_ge(S("bank_filled"), turn_of["yd", (n - 2) // TT, (n - 2) % TT] + 1)
                for half in range(2):
                    bank, read = bank_of("ar", g, t, half)
                    A(at(EX + n % 2 * 1024 + half * 512, [(1, 512)]), bank, ACT.Exp).then_inc(read, 1)
                act.drain().then_inc(S("ex_ready"), 1)

            center(0)
            for n in range(6):
                if n + 1 < 6:
                    center(n + 1)
                silu(n)
            for nm, dst in (("ce", EE), ("cw", WW), ("ctot", TOT)):
                bank, read = bank_of(nm)
                A(at(dst, [(1, CW)]), bank[:, 0:CW], ACT.Exp).then_inc(read, 1)
            act.drain().then_inc(S("coef_exp"), 1)
            for g in range(SG):
                for part in range(2):
                    bank, read = bank_of("bg", g, part)
                    w = (512, P)[part]
                    A(at(BTOK + part * 512, [(1, w)]), bank[:, 0:w], ACT.Copy).then_inc(read, 1)
                act.drain().then_inc(S("btok_ready"), 1)
                for d in range(2):
                    bank, read = bank_of("in", g, d)
                    A(at(HP + (0, 7)[d] * 512, [(1, 512)]), bank, ACT.Copy).then_inc(read, 1)
                act.drain().then_inc(S("init_ready"), 1)
                if g:
                    act.wait_ge(S("yx_ready"), TT * g)
                for t in range(TT):
                    bank, read = bank_of("xg", g, t)
                    A(at(XT + t * 512, [(1, 512)]), bank, ACT.Copy).then_inc(read, 1)
                act.drain().then_inc(S("xt_ready"), 1)
                decays(g, 0)
                for d in range(2):
                    bank, read = bank_of("st", g, d)
                    if g:
                        act.wait_ge(S("ssd_state_out"), 32 * g)
                    A(at(FOUT + d * 512, [(1, 512)]), bank, ACT.Copy).then_inc(read, 1)
                act.drain().then_inc(S("fout_ready"), 1)
                for t in range(TT):
                    for n in next_tiles(g, t):
                        center(n)
                        silu(n)
                    if t + 1 < TT:
                        decays(g, t + 1)
            barrier(act, 8)

            def z_copies(c):
                for m in range(2):
                    bank, read = bank_of("zz", c, m)
                    A(at(ZT + (2 * c + m) * NT, [(1, 512)]), bank, ACT.Identity, scale=vcol(2, 96 + 2 * c + m)).then_inc(read, 1)
                bank, read = bank_of("zz", c, 2)
                for m in range(2):
                    i = A(at(ZT + (2 * c + m) * NT + 512, [(1, P)]), bank[:, m * P:(m + 1) * P], ACT.Identity, scale=vcol(2, 96 + 2 * c + m))
                i.then_inc(read, 1)
                act.drain().then_inc(S("zt_ready"), 1)

            def z_squares(c):
                for t in range(TT):
                    act.wait_ge(S("yz_ready"), TT * c + t + 1)
                    link(A(at(SQZ, [(1, 256)]), at(Y + t * DI + c * 256, [(1, 256)]), ACT.Square, accum_out=at(SUMS + t * 8 + c, [(1, 1)])))
            gate_copies(1)
            for c in range(8):
                for t in range(TT):
                    n = TT * c + t
                    bank, read = bank_of("z", c, t)
                    if n >= 4:
                        act.wait_ge(S("yz_ready"), n - 3)
                    A(at(SZ + (n % 4) * 256, [(1, 256)]), bank[:, 0:256], ACT.Silu).then_inc(read, 1)
                    act.drain().then_inc(S("sz_ready"), 1)
                if c:
                    z_squares(c - 1)
                    z_copies(c - 1)
            z_squares(7)
            act.drain().then_inc(S("sums_ready"), 1)
            z_copies(7)
            act.wait_ge(S("sums_added"), 1)
            A(at(STAT + 24, [(1, TT)]), at(STAT + 24, [(1, TT)]), ACT.Sqrt, bias=at(EPSB, [(1, 1)]), scale=1.0 / DI).then_inc(S("zrms_ready"), 1)
            for t in range(TT):
                act.wait_ge(S("res_ready"), TT + t + 1)
                link(A(at(SQ9, [(1, D)]), at(XRES9 + t * D, [(1, D)]), ACT.Square, accum_out=at(STAT + t, [(1, 1)])))
                A(at(STAT + 8 + t, [(1, 1)]), at(STAT + t, [(1, 1)]), ACT.Sqrt, bias=at(EPSB, [(1, 1)]), scale=1.0 / D).then_inc(S("rms_ready"), 1)

        @block.vector
        def _(dve):
            V = nc.vector
            chain = [0]

            def link(ins):
                chain[0] += 1
                ins.then_inc(S("dve_chain"), 1)
                dve.wait_ge(S("dve_chain"), chain[0])

            def settle():
                link(dve.drain())

            def bank_of(*name):
                t = turn_of[name]
                dve.wait_ge(S("bank_filled"), t + 1)
                return bank_ap(slot_of[name]), S(f"bank_read{slot_of[name]}")

            def tile_of(name, o):
                g = gemm_of[name, o]
                dve.wait_ge(S("gemm_filled"), g + 1)
                return GP[:, g % 2, 0:NT], S(f"gemm_read{g % 2}")

            def mul(o, x, y):
                return V.tensor_tensor(o, x, y, ALU.mult)

            def add(o, x, y):
                return V.tensor_tensor(o, x, y, ALU.add)

            def sub(o, x, y):
                return V.tensor_tensor(o, x, y, ALU.subtract)

            V.memset(at(EPSB, [(1, 2)]), EPS).then_inc(S("eps_ready"), 1)
            dve.wait_ge(S("s5_loaded"), 16 * 5)
            V.tensor_copy(at(SV5 + 4 * P, [(SP, 2), (1, SP)], 0, 64),
                          at(TMP5, [(1, 2)], 0, 64).unsqueeze(2).broadcast_to([64, 2, SP])).then_inc(S("s5rows"), 1)

            def f5(i, n=1):
                return at(TMP5 + 64 * i, [(1, 64 * n)])

            def sv(i):
                return at(SVC + 64 * i, [(1, 64)])
            dve.wait_ge(S("svc_ready"), 1)
            dve.wait_ge(S("s5rows"), 1)
            mul(f5(0), sv(0), sv(4))
            link(mul(f5(2), sv(1), sv(4)))

            def reduce_angle(x, k, n=64):
                link(V.tensor_scalar(k, x, 1.0 / TWO_PI, MAGIC, ALU.mult, ALU.add))
                link(V.tensor_scalar(k, k, MAGIC, None, ALU.subtract))
                for cst in (C1, C2, C3):
                    link(V.scalar_tensor_tensor(out=x, in0=k, scalar=-cst, in1=x, op0=ALU.mult, op1=ALU.add))
                link(V.tensor_scalar(x, x, 3.1415925, -3.1415925, ALU.min, ALU.max))
            reduce_angle(f5(2), f5(7))
            V.tensor_copy(f5(5), f5(2))
            link(V.scalar_tensor_tensor(out=f5(6), in0=f5(2), scalar=-1.0, in1=f5(2), op0=ALU.mult, op1=ALU.max))
            V.tensor_scalar(f5(6), f5(6), -1.0, math.pi / 2, ALU.mult, ALU.add).then_inc(S("s5_arg"), 1)

            def mod_part(name, b, m):
                bank, read = bank_of(name, "columns", b)
                V.tensor_tensor(at(MV + 2 * m, [(2, 4), (1, 2)]), bank[:, 0:8].rearrange("p (m w) -> p m w", w=2),
                                at(VC + 32 + m, [(1, 4)]).unsqueeze(2).broadcast_to([P, 4, 2]), ALU.add).then_inc(read, 1)

            def mod_finish(layer):
                mv = MV + layer * 48
                for b in range(4):
                    mod_part("mod0", b, 4 * b)
                settle()
                link(V.tensor_scalar(at(AB, [(1, 16)]), at(mv + 16, [(1, 16)]), 1.0, None, ALU.add))
                mul(at(AB, [(2, 8), (1, 2)]), at(AB, [(2, 8), (1, 2)]),
                    at(VC + 16 + 8 * layer, [(1, 8)]).unsqueeze(2).broadcast_to([P, 8, 2])).then_inc(S("mod_ready"), 1)

            def modulated(layer, t):
                which = 0 if t < 4 else 1
                bank, read = bank_of("xt", layer, t, 1)
                for j in range(4):
                    kd = 4 + j
                    i = V.tensor_scalar(at(HT + kd * NT + t * P, [(1, P)]), bank[:, j * P:(j + 1) * P], at(AB + kd * 2 + which, [(1, 1)]),
                                        at(MV + layer * 48 + kd * 2 + which, [(1, 1)]), ALU.mult, ALU.add)
                i.then_inc(read, 1)

            def normed(layer, t, xbuf):
                dve.wait_ge(S("rms_ready"), layer * TT + t + 1)
                link(V.reciprocal(at(STAT + 16 + t, [(1, 1)]), at(STAT + 8 + t, [(1, 1)])))
                if t >= 2:
                    dve.wait_ge(S("bank_filled"), turn_of["xt", layer, t - 2, 1] + 1)
                V.tensor_scalar(at((XN7 if layer else XN) + (t % 2) * D, [(1, D)]), at(xbuf + t * D, [(1, D)]), at(STAT + 16 + t, [(1, 1)]),
                                None, ALU.mult).then_inc(S("xn_ready"), 1)

            dve.wait_ge(S("s5_fun"), 1)
            lr, li = at(PW + 64, [(1, 64)]), at(PW + 9 * 64 + 64, [(1, 64)])
            mul(lr, f5(1), f5(4))
            mul(li, f5(1), f5(3))
            V.memset(at(PW, [(1, 64)]), 1.0)
            link(V.memset(at(PW + 9 * 64, [(1, 64)]), 0.0))
            link(V.tensor_scalar(f5(7), lr, -1.0, None, ALU.add))
            mul(f5(8), f5(7), sv(0))
            mul(f5(9), li, sv(1))
            mul(f5(10), li, sv(0))
            mul(f5(11), f5(7), sv(1))
            mul(f5(12), sv(0), sv(0))
            link(mul(f5(13), sv(1), sv(1)))
            add(f5(8), f5(8), f5(9))
            sub(f5(10), f5(10), f5(11))
            link(add(f5(12), f5(12), f5(13)))
            link(V.reciprocal(f5(12), f5(12)))
            mul(f5(8), f5(8), f5(12))
            link(mul(f5(9), f5(10), f5(12)))

            def power(dst, src, n, e):
                def pw(c, k, m):
                    return at(PW + c * 576 + k * 64, [(64, m), (1, 64)])

                def pe_(c):
                    return at(PW + c * 576 + e * 64, [(0, n), (1, 64)])
                t = [at(TMPB + 256 * j, [(64, n), (1, 64)]) for j in range(4)]
                mul(t[0], pw(0, src, n), pe_(0))
                mul(t[1], pw(1, src, n), pe_(1))
                mul(t[2], pw(0, src, n), pe_(1))
                link(mul(t[3], pw(1, src, n), pe_(0)))
                sub(pw(0, dst, n), t[0], t[1])
                link(add(pw(1, dst, n), t[2], t[3]))
            power(2, 1, 1, 1)
            power(3, 1, 2, 2)
            power(5, 1, 4, 4)
            for c in range(2):
                V.tensor_copy(at(PC + c * 576, [(9, 32), (1, 9)]), at(PW + c * 576, [(1, 32), (64, 9)]))
                V.tensor_copy(at(PC + c * 576 + 288, [(9, 32), (1, 9)]), at(PW + c * 576 + 8 * 64 + 32, [(1, 32), (-64, 9)]))
            for d in range(2):
                for c in range(2):
                    V.tensor_copy(at(SCA + d * 64 + c * 32, [(1, 32)]), at(PW + 8 * 64 + d * 32, [(1, 32)]))
                    V.tensor_scalar(at(SCA + 128 + d * 64 + c * 32, [(1, 32)]), at(PW + 576 + 8 * 64 + d * 32, [(1, 32)]),
                                    1.0 if c else -1.0, None, ALU.mult)
            dve.wait_ge(S("b_loaded"), 32)

            def hb(x):
                return x.unsqueeze(2).broadcast_to([P, 64, GS])

            def braw(c):
                return at(BRAW + c * 1024, [(16, 64), (1, 16)])

            def bbar(c):
                return at(BBAR + c * 1024, [(16, 64), (1, 16)])
            t0, t1 = (at(TMPB + 1024 * j, [(16, 64), (1, 16)]) for j in range(2))
            mul(t0, braw(0), hb(f5(8)))
            link(mul(t1, braw(1), hb(f5(9))))
            link(sub(bbar(0), t0, t1))
            mul(t0, braw(0), hb(f5(9)))
            link(mul(t1, braw(1), hb(f5(8))))
            link(add(bbar(1), t0, t1))
            for t in range(2):
                normed(0, t, X1)
            mod_finish(0)
            settle()
            for t in range(2, TT + 2):
                modulated(0, t - 2)
                if t < TT:
                    normed(0, t, X1)
            barrier(dve, 1)

            def input_matrices(o):
                if o >= 2:
                    dve.wait_ge(S("bank_filled"), turn_of["bt", o - 2, 3] + 1)
                for d in range(2):
                    def pc(c):
                        return at(PC + c * 576 + d * 288 + 4 * o * 9 + d, [(9, 4), (1, 8), (0, GS)])

                    def bb_(c):
                        return at(BBAR + c * 1024 + (d * 32 + 4 * o) * GS, [(GS, 4), (0, 8), (1, GS)])

                    def big(c):
                        return at(BB + (o % 2) * 2048 + (2 * d + c) * 512, [(128, 4), (16, 8), (1, 16)])
                    t0, t1 = (at(TB + 512 * j, [(128, 4), (16, 8), (1, 16)]) for j in range(2))
                    mul(t0, pc(0), bb_(0))
                    link(mul(t1, pc(1), bb_(1)))
                    link(sub(big(0), t0, t1))
                    mul(t0, pc(0), bb_(1))
                    link(mul(t1, pc(1), bb_(0)))
                    i = add(big(1), t0, t1)
                    if d:
                        i.then_inc(S("bb_ready"), 1)
                        dve.wait_ge(S("bb_ready"), o + 1)
                    else:
                        link(i)

            def chunk_copies(o):
                for half in range(2):
                    bank, read = bank_of("ma", o, half)
                    if o >= 2:
                        dve.wait_ge(S("bank_filled"), turn_of["ub", o - 2, 1] + 1)
                    V.tensor_copy(at(MT + (o % 2) * 1024 + (7 - 4 * half) * 16, [(-16, 4), (P, 8), (1, 16)], 0, 80),
                                  bank[0:80, :].rearrange("p (t g h) -> p t g h", t=4, h=16)).then_inc(read, 1)
                    dve.drain().then_inc(S("mt_ready"), 1)

            def backward_inputs(o):
                for c in range(2):
                    bank, read = bank_of("s", o, 2 + c)
                    V.tensor_copy(at(HS + (XC) * SLOTW + 64 + c * NPAIR + 4 * o, [(1, 4), (-SLOTW, XC)]),
                                  bank[:, 0:4 * XC].rearrange("p (q x) -> p q x", q=4)).then_inc(read, 1)

            input_matrices(0)
            for o in range(OCT):
                if o + 1 < OCT:
                    input_matrices(o + 1)
                chunk_copies(o)
                backward_inputs(o)
            dve.wait_ge(S("hs_forward"), 1)
            settle()
            for d, slot in ((0, 0), (1, CTXX + 1)):
                for c in range(2):
                    V.tensor_copy(at(HS + slot * SLOTW + d * 64 + c * 32, [(1, 32)]), at(SVC + 64 * (2 + c) + d * 32, [(1, 32)]))
            V.memset(at(HS + 64, [(1, 64)]), 0.0)
            for j, c, src in ((0, 0, 0), (0, 1, 128), (1, 0, 160), (1, 1, 32)):
                V.tensor_copy(at(SCB + 64 * j + 32 * c, [(128, 2), (1, 32)]), at(SCA + src, [(64, 2), (1, 32)]))
            settle()
            dve.drain().then_inc(S("scan_start"), 1)
            dstep = (CTXX + 1) * SLOTW + 64
            with dve.Fori(0, LATX - 1) as s:
                mul(at(SCP, [(128, 2), (64, 2), (1, 64)]), at(HS + s * SLOTW, [(dstep, 2), (0, 2), (1, 64)]),
                    at(SCB, [(128, 2), (64, 2), (1, 64)])).then_inc(S("scan_lat"), 1)
                dve.wait_ge(S("scan_lat"), s * 3 + 1)
                add(at(SCT, [(32, 4), (1, 32)]), at(SCP, [(64, 4), (1, 32)]), at(SCP + 32, [(64, 4), (1, 32)])).then_inc(S("scan_lat"), 1)
                hn = at(HS + SLOTW + s * SLOTW, [(dstep, 2), (1, 64)])
                dve.wait_ge(S("scan_lat"), s * 3 + 2)
                add(hn, hn, at(SCT, [(64, 2), (1, 64)])).then_inc(S("scan_lat"), 1)
                dve.wait_ge(S("scan_lat"), s * 3 + 3)
            barrier(dve, 2)

            for c in range(2):
                V.tensor_copy(at(FS + c * 64, [(1, 32)]), at(HS + (SLOTS - 1) * SLOTW + c * 32, [(1, 32)]))
                V.tensor_copy(at(FS + c * 64 + 32, [(1, 32)]), at(HS + CTXX * SLOTW + 64 + c * 32, [(1, 32)]))
            dve.drain().then_inc(S("fs_ready"), 1)
            link(V.memset(at(BBD, [(1, 512)]), 0.0))
            def conv_sides(name, o, part, n):
                dve.wait_ge(S("cv_center"), n + 1)
                tile, read = tile_of(name, o)
                cv = CV + (n % 2) * NT
                for base, m in ((0, NLAT), (NLAT, NCTX)):
                    V.scalar_tensor_tensor(out=at(cv + base + 1, [(1, m - 1)]), in0=tile[:, base:base + m - 1],
                                           scalar=vcol(1, 40 + 8 * part + o), in1=at(cv + base + 1, [(1, m - 1)]),
                                           op0=ALU.mult, op1=ALU.add)
                settle()
                for base, m in ((0, NLAT), (NLAT, NCTX)):
                    i = V.scalar_tensor_tensor(out=at(cv + base, [(1, m - 1)]), in0=tile[:, base + 1:base + m],
                                               scalar=vcol(1, 40 + 48 + 8 * part + o), in1=at(cv + base, [(1, m - 1)]),
                                               op0=ALU.mult, op1=ALU.add)
                i.then_inc(read, 1)
                settle()
                return cv

            def output_matrices(o):
                dve.wait_ge(S("ct_ready"), o + 1)
                if o == 2:
                    dve.wait_ge(S("s5_state_out"), 32)
                if o >= 3:
                    dve.wait_ge(S("bank_filled"), turn_of["y", o - 3, 1] + 1)
                for d in range(2):
                    def pc(c):
                        return at(PC + c * 576 + d * 288 + 4 * o * 9, [(9, 4), (1, 9), (0, GS)])

                    def ct(kind):
                        return at(CT + kind * 128 + d * 64, [(GS, 4), (0, 9), (1, GS)])

                    def big(c):
                        return at(CE + (o % 3) * 2304 + (2 * d + c) * 576, [(144, 4), (16, 9), (1, 16)])
                    other = at(TC, [(144, 4), (16, 9), (1, 16)])
                    for c in range(2):
                        mul(big(c), pc(0), ct(c))
                        link(mul(other, pc(1), ct(1 + c)))
                        link(add(big(c), big(c), other))
                for e in range(2):
                    V.tensor_copy(at(BBD + 16 * e, [(256, 2), (128, 2), (32, 4), (1, GS)], 64 * e, 64)[:, 0],
                                  at(BBAR + 4 * o * GS, [(512, 2), (1024, 2), (GS, 4), (1, GS)], 64 * e, 64)[:, 0])
                    V.tensor_copy(at(BBD + 16 * e, [(256, 2), (128, 2), (32, 4), (1, GS)], 64 * e, 64)[:, 1],
                                  at(BBAR + 4 * o * GS, [(512, 2), (1024, 2), (GS, 4), (1, GS)], 64 * e, 64)[:, 1])
                dve.drain().then_inc(S("ce_ready"), 1)

            def lag_strip(o):
                bank, read = bank_of("k", o)
                ws = WS[o % 2]
                if o >= 2:
                    dve.wait_ge(S(f"strip_out{o % 2}"), 16 * (o // 2))
                V.tensor_copy(at(ws + 112, [(1, P)]), bank[:, 0:P])
                V.tensor_copy(at(ws, [(1, 112)]), bank[:, P:P + 112])
                settle()
                add(at(ws + 112, [(1, 16)]), at(ws + 112, [(1, 16)]), bank[:, P + 112:2 * P]).then_inc(read, 1)
                settle()
                V.scalar_tensor_tensor(out=at(ws + 112, [(1, 16)]), in0=at(TAB + T_M16 - T_TN, [(1, 16)]), scalar=vcol(1, 8 + o),
                                       in1=at(ws + 112, [(1, 16)]), op0=ALU.mult, op1=ALU.add).then_inc(S("ws_ready"), 1)

            dve.wait_ge(S("tab_loaded"), 16)
            output_matrices(0)
            for o in range(OCT + 2):
                if o >= 2:
                    for half in range(2):
                        bank, read = bank_of("yt", o - 2, half)
                        if o >= 3 and half == 0:
                            dve.wait_ge(S("bank_filled"), turn_of["yc", o - 3, 1] + 1)
                        V.tensor_copy(at(MT2 + half * 16, [(32, 4), (P, 8), (1, 16)], 0, XC),
                                      bank[0:XC, :].rearrange("p (g t h) -> p g t h", g=4, h=16)).then_inc(read, 1)
                        dve.drain().then_inc(S("mt2_ready"), 1)
                if o < OCT:
                    lag_strip(o)
                if o + 1 < OCT:
                    output_matrices(o + 1)
            barrier(dve, 3)

            for o in range(OCT):
                m = o % 2
                dve.wait_ge(S("glu_ready"), o + 1)
                z = at(ZA + o * NT, [(1, NT)])
                mul(z, at(YT + o * YW, [(1, NT)]), at(TA + m * NT, [(1, NT)]))
                settle()
                mul(z, z, at(TG + m * NT, [(1, NT)])).then_inc(S("za_done"), 1)
            barrier(dve, 4)

            def mlp_args(n, rows):
                for half, (c0, cn) in enumerate(((0, 512), (512, P))):
                    bank, read = bank_of("mlp", n, half)
                    V.tensor_scalar(at(FA + c0, [(1, cn)], 0, rows), bank[0:rows, 0:cn], at(FCOL + 2 * (n - 1), [(1, 1)], 0, rows),
                                    at(FCOL + 2 * (n - 1) + 1, [(1, 1)], 0, rows), ALU.add, ALU.mult).then_inc(read, 1)
                settle()
                reduce_angle(at(FA, [(1, NT)], 0, rows), at(FK, [(1, NT)], 0, rows))
                dve.drain().then_inc(S("sin_arg"), 1)
            dve.wait_ge(S("fcol_loaded"), 16 * 6)
            mlp_args(1, 64)
            dve.wait_ge(S("sin_done"), 1)
            dve.drain().then_inc(S("mlp_ready"), 1)
            n = 0
            for name, part in (("v", 0), ("x1", 1)):
                for o in range(OCT):
                    if name == "v" and o == 1:
                        mlp_args(2, P)
                        dve.wait_ge(S("sin_done"), 2)
                        V.tensor_copy(at(FO2, [(1, NT)], 0, 64), at(FE, [(1, NT)], 0, 64))
                        link(V.tensor_scalar(at(FO2, [(1, NT)], 64, 64), at(FE, [(1, NT)], 64, 64), -1.0, None, ALU.mult))
                        V.memset(at(FE, [(NLAT, 2)], 64, 64), 0.0)
                        dve.drain().then_inc(S("mlp_ready"), 1)
                    cv = conv_sides(name, o, part, n)
                    if n >= 2:
                        prev = (name, o - 2) if o >= 2 else ("v", o + 6)
                        dve.wait_ge(S("bank_filled"), turn_of[prev[0] + "t", prev[1], 1] + 1)
                    pq = PQ + (o % 2) * NT
                    first, mirrored = at(cv, [(1, 256)]), at(cv + NLAT - 1, [(-1, 256)])
                    if name == "v":
                        add(at(pq, [(1, 256)]), first, mirrored)
                        sub(at(pq + 256, [(1, 256)]), first, mirrored)
                    else:
                        V.tensor_copy(at(pq, [(1, 256)]), first)
                        V.tensor_copy(at(pq + 256, [(1, 256)]), mirrored)
                    V.tensor_copy(at(pq + NLAT, [(1, NCTX)]), at(cv + NLAT, [(1, NCTX)])).then_inc(S("cv_free"), 1)
                    dve.drain().then_inc(S(name + "_conv"), 1)
                    n += 1
            barrier(dve, 5)

            def window_taps(i):
                dve.wait_ge(S("win_ready"), i + 1)
                if i:
                    dve.wait_ge(S("bank_filled"), turn_of["khc", i - 1] + 1)
                for n in range(5):
                    bank, read = bank_of("f", i, n)
                    mul(at(TAPS + n * HW, [(5 * HW, 2), (1, HW)]), bank.rearrange("p (a b) -> p a b", a=2),
                        at(WIN + n * HW, [(0, 2), (1, HW)])).then_inc(read, 1)
                dve.drain().then_inc(S("taps_ready"), 1)

            def kh_combine(i):
                for kind in range(2):
                    for ft in range(2):
                        bank, read = bank_of("kh", i, kind, ft)
                        n = 4 * i + 2 * kind + ft
                        dve.wait_ge(S("kh_odd"), n + 1)
                        odd = at(HTMP + (n % 2) * HW, [(1, HW)])
                        add(at(KH + (kind * 5 + ft) * HW, [(1, HW)]), bank[:, 0:HW], odd)
                        sub(at(KH + (kind * 5 + ft + 2) * HW, [(1, HW)]), bank[:, 0:HW], odd).then_inc(read, 1)
                        dve.drain().then_inc(S("kh_done"), 1)

            def products(i):
                dve.wait_ge(S("fq_ready"), i + 1)
                dve.wait_ge(S("khc_ready"), i + 1)
                if i:
                    dve.wait_ge(S("bank_filled"), turn_of["yi", i - 1, 2] + 1)
                n, part = 5 * HW, 640
                for c0 in (0, part):
                    p, q, kr, ki = (at(b + c0, [(1, part)]) for b in (FQ, FQ + n, KH, KH + n))
                    p1, q1, t = at(PR + c0, [(1, part)]), at(PR + n + c0, [(1, part)]), at(PT, [(1, part)])
                    mul(p1, kr, p)
                    link(mul(t, ki, q))
                    link(add(p1, p1, t))
                    mul(q1, kr, q)
                    link(mul(t, ki, p))
                    link(sub(q1, q1, t))
                dve.drain().then_inc(S("pr_ready"), 1)

            def outputs(i):
                w, r = ITEMS[i]
                for tt in range(2):
                    bank, read = bank_of("yi", i, tt)
                    n = 2 * i + tt
                    dve.wait_ge(S("yi_odd"), n + 1)
                    odd = at(MTMP + (n % 2) * HW, [(1, HW)])
                    va, vb = (at(VS + (2 * h + tt) * H1 + w * HW, [(1, HW)]) for h in range(2))
                    if r:
                        add(va, bank[:, 0:HW], odd)
                        sub(vb, bank[:, 0:HW], odd).then_inc(read, 1)
                    else:
                        ta, tb = at(YT2, [(1, HW)]), at(YT2 + HW, [(1, HW)])
                        add(ta, bank[:, 0:HW], odd)
                        sub(tb, bank[:, 0:HW], odd).then_inc(read, 1)
                        settle()
                        mul(ta, ta, at(XS + tt * H1 + w * HW, [(1, HW)]))
                        mul(tb, tb, at(XS + (2 + tt) * H1 + w * HW, [(1, HW)]))
                        settle()
                        add(va, ta, tb)
                        sub(vb, ta, tb)
                    dve.drain().then_inc(S("yi_done"), 1)
                bank, read = bank_of("yi", i, 2)
                vc = at(VS + 4 * H1 + w * HW, [(1, HW)])
                if r:
                    V.tensor_copy(vc, bank[:, 0:HW]).then_inc(read, 1)
                else:
                    mul(vc, bank[:, 0:HW], at(XS + 4 * H1 + w * HW, [(1, HW)])).then_inc(read, 1)
                dve.drain().then_inc(S("yh_ready" if r else "z_ready"), 1)

            def gated(w):
                for m in range(2):
                    gb = GB + (2 * w + m) * NT
                    bank, read = bank_of("zt", w, m, 0)
                    mul(at(gb, [(1, 256)]), at(gb, [(1, 256)]), bank[:, 0:256])
                    back = at(gb + NLAT - 1, [(-1, 256)])
                    mul(back, back, bank[:, 256:512]).then_inc(read, 1)
                    bank, read = bank_of("zt", w, m, 1)
                    mul(at(gb + NLAT, [(1, P)]), at(gb + NLAT, [(1, P)]), bank[:, 0:P]).then_inc(read, 1)

            window_taps(0)
            kh_combine(0)
            window_taps(1)
            for i in range(2 * NW):
                products(i)
                if i + 1 < 2 * NW:
                    kh_combine(i + 1)
                if i + 2 < 2 * NW:
                    window_taps(i + 2)
                if i and ITEMS[i - 1][1]:
                    gated(ITEMS[i - 1][0])
                if i:
                    mod_part("mod1", i - 1, 16 + 4 * (i - 1))
                outputs(i)
            gated(NW - 1)
            mod_part("mod1", 2 * NW - 1, 16 + 4 * (2 * NW - 1))
            barrier(dve, 6)

            def gates(layer):
                for w in range(2):
                    for k in range(8):
                        V.tensor_scalar(at((DG9 if layer else DG) + w * D + k * P, [(1, P)]), at(IDENT, [(1, P)]),
                                        at(MV + layer * 48 + 32 + 2 * k + w, [(1, 1)]), None, ALU.mult)
                dve.drain().then_inc(S("dg_ready"), 1)

            def scale_terms(layer):
                link(V.tensor_scalar(at(AB, [(1, 16)]), at(MV + layer * 48 + 16, [(1, 16)]), 1.0, None, ALU.add))
                mul(at(AB, [(2, 8), (1, 2)]), at(AB, [(2, 8), (1, 2)]),
                    at(VC + 16 + 8 * layer, [(1, 8)]).unsqueeze(2).broadcast_to([P, 8, 2])).then_inc(S("mod_ready"), 1)

            def residual(layer):
                for half in range(2):
                    if half == 0:
                        dve.wait_ge(S("gr_ready"), layer + 1)
                    acc4 = bank_of("acc4", layer, half)
                    for t in (0, 1, 2, 3, 4):
                        w = 0 if t < 4 else 1
                        acc, read = acc4
                        if t < 4:
                            acc, read = GP[:, t // 2, (t % 2) * 512:(t % 2) * 512 + 512], S("acc_read")
                        tmp = at((RT9 if layer else RT) + (t % 2) * 512, [(1, 512)])
                        x = at((XRES9 if layer else XRES) + t * D + half * 512, [(1, 512)])
                        gate = at((GR9 if layer else GR) + w * D + half * 512, [(1, 512)])
                        if layer:
                            V.scalar_tensor_tensor(out=tmp, in0=acc, scalar=at(STAT + 32 + t, [(1, 1)]), in1=gate,
                                                   op0=ALU.mult, op1=ALU.mult).then_inc(read, 1)
                        else:
                            mul(tmp, acc, gate).then_inc(read, 1)
                        settle()
                        add(x, x, tmp)
                        if half:
                            dve.drain().then_inc(S("res_ready"), 1)
                        settle()
            gates(0)
            scale_terms(1)
            dve.wait_ge(S("xres_loaded"), 80)
            residual(0)
            for t in range(TT + 1):
                if t < TT:
                    normed(1, t, XRES)
                if t:
                    modulated(1, t - 1)
            barrier(dve, 7)

            tri = (TAB + T_UP - T_TN, TAB + T_LO - T_TN)
            sub(at(SGT, [(1, P)]), at(tri[1], [(1, P)]), at(IDENT, [(1, P)]))
            sub(at(SLT, [(1, P)]), at(tri[0], [(1, P)]), at(IDENT, [(1, P)]))
            x, y, z = (at(SPT + i * CW, [(1, CW)]) for i in range(3))
            dt, ad = at(DTB, [(1, CW)]), at(AD, [(1, CW)])
            dve.wait_ge(S("ssd_rows"), 48)
            bank, read = bank_of("dt")
            V.tensor_tensor(at(SPT, [(SH, TT), (TT * SH, 2), (1, SH)]), bank[:, 0:CW].rearrange("p (t d h) -> p t d h", t=TT, d=2),
                            at(BROW, [(0, TT), (SH, 2), (1, SH)]), ALU.add).then_inc(read, 1)
            settle()
            link(V.scalar_tensor_tensor(out=y, in0=x, scalar=-1.0, in1=x, op0=ALU.mult, op1=ALU.min))
            V.tensor_scalar(x, x, 0.0, None, ALU.max)
            dve.drain().then_inc(S("sp_arg"), 1)
            dve.wait_ge(S("sp_exp"), 1)
            link(V.tensor_scalar(z, y, 2.0, None, ALU.add))
            link(V.reciprocal(z, z))
            link(mul(y, y, z))
            link(mul(z, y, y))
            link(V.tensor_scalar(dt, z, 1.0 / 17, 1.0 / 15, ALU.mult, ALU.add))
            for k in (13, 11, 9, 7, 5, 3, 1):
                link(mul(dt, dt, z))
                link(V.tensor_scalar(dt, dt, 1.0 / k, None, ALU.add))
            link(mul(dt, dt, y))
            link(V.scalar_tensor_tensor(out=dt, in0=dt, scalar=2.0, in1=x, op0=ALU.mult, op1=ALU.add))
            dve.wait_ge(S("arow_ready"), 1)
            for d in range(2):
                V.scalar_tensor_tensor(out=at(AD + d * TT * SH, [(SH, TT), (1, SH)]), in0=at(DTB + d * TT * SH, [(SH, TT), (1, SH)]),
                                       scalar=-1.0, in1=at(AROW + d * SH, [(0, TT), (1, SH)]), op0=ALU.mult, op1=ALU.mult)
            dve.drain().then_inc(S("ad_ready"), 1)

            def ssd_sides(n):
                g, j = n // 6, n % 6
                o, dst = (16 + 4 * j + g, BC + (g % 2) * 2 * NT + j * NT) if j < 2 else (4 * g + j - 2, XCH + (j - 2) * NT)
                dve.wait_ge(S("cv_center8"), n + 1)
                tile, read = tile_of("ssd_g", n)
                for base, m in ((0, NLAT), (NLAT, NCTX)):
                    V.scalar_tensor_tensor(out=at(dst + base + 1, [(1, m - 1)]), in0=tile[:, base:base + m - 1],
                                           scalar=vcol(2, 24 + o), in1=at(dst + base + 1, [(1, m - 1)]), op0=ALU.mult, op1=ALU.add)
                settle()
                for base, m in ((0, NLAT), (NLAT, NCTX)):
                    i = V.scalar_tensor_tensor(out=at(dst + base, [(1, m - 1)]), in0=tile[:, base + 1:base + m],
                                               scalar=vcol(2, 24 + 48 + o), in1=at(dst + base, [(1, m - 1)]), op0=ALU.mult, op1=ALU.add)
                i.then_inc(read, 1)
                dve.drain().then_inc(S("cv_sides"), 1)

            def heads(base, n=64):
                return at(base, [(n, 8), (1, n)])

            def state_step(g, k):
                d, t = STATES[k]
                bank, read = bank_of("st", g, k)
                if k == 2:
                    dve.wait_ge(S("init_ready"), g + 1)
                src = HP + (4 * d + t) * 512
                dst = src + (512, -512)[d]
                link(mul(heads(dst), heads(src), coef(TOT, d, t, g, 64)))
                add(at(dst, [(1, 512)]), at(dst, [(1, 512)]), bank).then_inc(read, 1)
                settle()

            def weighted(g, t):
                n = TT * g + t
                dve.wait_ge(S("ex_ready"), n + 1)
                dve.wait_ge(S("w_ready"), n + 1)
                ex = at(EX + n % 2 * 1024, [(1, 1024)])
                mul(ex, ex, at(MM, [(1, 1024)]))
                dve.drain().then_inc(S("mm_ready"), 1)

            for n in range(6):
                ssd_sides(n)
            dve.wait_ge(S("coef_exp"), 1)
            mul(at(WW, [(1, CW)]), at(WW, [(1, CW)]), dt)
            dve.drain().then_inc(S("ww_ready"), 1)
            for g in range(SG):
                settle()
                for part in range(2):
                    bank, read = bank_of("cb", g, part)
                    m = (4, 1)[part]
                    for d in range(2):
                        i = mul(at(CBM + d * TT * P + part * 512, [(P, m), (1, P)]), bank[:, 0:m * P].rearrange("p (a b) -> p a b", a=m),
                                at(tri[d], [(0, m), (1, P)]))
                    i.then_inc(read, 1)
                dve.drain().then_inc(S("cb_ready"), 1)
                for k in range(2, 8):
                    state_step(g, k)
                dve.wait_ge(S("xt_ready"), g + 1)
                settle()
                dve.sem_inc(S("hp_ready"), 1)
                weighted(g, 0)
                for t in range(TT):
                    for n8 in next_tiles(g, t):
                        ssd_sides(n8)
                    if t + 1 < TT:
                        weighted(g, t + 1)
                    tf, tb = YTMP, YTMP + 512
                    out = at(Y + t * DI + g * 512, [(1, 512)])
                    if t < 4:
                        for d in range(2):
                            bank, read = bank_of("yo", g, t, d)
                            mul(heads((tf, tb)[d]), bank.rearrange("p (h c) -> p h c", h=8), coef(EE, d, t, g, 64)).then_inc(read, 1)
                        settle()
                        add(at(tf, [(1, 512)]), at(tf, [(1, 512)]), at(tb, [(1, 512)]))
                    bank, read = bank_of("yd", g, t)
                    dve.wait_ge(S("yx_ready"), TT * g + t + 1)
                    add(out, out, bank).then_inc(read, 1)
                    settle()
                    if t < 4:
                        add(out, out, at(tf, [(1, 512)]))
                        settle()
            barrier(dve, 8)

            gates(1)
            for c in range(8):
                for t in range(TT):
                    n = TT * c + t
                    dve.wait_ge(S("sz_ready"), n + 1)
                    y = at(Y + t * DI + c * 256, [(1, 256)])
                    mul(y, y, at(SZ + (n % 4) * 256, [(1, 256)])).then_inc(S("yz_ready"), 1)
            dve.wait_ge(S("sums_ready"), 1)
            V.tensor_reduce(at(STAT + 24, [(1, TT)]), at(SUMS, [(8, TT), (1, 8)]), mybir.AxisListType.X, ALU.add).then_inc(S("sums_added"), 1)
            dve.wait_ge(S("zrms_ready"), 1)
            link(V.reciprocal(at(STAT + 32, [(1, TT)]), at(STAT + 24, [(1, TT)])))
            dve.wait_ge(S("xres_loaded"), 160)
            residual(1)
            dve.wait_ge(S("fnw_loaded"), 16)
            for t in range(TT):
                dve.wait_ge(S("rms_ready"), 2 * TT + t + 1)
                link(V.reciprocal(at(STAT + 16 + t, [(1, 1)]), at(STAT + 8 + t, [(1, 1)])))
                x = at(XRES9 + t * D, [(1, D)])
                V.scalar_tensor_tensor(out=x, in0=x, scalar=at(STAT + 16 + t, [(1, 1)]), in1=at(FNW, [(1, D)]),
                                       op0=ALU.mult, op1=ALU.mult).then_inc(S("y_ready"), 1)

        @block.gpsimd
        def _(pool):
            G = nc.gpsimd
            G.memset(at(ONES, [(1, P)]), 1.0).then_inc(S("ident_ready"), 1)
            G.memset(at(IDENT, [(1, P)]), 0.0).then_inc(S("ident_ready"), 1)
            pool.wait_ge(S("ident_ready"), 2)
            G.affine_select(out=at(IDENT, [(1, P)]), in_=at(IDENT, [(1, P)]), compare_op=ALU.not_equal, fill=1.0, base=0,
                            pattern=[[-1, P]], channel_multiplier=1).then_inc(S("ident_ready"), 1)
            barrier(pool, 1)
            G.memset(at(U + GAP, [(XC, 64)]), 0.0).then_inc(S("u_gap"), 1)
            pool.wait_ge(S("scan_start"), 1)
            pool.wait_ge(S("bank_filled"), turn_of["s", OCT - 1, 3] + 1)
            for c, nm in enumerate(("s5_c_re", "s5_c_im")):
                for d in range(2):
                    pool.dma_start(at(CRAW + (2 * c + d) * OCT * SP, [(SP, OCT), (1, SP)]),
                                   a[nm][0, d].rearrange("(o g) h p -> (g h) o p", g=8)).then_inc(S("c_loaded"), 16)
            dstep = (LATX + 1) * SLOTW - 64
            h0 = HS + 64
            with pool.Fori(0, CTXX) as s:
                h = at(h0 + s * SLOTW, [(dstep, 2), (1, 64)])
                hc = at(h0 + s * SLOTW, [(dstep, 2), (32, 2), (1, 32)])
                hn = at(h0 + SLOTW + s * SLOTW, [(dstep, 2), (1, 64)])
                m1, m2 = at(SCT + 256, [(64, 2), (1, 64)]), at(SCT + 384, [(64, 2), (1, 64)])
                G.tensor_tensor(m1, h, at(SCA + 64, [(-64, 2), (1, 64)]), ALU.mult).then_inc(S("scan_ctx"), 1)
                G.tensor_tensor(at(SCT + 416, [(64, 2), (-32, 2), (1, 32)]), hc,
                                at(SCA + 224, [(-64, 2), (-32, 2), (1, 32)]), ALU.mult).then_inc(S("scan_ctx"), 1)
                pool.wait_ge(S("scan_ctx"), s * 4 + 2)
                G.tensor_tensor(m1, m1, m2, ALU.add).then_inc(S("scan_ctx"), 1)
                pool.wait_ge(S("scan_ctx"), s * 4 + 3)
                G.tensor_tensor(hn, hn, m1, ALU.add).then_inc(S("scan_ctx"), 1)
                pool.wait_ge(S("scan_ctx"), s * 4 + 4)
            for o in range(OCT):
                pool.wait_ge(S("x2_ready"), o + 1)
                cv, left = CVX + (o % 2) * NT, TLX + (o % 2) * 2 * NT
                for shift, src in ((1, left), (0, left + NT)):
                    for base, m in ((0, NLAT - 1), (NLAT, NCTX - 1)):
                        out = at(cv + base + shift, [(1, m)])
                        G.tensor_tensor(out, out, at(src + base + 1 - shift, [(1, m)]), ALU.add).then_inc(S("x2_sum"), 1)
                    pool.wait_ge(S("x2_sum"), 4 * o + 4 - 2 * shift)
                gb = at(GB + o * NT, [(1, NT)])
                G.tensor_tensor(gb, gb, at(cv, [(1, NT)]), ALU.mult).then_inc(S("x2_used"), 1)
            barrier(pool, 2)

            pool.wait_ge(S("fo_ready"), 1)
            for c, nm in enumerate(("new_re", "new_im")):
                pool.dma_start(outs[nm].rearrange("b a d (q e) p -> (b a d q) (e p)", e=2),
                               at(FO + c * P, [(1, P)], 0, 64)).then_inc(S("s5_state_out"), 16)
            for o in range(OCT):
                pool.wait_ge(S("ws_ready"), o + 1)
                pool.dma_start(strips[o], at(WS[o % 2], [(1, 240)])).then_inc(S(f"strip_out{o % 2}"), 16)
                pool.wait_ge(S(f"strip_out{o % 2}"), 16 * (o // 2 + 1))
                if o >= 2:
                    pool.wait_ge(S("bank_filled"), turn_of["y", o - 2, 1] + 1)
                for t in range(Q8):
                    pool.dma_start(at(TTB + (o % 2) * 1024, [(P, 8), (1, P)], 16 * t, 16),
                                   strips[o].rearrange("(g h) c -> h g c", h=GS)[:, :, 16 * t:16 * t + P]).then_inc(S(f"t_loaded{o % 2}"), 16)
            pool.wait_ge(S("s5_state_out"), 32)
            barrier(pool, 3)
            pool.dma_start(at(EMB, [(1, NT)], 0, 33), a["emb"]).then_inc(S("mlp_loaded"), 16)
            pool.dma_start(at(W3 + HW, [(1, 64)], 0, 33), a["hy_f_w1"][0]).then_inc(S("mlp_loaded"), 16)
            for j in range(2):
                pool.dma_start(at(W3 + 64 * j, [(1, 64)], 0, 64), a["hy_f_w2"][0]).then_inc(S("mlp_loaded"), 16)
            for j, nm in enumerate(("hy_f_b1", "hy_f_freq1")):
                pool.dma_start(at(FCOL + j, [(1, 1)], 0, 64), a[nm].rearrange("a h -> h a")).then_inc(S("fcol_loaded"), 16)
            for j, nm in enumerate(("hy_f_b2", "hy_f_freq2")):
                for copy in range(2):
                    pool.dma_start(at(FCOL + 2 + j, [(1, 1)], 64 * copy, 64), a[nm].rearrange("a h -> h a")).then_inc(S("fcol_loaded"), 16)
            barrier(pool, 4)
            pool.dma_start(at(CX, [(1, 640)]), a["tables"][:, T_CX:T_CX + 640]).then_inc(S("cs_loaded"), 16)
            pool.dma_start(at(CS, [(1, 2048)]), a["tables"][:, T_CS:T_CS + 2048]).then_inc(S("cs_loaded"), 16)

            def filter_weights(i):
                w, r = ITEMS[i]
                pool.wait_ge(S("bank_filled"), (turn_of["f", i - 2, 4] if i >= 2 else turn_of["mlp", 2, 1]) + 1)
                w3 = a["hy_f_w3"][0].rearrange("h (r d c) -> d h r c", r=2, d=2)
                for d in range(2):
                    pool.dma_start(at(W3 + (i % 2) * HW, [(1, HW)], 64 * d, 64),
                                   w3[d, :, r, w * HW:(w + 1) * HW]).then_inc(S(f"w3_loaded{i % 2}"), 16)
                if i:
                    pool.wait_ge(S("bank_filled"), turn_of["f", i - 1, 4] + 1)
                pool.dma_start(at(FBIAS, [(1, HW)], 0, 1), a["hy_bias"][0, r:r + 1, w * HW:(w + 1) * HW]).then_inc(S("fbias_loaded"), 16)
            for i in range(1):
                filter_weights(i)
            barrier(pool, 5)
            pool.dma_start(at(DEL, [(1, H1)]), a["deltas"][0].partition_broadcast(P)).then_inc(S("deltas_loaded"), 16)
            pool.dma_start(at(GF, [(1, 2048)]), a["tables"][:, T_GF:T_GF + 2048]).then_inc(S("hy_tables"), 16)
            pool.dma_start(at(GI, [(1, 2048)]), a["tables"][:, T_GI:T_GI + 2048]).then_inc(S("hy_tables"), 16)

            for i in range(1, 2 * NW):
                filter_weights(i)
            barrier(pool, 6)
            for t in range(TT):
                src = a["x_sample"][0, t * P:(t + 1) * P, :] if t < 4 else a["x_prompt"][0]
                pool.dma_start(at(XRES + t * D, [(1, D)]), src).then_inc(S("xres_loaded"), 16)
            for t in range(TT):
                pool.wait_ge(S("res_ready"), t + 1)
                pool.dma_start(spill[t], at(XRES + t * D, [(1, D)])).then_inc(S("spilled"), 16)
            pool.wait_ge(S("spilled"), 16 * TT)
            barrier(pool, 7)

            for row, nm, n in ((BROW, "ssd_dt_bias", 64), (AROW, "ssd_a_log", 64), (DROW, "ssd_d", SH)):
                src = a[nm][0].rearrange("d h -> (d h)") if n == 64 else a[nm][0]
                pool.dma_start(at(row, [(1, n)]), src.partition_broadcast(P)).then_inc(S("ssd_rows"), 16)

            def load_init(g):
                for d in range(2):
                    pool.dma_start(at(INIT + d * 512, [(P, 4), (1, P)]),
                                   a["state_ssd"][0, 0, d, 8 * g:8 * g + 8].rearrange("(j e) p n -> (e p) j n", e=2)).then_inc(S("init_loaded"), 16)

            def masked(g, t):
                n = TT * g + t
                if n:
                    pool.wait_ge(S("bank_filled"), (turn_of["ar", g, t - 1, 1] if t else turn_of["ar", g - 1, 4, 1]) + 1)
                for d, mask in enumerate((TAB + T_UP - T_TN, TAB + T_LO - T_TN)):
                    G.tensor_tensor(at(AM + d * 1024, [(P, 8), (1, P)]), at(mask, [(0, 8), (1, P)]), coef(AD, d, t, g, P),
                                    ALU.mult).then_inc(S("am_ready"), 1)
            def state_input(g, k):
                d, t = STATES[k]
                if k >= 2:
                    pool.wait_ge(S("bank_filled"), turn_of["st", g, k - 2] + 1)
                G.tensor_tensor(at(XW + (k % 2) * 512, [(64, 8), (1, 64)]), at(XT + t * 512, [(64, 8), (1, 64)]), coef(WW, d, t, g, 64),
                                ALU.mult).then_inc(S("xw_ready"), 1)


            def weights(g, t):
                n = TT * g + t
                pool.wait_ge(S("cb_ready"), g + 1)
                if n:
                    pool.wait_ge(S("mm_ready"), n)
                for d in range(2):
                    G.tensor_tensor(at(MM + d * 1024, [(P, 8), (1, P)]), at(CBM + (TT * d + t) * P, [(0, 8), (1, P)]),
                                    coef(DTB, d, t, g, P), ALU.mult).then_inc(S("w_parts"), 1)
                pool.wait_ge(S("w_parts"), 2 * n + 2)
                w = at(MM, [(1, 1024)])
                G.tensor_tensor(w, w, at(MM + 1024, [(1, 1024)]), ALU.add).then_inc(S("w_ready"), 1)
            load_init(0)
            pool.wait_ge(S("ssd_rows"), 48)
            pool.wait_ge(S("ad_ready"), 1)
            masked(0, 0)
            for g in range(SG):
                pool.wait_ge(S("xt_ready"), g + 1)
                if g == 0:
                    pool.wait_ge(S("ww_ready"), 1)
                for k in range(8):
                    state_input(g, k)
                weights(g, 0)
                for t in range(TT):
                    if t + 1 < TT:
                        masked(g, t + 1)
                    if t + 1 < TT:
                        weights(g, t + 1)
                    G.tensor_tensor(at(Y + t * DI + g * 512, [(64, 8), (1, 64)]), at(XT + t * 512, [(64, 8), (1, 64)]),
                                    at(DROW + 8 * g, [(1, 8), (0, 64)]), ALU.mult).then_inc(S("yx_ready"), 1)
                    if t == 0 and g < 3:
                        pool.wait_ge(S("bank_filled"), turn_of["in", g, 1] + 1)
                        load_init(g + 1)
                pool.wait_ge(S("fout_ready"), g + 1)
                for d in range(2):
                    pool.dma_start(outs["new_ssd"][0, 0, d, 8 * g:8 * g + 8].rearrange("(j e) p n -> (e p) j n", e=2),
                                   at(FOUT + d * 512, [(P, 4), (1, P)])).then_inc(S("ssd_state_out"), 16)
                if g < 3:
                    masked(g + 1, 0)
            pool.wait_ge(S("ssd_state_out"), 32 * SG)
            barrier(pool, 8)

            for t in range(TT):
                pool.dma_start(at(XRES9 + t * D, [(1, D)]), spill[t]).then_inc(S("xres_loaded"), 16)
            pool.dma_start(at(FNW, [(1, D)]), a["final_norm_w"].partition_broadcast(P)).then_inc(S("fnw_loaded"), 16)
            for t in range(TT):
                pool.wait_ge(S("y_ready"), t + 1)
                dst = outs["y_sample"][0, t * P:(t + 1) * P, :] if t < 4 else outs["y_prompt"][0]
                pool.dma_start(dst, at(XRES9 + t * D, [(1, D)])).then_inc(S("y_out"), 16)
            pool.wait_ge(S("y_out"), 16 * TT)

        @block.sync
        def _(sp):
            def stream(name, count, src, sub_):
                base = chunk[name]
                assert base % NSLOT == 0 and count % NSLOT == 0

                def four(it, first):
                    for j in range(4):
                        if first is None or first + j >= NSLOT:
                            sp.wait_ge(S("ring_used"), it * 4 + (base + j - NSLOT + 1))
                        sp.dma_start(at(ring(j), sub_), src(it * 4 + j)).then_inc(S(f"ring_full{j}"), 16)
                done = 0
                if base == 0:
                    four(0, 0)
                    done = 1
                    for t in range(TT):
                        x = a["x_sample"][0, t * P:(t + 1) * P, :] if t < 4 else a["x_prompt"][0]
                        sp.dma_start(at(X1 + t * D, [(1, D)]), x).then_inc(S(f"x_loaded{t}"), 16)
                if count // 4 - done > 0:
                    with sp.Fori(done, count // 4) as it:
                        four(it, None)
            sub8 = [(256, 8), (1, 256)]

            def cols8(w, c0):
                v = w.rearrange("(k p) n -> p k n", p=P)
                return lambda i: v[:, :, bass.ds(i * 256 + c0, 256)]
            stream("mod0", 8, cols8(a["mod_w"][0], 0), sub8)
            win = a["ev_w_in"][0]
            stream("u", 4, cols8(win, 0), sub8)
            stream("gb", 4, cols8(win, 5 * 1024), sub8)

            stream("x2", 4, cols8(win, 4 * 1024), sub8)
            wglu = a["s5_glu_w"][0].rearrange("(k p) n -> p k n", p=P)
            wga = win.rearrange("(k p) n -> p k n", p=P)
            for i in range(8):
                n = chunk["ga_glu"] + i
                sp.wait_ge(S("ring_used"), n - NSLOT + 1)
                c0 = (i // 2) * 256
                src = wglu[:, :, c0:c0 + 256] if i % 2 else wga[:, :, 1024 + c0:1024 + c0 + 256]
                sp.dma_start(at(ring(n % NSLOT), sub8), src).then_inc(S(f"ring_full{n % NSLOT}"), 16)
            stream("v", 4, cols8(win, 2 * 1024), sub8)
            stream("x1", 4, cols8(win, 3 * 1024), sub8)

            for i in range(16):
                n = chunk["mod1"] + i
                c0 = (8 + i) * 256 if i < 4 else (i - 4) * 256
                sp.wait_ge(S("ring_used"), n - NSLOT + 1)
                sp.dma_start(at(ring(n % NSLOT), sub8),
                             a["mod_w"][min(i // 4, 1)].rearrange("(k p) n -> p k n", p=P)[:, :, c0:c0 + 256]).then_inc(S(f"ring_full{n % NSLOT}"), 16)

            def stream_out(name, w):
                v = w.rearrange("(c k p) n -> c p k n", k=4, p=P)
                for i in range(8):
                    n = chunk[name] + i
                    sp.wait_ge(S("ring_used"), n - NSLOT + 1)
                    sp.dma_start(at(ring(n % NSLOT), [(512, 4), (1, 512)]),
                                 v[i % 4, :, :, (i // 4) * 512:(i // 4) * 512 + 512]).then_inc(S(f"ring_full{n % NSLOT}"), 16)
            stream_out("ev_out", a["ev_w_out"][0])

            def load_chunk(n, dims, src):
                sp.wait_ge(S("ring_used"), n - NSLOT + 1)
                sp.dma_start(at(ring(n % NSLOT), dims), src).then_inc(S(f"ring_full{n % NSLOT}"), 16)
            wssd = a["ssd_w_in"][0].rearrange("(k p) n -> p k n", p=P)
            load_chunk(chunk["ssd_dt"], [(64, 8), (1, 64)], wssd[:, :, 5120:5184])
            for g in range(SG):
                n = chunk["ssd_g"] + 3 * g
                load_chunk(n, [(256, 8), (1, P)], wssd[:, :, 2 * DI + g * P:2 * DI + (g + 1) * P])
                sp.dma_start(at(ring(n % NSLOT) + P, [(256, 8), (1, P)]),
                             wssd[:, :, 2 * DI + 512 + g * P:2 * DI + 512 + (g + 1) * P]).then_inc(S(f"ssd_c_loaded{g % 2}"), 16)
                for j in range(2):
                    c0 = DI + g * 512 + j * 256
                    load_chunk(n + 1 + j, sub8, wssd[:, :, c0:c0 + 256])
            for c in range(8):
                load_chunk(chunk["ssd_z"] + c, sub8, wssd[:, :, c * 256:(c + 1) * 256])
            stream_out("ssd_out", a["ssd_w_out"][0])


_OUTS = [("y_prompt", (1, NCTX, D)), ("y_sample", (1, NLAT, D)), ("new_re", (1, 1, 2, 64, SP)), ("new_im", (1, 1, 2, 64, SP)),
         ("new_ssd", (1, 1, 2, SH, SHD, SN))]


def kernel(**inputs):
    import concourse.bacc as bacc
    from concourse.bass_utils import run_bass_kernel_spmd

    arrays = {name: np.ascontiguousarray(value) for name, value in inputs.items()}
    arrays["tables"], arrays["emb"], arrays["deltas"] = constant_tables()
    nc = bacc.Bacc("TRN2", target_bir_lowering=False, num_devices=1)
    ins = {name: nc.dram_tensor(name, value.shape, mybir.dt.from_np(value.dtype), kind="ExternalInput").ap()
           for name, value in arrays.items()}
    outs = {name: nc.dram_tensor(name, shape, F32, kind="ExternalOutput").ap() for name, shape in _OUTS}
    build(nc, ins, outs)
    result = run_bass_kernel_spmd(nc, [arrays], core_ids=[0]).results[0]
    return tuple(result[name] for name, _ in _OUTS)
```
